# Optimizing a Trainium2 kernel written in Bass

```python
import math
import jax
import jax.numpy as jnp
from jax import lax
import numpy as np

D_MODEL = 1024
BATCH = 1
SEQ = 1024
DEPTH = 1
DEC_BATCH = 8
DEC_SEQ = 4
PAST_LEN = 4096
PAGE_SIZE = 128

MIX_WIDTH = D_MODEL
ATTN_HEADS = 8
ATTN_KV_HEADS = 2
HEAD_DIM = 64
GQA_GROUP = ATTN_HEADS // ATTN_KV_HEADS
ATTN_WIDTH = ATTN_HEADS * HEAD_DIM
KV_WIDTH = ATTN_KV_HEADS * HEAD_DIM
WINDOW = 128
ATTN_BLOCK = WINDOW
ATTN_SCALE = HEAD_DIM ** -0.5
REL_BUCKETS = 32
REL_MAX_DIST = WINDOW
HG_WIDTH = MIX_WIDTH - ATTN_WIDTH
HG_HEADS = 4
HG_DK = HG_WIDTH // HG_HEADS
HG_DV = HG_WIDTH // HG_HEADS
HG_CHUNK = 64
PEER_HEADS = 8
PEER_NKEYS = 128
PEER_EXPERTS = PEER_NKEYS * PEER_NKEYS
PEER_DKEY = 256
PEER_HALF = PEER_DKEY // 2
PEER_TOPK = 16
PEER_BLOCK = 128
EPS = 1e-6
IN_WIDTH = ATTN_WIDTH + 2 * KV_WIDTH + 4 * HG_WIDTH
SPLITS = [ATTN_WIDTH, ATTN_WIDTH + KV_WIDTH, ATTN_WIDTH + 2 * KV_WIDTH,
          ATTN_WIDTH + 2 * KV_WIDTH + HG_WIDTH, ATTN_WIDTH + 2 * KV_WIDTH + 2 * HG_WIDTH,
          ATTN_WIDTH + 2 * KV_WIDTH + 3 * HG_WIDTH]
F32 = jnp.float32

kernel_name = 'hymba_swa_hgrn2_peer_step'

def rmsnorm(x, w):
    xf = x.astype(F32)
    y = xf * lax.rsqrt(jnp.mean(xf * xf, axis=-1, keepdims=True) + EPS)
    return (y * w.astype(F32)).astype(x.dtype)

def t5_bucket(dist):
    n = jnp.maximum(dist, 0)
    max_exact = REL_BUCKETS // 2
    nf = jnp.maximum(n, 1).astype(F32)
    large = max_exact + (jnp.log(nf / max_exact) / math.log(REL_MAX_DIST / max_exact)
                         * (REL_BUCKETS - max_exact)).astype(jnp.int32)
    large = jnp.minimum(large, REL_BUCKETS - 1)
    return jnp.where(n < max_exact, n, large)

def rel_bias(dist, table):
    q_len, k_len = dist.shape
    b = table.astype(F32)[t5_bucket(dist)]
    return jnp.transpose(b, (2, 0, 1)).reshape(ATTN_KV_HEADS, GQA_GROUP, q_len, k_len)

def sink_softmax(s, mask, sinks):
    sink = sinks.astype(F32).reshape(ATTN_KV_HEADS, GQA_GROUP, 1, 1)
    s = jnp.where(mask, s, -jnp.inf)
    m = jnp.maximum(jnp.max(s, axis=-1, keepdims=True), sink)
    p = jnp.exp(s - m)
    return p / (jnp.sum(p, axis=-1, keepdims=True) + jnp.exp(sink - m))

def swa_prompt(q, k, v, sinks, rel_table):
    bsz, seq = q.shape[:2]
    nb = seq // ATTN_BLOCK
    qb = q.reshape(bsz, nb, ATTN_BLOCK, ATTN_KV_HEADS, GQA_GROUP, HEAD_DIM)
    kb = k.reshape(bsz, nb, ATTN_BLOCK, ATTN_KV_HEADS, HEAD_DIM)
    vb = v.reshape(bsz, nb, ATTN_BLOCK, ATTN_KV_HEADS, HEAD_DIM)
    pad = ((0, 0), (1, 0), (0, 0), (0, 0), (0, 0))
    kk = jnp.concatenate([jnp.pad(kb[:, :-1], pad), kb], axis=2)
    vv = jnp.concatenate([jnp.pad(vb[:, :-1], pad), vb], axis=2)
    s = jnp.einsum('bnqhgd,bnkhd->bnhgqk', qb, kk).astype(F32) * ATTN_SCALE
    dist = (jnp.arange(ATTN_BLOCK)[:, None] + ATTN_BLOCK) - jnp.arange(2 * ATTN_BLOCK)[None, :]
    kpos = jnp.arange(nb)[:, None] * ATTN_BLOCK - ATTN_BLOCK + jnp.arange(2 * ATTN_BLOCK)[None, :]
    mask = ((dist >= 0) & (dist <= WINDOW))[None] & (kpos >= 0)[:, None, :]
    p = sink_softmax(s + rel_bias(dist, rel_table), mask[:, None, None], sinks)
    o = jnp.einsum('bnhgqk,bnkhd->bnqhgd', p, vv.astype(F32))
    return o.reshape(bsz, seq, ATTN_WIDTH)

def swa_sample(q, k, v, k_buf, v_buf, sinks, rel_table):
    bsz, t = q.shape[:2]
    wb = k_buf.shape[1]
    kk = jnp.concatenate([k_buf.astype(k.dtype), k], axis=1)
    vv = jnp.concatenate([v_buf.astype(v.dtype), v], axis=1)
    qg = q.reshape(bsz, t, ATTN_KV_HEADS, GQA_GROUP, HEAD_DIM)
    s = jnp.einsum('bqhgd,bkhd->bhgqk', qg, kk).astype(F32) * ATTN_SCALE
    dist = (wb + jnp.arange(t))[:, None] - jnp.arange(wb + t)[None, :]
    mask = (dist >= 0) & (dist <= WINDOW)
    p = sink_softmax(s + rel_bias(dist, rel_table), mask, sinks)
    o = jnp.einsum('bhgqk,bkhd->bqhgd', p, vv.astype(F32)).reshape(bsz, t, ATTN_WIDTH)
    return o, kk[:, t:], vv[:, t:]

def hgrn2_chunked(q, k, logf, v, s0, chunk):
    bsz, t = q.shape[:2]
    n = t // chunk

    def split(a):
        a = a.reshape(bsz, n, chunk, HG_HEADS, a.shape[-1])
        return jnp.transpose(a, (1, 0, 3, 2, 4))

    idx = jnp.arange(chunk)
    causal = (idx[:, None] >= idx[None, :])[:, :, None]

    def step(state, inp):
        qc, kc, gc, vc = inp
        b = jnp.cumsum(gc, axis=-2)
        dec = jnp.exp(jnp.where(causal, b[:, :, :, None, :] - b[:, :, None, :, :], -jnp.inf))
        a = jnp.einsum('bhtk,bhtsk,bhsk->bhts', qc, dec, kc)
        o = jnp.einsum('bhts,bhsv->bhtv', a, vc) + jnp.einsum('bhtk,bhkv->bhtv', qc * jnp.exp(b), state)
        b_last = b[:, :, -1:, :]
        state = jnp.exp(b_last[:, :, 0, :])[..., None] * state + jnp.einsum(
            'bhsk,bhsv->bhkv', kc * jnp.exp(b_last - b), vc)
        return state, o

    s_new, o = lax.scan(step, s0, (split(q), split(k), split(logf), split(v)))
    o = jnp.transpose(o, (1, 0, 3, 2, 4)).reshape(bsz, t, HG_HEADS, HG_DV)
    return o, s_new

def peer(x2d, w_q, sub_keys, u, v):
    n_tok, d = x2d.shape
    nblk = -(-n_tok // PEER_BLOCK)
    xp = jnp.pad(x2d, ((0, nblk * PEER_BLOCK - n_tok), (0, 0))).reshape(nblk, PEER_BLOCK, d)
    keys = sub_keys.astype(F32)

    def blk(xb):
        qry = (xb @ w_q).astype(F32).reshape(PEER_BLOCK, PEER_HEADS, 2, PEER_HALF)
        sc = jnp.einsum('thcd,hcnd->thcn', qry, keys)
        sv, si = lax.top_k(sc, PEER_TOPK)
        cand = sv[:, :, 0, :, None] + sv[:, :, 1, None, :]
        cidx = si[:, :, 0, :, None] * PEER_NKEYS + si[:, :, 1, None, :]
        fv, fi = lax.top_k(cand.reshape(PEER_BLOCK, PEER_HEADS, PEER_TOPK * PEER_TOPK), PEER_TOPK)
        eidx = jnp.take_along_axis(cidx.reshape(PEER_BLOCK, PEER_HEADS, PEER_TOPK * PEER_TOPK), fi, axis=-1)
        gate = jax.nn.softmax(fv, axis=-1)
        ue = u[eidx]
        ve = v[eidx]
        act = jax.nn.gelu(jnp.einsum('thkd,td->thk', ue, xb).astype(F32), approximate=False)
        return jnp.einsum('thk,thkd->td', (gate * act).astype(xb.dtype), ve)

    y = lax.map(blk, xp).reshape(nblk * PEER_BLOCK, d)
    return y[:n_tok]

def decoder_layer(x, cache, lb, norm_mix_w, w_in, sinks, rel_table, hg_norm_w, w_o,
                  norm_ffn_w, peer_w_q, peer_sub_keys, peer_u, peer_v):
    bsz, t, _ = x.shape
    xn = rmsnorm(x, norm_mix_w)
    proj = xn @ w_in
    q_a, k_a, v_a, q_h, f_h, i_h, g_h = jnp.split(proj, SPLITS, axis=-1)
    q_a = q_a.reshape(bsz, t, ATTN_HEADS, HEAD_DIM)
    k_a = k_a.reshape(bsz, t, ATTN_KV_HEADS, HEAD_DIM)
    v_a = v_a.reshape(bsz, t, ATTN_KV_HEADS, HEAD_DIM)
    if cache is None:
        attn = swa_prompt(q_a, k_a, v_a, sinks, rel_table)
        wb = min(WINDOW, t)
        k_new, v_new = k_a[:, t - wb:], v_a[:, t - wb:]
        s0 = jnp.zeros((bsz, HG_HEADS, HG_DK, HG_DV), F32)
    else:
        k_buf, v_buf, s_prev = cache
        attn, k_new, v_new = swa_sample(q_a, k_a, v_a, k_buf, v_buf, sinks, rel_table)
        s0 = s_prev.astype(F32)
    fgate = lb + (1.0 - lb) * jax.nn.sigmoid(f_h.astype(F32))
    heads = lambda a: a.reshape(bsz, t, HG_HEADS, -1)
    o_h, s_new = hgrn2_chunked(heads(jax.nn.silu(q_h.astype(F32))), heads(1.0 - fgate),
                               heads(jnp.log(fgate)), heads(i_h.astype(F32)), s0,
                               math.gcd(t, HG_CHUNK))
    o_h = o_h * lax.rsqrt(jnp.mean(o_h * o_h, axis=-1, keepdims=True) + EPS)
    o_h = o_h.reshape(bsz, t, HG_WIDTH) * hg_norm_w.astype(F32) * jax.nn.silu(g_h.astype(F32))
    mix = jnp.concatenate([attn.astype(x.dtype), o_h.astype(x.dtype)], axis=-1) @ w_o
    h = x + mix
    hn = rmsnorm(h, norm_ffn_w)
    y = h + peer(hn.reshape(bsz * t, D_MODEL), peer_w_q, peer_sub_keys, peer_u, peer_v).reshape(bsz, t, D_MODEL)
    return y, k_new.astype(x.dtype), v_new.astype(x.dtype), s_new.astype(x.dtype)

def setup_inputs(seed: int = 0) -> dict:
    key = jax.random.key(seed)
    ks = jax.random.split(key, 18)

    def nrm(k, shape, scale):
        return jax.random.normal(k, shape, F32) * scale

    win_buf = min(WINDOW, PAST_LEN)
    return {
        'x_prompt': nrm(ks[0], (BATCH, SEQ, D_MODEL), 1.0),
        'x_sample': nrm(ks[1], (DEC_BATCH, DEC_SEQ, D_MODEL), 1.0),
        'cache_k_win': nrm(ks[2], (DEPTH, DEC_BATCH, win_buf, ATTN_KV_HEADS, HEAD_DIM), 1.0),
        'cache_v_win': nrm(ks[3], (DEPTH, DEC_BATCH, win_buf, ATTN_KV_HEADS, HEAD_DIM), 1.0),
        'state_hgrn': nrm(ks[4], (DEPTH, DEC_BATCH, HG_HEADS, HG_DK, HG_DV), 0.5),
        'norm_mix_w': 1.0 + nrm(ks[5], (DEPTH, D_MODEL), 0.02),
        'w_in': nrm(ks[6], (DEPTH, D_MODEL, IN_WIDTH), D_MODEL ** -0.5),
        'attn_sinks': nrm(ks[7], (DEPTH, ATTN_HEADS), 0.5),
        'rel_bias_table': nrm(ks[8], (REL_BUCKETS, ATTN_HEADS), 0.5),
        'hg_lb': nrm(ks[9], (DEPTH + 1, HG_WIDTH), 0.1),
        'hg_norm_w': 1.0 + nrm(ks[10], (DEPTH, HG_WIDTH), 0.02),
        'w_o': nrm(ks[11], (DEPTH, MIX_WIDTH, D_MODEL), MIX_WIDTH ** -0.5),
        'norm_ffn_w': 1.0 + nrm(ks[12], (DEPTH, D_MODEL), 0.02),
        'peer_w_q': nrm(ks[13], (DEPTH, D_MODEL, PEER_HEADS * PEER_DKEY), D_MODEL ** -0.5),
        'peer_sub_keys': nrm(ks[14], (DEPTH, PEER_HEADS, 2, PEER_NKEYS, PEER_HALF), PEER_HALF ** -0.5),
        'peer_u': nrm(ks[15], (DEPTH, PEER_EXPERTS, D_MODEL), D_MODEL ** -0.5),
        'peer_v': nrm(ks[16], (DEPTH, PEER_EXPERTS, D_MODEL), 0.5),
        'norm_final_w': 1.0 + nrm(ks[17], (D_MODEL,), 0.02),
    }

def reference(x_prompt, x_sample, cache_k_win, cache_v_win, state_hgrn, norm_mix_w, w_in,
              attn_sinks, rel_bias_table, hg_lb, hg_norm_w, w_o, norm_ffn_w, peer_w_q,
              peer_sub_keys, peer_u, peer_v, norm_final_w):
    lower_bounds = jnp.cumsum(jax.nn.softmax(hg_lb.astype(F32), axis=0), axis=0)
    xp, xs = x_prompt, x_sample
    kp_l, vp_l, sp_l, ks_l, vs_l, ss_l = [], [], [], [], [], []
    for l in range(DEPTH):
        weights = (lower_bounds[l], norm_mix_w[l], w_in[l], attn_sinks[l], rel_bias_table, hg_norm_w[l],
                   w_o[l], norm_ffn_w[l], peer_w_q[l], peer_sub_keys[l], peer_u[l], peer_v[l])
        xp, kp, vp, sp = decoder_layer(xp, None, *weights)
        xs, ksm, vsm, ssm = decoder_layer(xs, (cache_k_win[l], cache_v_win[l], state_hgrn[l]), *weights)
        kp_l.append(kp)
        vp_l.append(vp)
        sp_l.append(sp)
        ks_l.append(ksm)
        vs_l.append(vsm)
        ss_l.append(ssm)
    y_prompt = rmsnorm(xp, norm_final_w)
    y_sample = rmsnorm(xs, norm_final_w)
    return (y_prompt, y_sample, jnp.stack(kp_l), jnp.stack(vp_l), jnp.stack(sp_l),
            jnp.stack(ks_l), jnp.stack(vs_l), jnp.stack(ss_l))


_drawn_inputs = setup_inputs


def setup_inputs(seed=0):
    import zlib

    import numpy as np

    out = dict(_drawn_inputs(seed))
    spreads = {}
    factors = {'attn_sinks': 25.521, 'norm_final_w': 8.105}
    for name, (base, spread) in spreads.items():
        noise = np.random.default_rng([zlib.crc32(name.encode()), seed]).standard_normal(out[name].shape)
        drawn = base * np.exp(spread * noise) if base else spread * noise
        out[name] = jnp.asarray(drawn.astype(out[name].dtype))
    for name, factor in factors.items():
        out[name] = (out[name] * factor).astype(out[name].dtype)
    return out
```

```python
from contextlib import ExitStack

import numpy as np
import concourse.bass as bass
from concourse import mybir

F32 = mybir.dt.float32
I32 = mybir.dt.int32
U32 = mybir.dt.uint32
U8 = mybir.dt.uint8
ALU = mybir.AluOpType
ACT = mybir.ActivationFunctionType
AX = mybir.AxisListType

P = 128
D = 1024
DC = D // P
SEQ, DEC_B, DEC_T = 1024, 8, 4
NS = DEC_B * DEC_T
TILES = SEQ // P
TOK = SEQ + NS
HEADS, KV, DH = 8, 2, 64
GRP = HEADS // KV
SCALE = DH ** -0.5
HG = 4
BUCKETS, WINDOW = 32, 128
NEG = -1.0e30
CHUNKS = 22
C_Q, C_K, C_V, C_QH, C_F, C_I, C_G = 0, 4, 5, 6, 10, 14, 18
PH, TOPK = 8, 16
PICKS = PH * TOPK
LEVELS = [64, 32, 16, 8, 4, 2, 1]
NL = len(LEVELS) + 1
LOWEST = -3.0e38
EPS = 1e-6
U_RING, V_RING = 8, 4
V_LAG = 3
SGRP = P // NS
S_OFF = (C_G + 4 - 1) * NS
LOOP = TILES - 2
DVE_PER, ACT_PER = 153, 14


def steps_of(tile):
    return PICKS // SGRP if isinstance(tile, int) and tile == TILES else PICKS


def hold(eng, semaphore, value, held):
    eng.wait_ge(semaphore, value)
    if not isinstance(value, int):
        eng.sem_inc(held, 1)


def summed(n):
    return n + 2


class Own:

    def __init__(self, eng, semaphore, per_turn):
        self.eng, self.semaphore, self.per_turn = eng, semaphore, per_turn
        self.count, self.turn, self.at_start = 0, None, 0

    def mark(self, instruction):
        self.count += 1
        instruction.then_inc(self.semaphore, 1)

    def settle(self):
        value = self.count if self.turn is None else self.turn * self.per_turn + self.count
        self.eng.wait_ge(self.semaphore, value)

    def settle_held(self, held):
        self.settle()
        if self.turn is not None:
            self.eng.sem_inc(held, 1)

    def begin(self, turn):
        self.turn, self.at_start = turn, self.count

    def end(self, turns):
        assert self.count - self.at_start == self.per_turn, (self.semaphore, self.count - self.at_start)
        self.count = self.at_start + turns * self.per_turn
        self.turn = None


def build(nc, a):
    proj = nc.dram_tensor("proj", (CHUNKS, P, TOK), F32, kind="Internal").ap()
    h_dram = nc.dram_tensor("h_dram", (TOK, D), F32, kind="Internal").ap()

    ctx = ExitStack()
    with ctx:
        def sb(name, shape, dt=F32):
            return ctx.enter_context(nc.sbuf_tensor(name, shape, dt))

        def sem(name):
            return ctx.enter_context(nc.semaphore(name))

        w_o = sb("w_o", [P, DC, D])
        w_q = sb("w_q", [P, DC, 2 * D])
        keys = sb("keys", [P, 2 * PH, P])
        rows = sb("rows", [P, (U_RING + V_RING) * D])
        hn_u = sb("hn_u", [P, D])
        hn = sb("hn", [P, D])
        hx = sb("hx", [P, D])
        bias = sb("bias", [P, HEADS * 2 * P])
        r1 = sb("r1", [P, (CHUNKS - 1) * P])
        r2 = sb("r2", [P, 2 * D])
        r3 = sb("r3", [P, D])
        state = sb("state", [P, HG, P])
        a_t = sb("a_t", [P, HG, P])
        diag = sb("diag", [P, 2, P])
        ident = sb("ident", [P, P])
        level_masks = sb("level_masks", [P, NL, P], U8)
        k_t = sb("k_t", [P, 2, P])
        v_n = sb("v_n", [P, 2, P])
        gate_f, gate_u, act_u, w_v = (sb(n, [P, PICKS]) for n in ("gate_f", "gate_u", "act_u", "w_v"))
        idx_f, idx_u, idx_v = (sb(n, [P, PICKS], I32) for n in ("idx_f", "idx_u", "idx_v"))
        small = sb("small", [P, 192])
        ps = ctx.enter_context(nc.psum_tensor("ps", [P, 8, 512], F32))
        Y = [ps[:, 0, :], ps[:, 1, :]]
        F = [ps[:, 2 + n, :] for n in range(6)]

        taken = [0]

        def vec(n):
            taken[0] += n
            return small[:, taken[0] - n:taken[0]]

        eps, one = vec(1), vec(1)
        w_mix = vec(DC)
        mix_scale = vec(DC)
        lb_in, lb, oml = vec(2 * HG), vec(HG), vec(HG)
        sinks, sinks_s = vec(HEADS), vec(KV)
        rmax, nmax, den, esink = vec(GRP), vec(HEADS), vec(HEADS), vec(HEADS)
        decay, ssq4 = vec(HG), vec(HG)
        ssq, rstd = vec(1), vec(1)
        ssq_y, rstd_y = vec(1), vec(1)
        gsum, iota16 = vec(PH), vec(TOPK)
        tsel, tab_rep, bsel = vec(DEC_T), vec(HEADS), vec(DEC_B)
        fold = vec(NS)
        assert taken[0] <= 192

        names = """consts_in weights_in x_a0 x_a1 a_ssq a_root a_scaled a_turned a_kept w_a0 w_a1
            wp_done kept_lo kept_hi proj_out0 proj_out1 table_in bias_mm bias_kept
            x_in proj_in wffn_in kv_shifted turned kept_ig v_kept
            scores s_masked p_ready p_turned p_kept pv mix_attn
            hg_f hg_ln hg_k lev_d lev_e lev_q lev_mm lev_kept
            qe_exp qe_ready kd_d kd_exp kd_ready kd_turned kd_kept hg_out s_new rms_root mix_ready
            mix_turned mix_kept h_mm h_ready h_stored ssq_root hn_ready hn_turned hn_kept hn_taken
            qry_mm qry_kept sc_mm sc_kept gate_d gate_exp topk_done idx_taken
            h_back wfin_in y_taken y_root y_ready y_out
            dots act_ready wv_ready diag_ready vsum
            own_dve own_act held_sp held_pool held_dve u_written v_written idx_moved
            caches_in out_kv k7_turned k7_kept set_up lb_shifted lb_exp s_turned s_tab_ready s_bias_mm s_bias_kept
            st_in0 st_in1 st_out0 st_out1 kdm_ready st_mm st_new ot_kept ot_turned o_kept""".split()
        S = {n: sem(n) for n in names}
        u_row = [sem(f"u_row{n}") for n in range(U_RING)]
        v_row = [sem(f"v_row{n}") for n in range(V_RING)]

        u_rows = rows[:, 0:U_RING * D].rearrange("p (r d) -> p r d", d=D)
        v_rows = rows[:, U_RING * D:].rearrange("p (r d) -> p r d", d=D)
        pj = r1[:, :].rearrange("p (c t) -> p c t", t=P)
        spj = r1[:, 0:S_OFF].rearrange("p (c t) -> p c t", t=NS)

        def slots(c, n, view=pj):
            c = c if c < C_K else c - 1
            return view[:, c:c + n, :]

        bias_v = bias[:, :].rearrange("p (h s) -> p h s", h=HEADS)
        probs = r2[:, 0:D].rearrange("p (h s) -> p h s", h=GRP)
        probs_t = r2[:, D:2 * D].rearrange("p (h b t) -> p h b t", h=GRP, b=2)
        lev = [r2[:, 0:512], r2[:, 512:1024]]
        kd_n, cum = r2[:, 1024:1536], r2[:, 1536:2048]
        mix = r3
        mix_t = r2[:, 0:D].rearrange("p (c t) -> p c t", c=DC)
        hn_t = r2[:, D:2 * D].rearrange("p (c t) -> p c t", c=DC)
        qry = [r2[:, 0:512].rearrange("p (c t) -> p c t", c=4), r2[:, 512:1024].rearrange("p (c t) -> p c t", c=4)]
        sc = r1[:, 0:2 * D].rearrange("p (c n) -> p c n", c=2 * PH)
        cand = r2[:, :].rearrange("p (h x) -> p h x", h=PH)
        sv = r3[:, 0:256].rearrange("p (c k) -> p c k", c=2 * PH)
        si = r3[:, 256:512].bitcast(U32).rearrange("p (c k) -> p c k", c=2 * PH)
        si_f = r3[:, 512:768].rearrange("p (c k) -> p c k", c=2 * PH)
        fv = r3[:, 768:896].rearrange("p (h k) -> p h k", h=PH)
        fi = r3[:, 896:1024].bitcast(U32).rearrange("p (h k) -> p h k", h=PH)
        onehot = r1[:, 0:2 * D].rearrange("p (x k) -> p x k", k=TOPK)
        pos = [r1[:, 2048 + n * PICKS:2048 + (n + 1) * PICKS] for n in range(4)]

        x_a = [rows[:, 0:D], rows[:, D:2 * D]]
        xn_t = rows[:, 2 * D:2 * D + DC * TOK].rearrange("p (c t) -> p c t", c=DC)
        staged = [rows[:, 2 * D + DC * TOK:2 * D + (DC + 1) * TOK], r2[:, 0:TOK]]
        wp = [r1[:, n * D:(n + 1) * D].rearrange("p (c n) -> p c n", c=DC) for n in range(2)]
        table, bucket_of = hn[0:BUCKETS + 1, 0:HEADS], hx[0:BUCKETS + 1, 0:3 * P - 1]

        kc_t = bias[:, 0:D]
        vc = bias[:, D:2 * D].rearrange("p (b x) -> p b x", b=DEC_B)
        s_probs = r2[:, 0:D + NS]
        s_probs_t = [r2[:, D + NS + c * P:D + NS + (c + 1) * P] if c < 7 else
                     hn[:, 660 + (c - 7) * P:660 + (c - 6) * P] for c in range(9)]
        s_mask = r1[:, S_OFF:S_OFF + D + NS]
        s_bias = hn[:, 0:264].rearrange("p (g j) -> p g j", g=KV)
        s_oh = hn[:, 264:396]
        s_tab = hn[:, 396:652]
        s_nat = r1[0:NS, S_OFF:S_OFF + D]
        s_st = [bias[:, 0:512], bias[:, 512:1024]]
        s_cum, s_reset = bias[:, 1024:1152], bias[:, 1152:1280]
        s_lev = [bias[:, 1280:1408], bias[:, 1408:1536]]
        s_qe, s_dec, s_ot = bias[:, 1536:1664], bias[:, 1664:1696], bias[:, 1696:1824]
        s_kdn, s_kdm = r2[0:NS, 1024:1536], [r2[0:NS, 0:512], r2[0:NS, 512:1024]]
        last_pos = DEC_T - 1

        x_tiles = a["x_prompt"].rearrange("(i p) d -> i p d", p=P)
        proj_tiles = proj[:, :, 0:SEQ].rearrange("c p (i t) -> i p c t", t=P)
        proj_s = proj[:, :, SEQ:TOK].rearrange("c p t -> p c t")
        h_tiles = h_dram[0:SEQ, :].rearrange("(i p) d -> i p d", p=P)
        y_tiles = a["y_prompt"].rearrange("(i p) d -> i p d", p=P)

        def ntok(f):
            return NS if isinstance(f, int) and f == TILES else P

        def is_sample(f):
            return isinstance(f, int) and f == TILES

        def periods(eng, own, body):
            body(-2)
            body(-1)
            with eng.Fori(0, LOOP) as p:
                if own:
                    own.begin(p)
                body(p)
                if own:
                    own.end(LOOP)
            for q in range(LOOP, TILES + 1):
                body(q)

        def parts(p):
            if isinstance(p, int):
                return (p if p >= 0 else None, p + 1 if -1 <= p < TILES else None,
                        p + 2 if p + 2 <= TILES else None)
            return p, p + 1, p + 2

        block = ctx.enter_context(nc.Block())

        @block.sync
        def _(sp):
            for dst, src in ((ident[:, :], "ident"), (w_mix, "norm_mix_t"), (mix_scale[:, 4:8], "hg_norm_t"),
                             (lb_in, "hg_lb_t"), (sinks, "sinks"), (sinks_s, "sinks_s"), (iota16, "iota16"),
                             (tsel, "tsel"), (tab_rep, "table_rep"), (bsel, "bsel"), (fold, "fold")):
                sp.dma_start(dst, a[src]).then_inc(S["consts_in"], 16)
            sp.dma_start(hn_u[:, :], a["level_masks"]).then_inc(S["consts_in"], 16)
            sp.dma_start(table[0:BUCKETS, :], a["table"]).then_inc(S["table_in"], 16)
            sp.dma_start(bucket_of, a["bucket_of"]).then_inc(S["table_in"], 16)

            for i in range(TILES + 1):
                if i >= 2:
                    sp.wait_ge(S["a_turned"], i - 1)
                if i < TILES:
                    sp.dma_start(x_a[i % 2], x_tiles[i]).then_inc(S[f"x_a{i % 2}"], 16)
                else:
                    sp.dma_start(x_a[i % 2][0:NS, :], a["x_sample"]).then_inc(S[f"x_a{i % 2}"], 16)
                if i < 2:
                    sp.dma_start(wp[i], a["w_in"][i]).then_inc(S[f"w_a{i}"], 16)
            sp.dma_start(w_o[:, :, :], a["w_o"].rearrange("(c p) n -> p c n", p=P)).then_inc(S["weights_in"], 16)
            sp.dma_start(w_q[:, :, :], a["w_q"].rearrange("(c p) n -> p c n", p=P)).then_inc(S["weights_in"], 16)
            sp.dma_start(keys[:, :, :], a["keys_t"]).then_inc(S["weights_in"], 16)
            with sp.Fori(0, CHUNKS // 2 - 1) as it:
                for j in range(2):
                    sp.wait_ge(S["wp_done"], 2 * it + j + 1)
                    sp.dma_start(wp[j], a["w_in"][2 * it + j + 2]).then_inc(S[f"w_a{j}"], 16)
                    sp.wait_ge(S["kept_lo"], 2 * it + j + 1)
                    sp.wait_ge(S["kept_hi"], 2 * it + j + 1)
                    sp.dma_start(proj[2 * it + j], staged[j]).then_inc(S[f"proj_out{j}"], 16)
            for j in range(2):
                sp.wait_ge(S["kept_lo"], CHUNKS - 1 + j)
                sp.wait_ge(S["kept_hi"], CHUNKS - 1 + j)
                sp.dma_start(proj[CHUNKS - 2 + j], staged[j]).then_inc(S[f"proj_out{j}"], 16)
            for j in range(2):
                sp.wait_ge(S[f"proj_out{j}"], 16 * (CHUNKS // 2))

            def body(p):
                v, u, f = parts(p)
                if f is not None:
                    sample = is_sample(f)
                    first = isinstance(f, int) and f == 0
                    n = ntok(f)
                    if first:
                        sp.wait_ge(S["bias_mm"], 1)
                    else:
                        hold(sp, S["hn_ready"], f, S["held_sp"])
                    sp.dma_start(hx[0:n, :], a["x_sample"] if sample else x_tiles[f]).then_inc(S["x_in"], 16)
                    if not first:
                        hold(sp, S["topk_done"], f, S["held_sp"])
                    if sample:
                        sp.dma_start(a["v_win_prompt"], v_n[:, 1, :]).then_inc(S["out_kv"], 16)
                        sp.dma_start(a["state_prompt"], state[:, :, :]).then_inc(S["out_kv"], 16)
                        sp.wait_ge(S["k7_kept"], 1)
                        sp.dma_start(a["k_win_prompt"], r3[:, 896:1024]).then_inc(S["out_kv"], 16)
                        for out_name, in_name in (("k_win_sample", "cache_k"), ("v_win_sample", "cache_v")):
                            sp.dma_start(a[out_name][:, 0:WINDOW - DEC_T, :], a[in_name][:, DEC_T:WINDOW, :])\
                              .then_inc(S["out_kv"], 16)
                        sp.dma_start(kc_t.rearrange("p (b j) -> p b j", b=DEC_B), a["cache_k_t"].rearrange("b p j -> p b j"))\
                          .then_inc(S["caches_in"], 16)
                        sp.dma_start(vc, a["cache_v"].rearrange("b j x -> j b x")).then_inc(S["caches_in"], 16)
                        sp.dma_start(s_mask, a["s_mask"]).then_inc(S["caches_in"], 16)
                        sp.wait_ge(S["hn_taken"], TILES)
                        sp.dma_start(s_oh, a["s_onehot"]).then_inc(S["caches_in"], 16)
                        sp.dma_start(k_t[:, 1, 0:NS], proj_s[:, C_K, :]).then_inc(S["proj_in"], 16)
                        sp.dma_start(spj[:, 0:C_K, :], proj_s[:, 0:C_K, :]).then_inc(S["proj_in"], 16)
                        sp.dma_start(spj[:, C_K:, :], proj_s[:, C_V:, :]).then_inc(S["proj_in"], 16)
                    else:
                        if not first:
                            sp.wait_ge(S["kv_shifted"], f + 1)
                        sp.dma_start(k_t[:, 1, :], proj_tiles[f, :, C_K, :]).then_inc(S["proj_in"], 16)
                        sp.dma_start(pj[:, 0:C_K, :], proj_tiles[f, :, 0:C_K, :]).then_inc(S["proj_in"], 16)
                        sp.dma_start(pj[:, C_K:, :], proj_tiles[f, :, C_V:, :]).then_inc(S["proj_in"], 16)
                    if sample:
                        sp.wait_ge(S["v_kept"], f + 2)
                        for b in range(DEC_B):
                            sp.dma_start(a["k_win_sample"][b, WINDOW - DEC_T:WINDOW, :],
                                         r3[DEC_T * b:DEC_T * (b + 1), 896:1024]).then_inc(S["out_kv"], 16)
                            sp.dma_start(a["v_win_sample"][b, WINDOW - DEC_T:WINDOW, :],
                                         v_n[DEC_T * b:DEC_T * (b + 1), 1, :]).then_inc(S["out_kv"], 16)
                        sp.wait_ge(S["pv"], 2 * f + 2)
                        for b in range(DEC_B):
                            if b >= 2:
                                sp.wait_ge(S["st_new"], b - 1)
                                sp.dma_start(a["state_out"][b - 2], s_st[b % 2]).then_inc(S[f"st_out{b % 2}"], 16)
                                sp.wait_ge(S[f"st_out{b % 2}"], 16 * (b // 2))
                            sp.dma_start(s_st[b % 2].rearrange("p (h x) -> p h x", h=HG), a["state_in"][b])\
                              .then_inc(S[f"st_in{b % 2}"], 16)
                        for b in range(DEC_B - 2, DEC_B):
                            sp.wait_ge(S["st_new"], b + 1)
                            sp.dma_start(a["state_out"][b], s_st[b % 2]).then_inc(S[f"st_out{b % 2}"], 16)
                            sp.wait_ge(S[f"st_out{b % 2}"], 16 * (DEC_B // 2))
                    sp.wait_ge(S["mix_turned"], f + 1)
                    sp.dma_start(r3[:, :], a["norm_ffn"]).then_inc(S["wffn_in"], 16)
                    hold(sp, S["h_ready"], f + 1, S["held_sp"])
                    h_at = h_dram[SEQ:TOK, :] if sample else h_tiles[f]
                    sp.dma_start(h_at, hx[0:n, :]).then_inc(S["h_stored"], 16)
                    sp.wait_ge(S["h_stored"], 16 * f + 16)
                if v is not None:
                    if f is not None:
                        sp.wait_ge(S["hn_ready"], f + 1)
                        hold(sp, S["topk_done"], f + 1, S["held_sp"])
                    nv = ntok(v)
                    sp.dma_start(hx[0:nv, :], h_dram[SEQ:TOK, :] if is_sample(v) else h_tiles[v])\
                      .then_inc(S["h_back"], 16)
                    sp.dma_start(r3[:, :], a["norm_final"]).then_inc(S["wfin_in"], 16)
                    hold(sp, S["y_ready"], v + 1, S["held_sp"])
                    sp.dma_start(a["y_sample"] if is_sample(v) else y_tiles[v], hx[0:nv, :]).then_inc(S["y_out"], 16)
                    hold(sp, S["y_out"], 16 * v + 16, S["held_sp"])

            periods(sp, None, body)
            sp.wait_ge(S["y_out"], 16 * (TILES + 1))
            sp.wait_ge(S["out_kv"], 16 * (3 + 2 + 2 * DEC_B))

        @block.gpsimd
        def _(pool):
            def body(p):
                v, u, f = parts(p)
                for k in range(PICKS + V_LAG):
                    if u is not None and k < steps_of(u):
                        if k == 0 and isinstance(p, int) and p == -1:
                            pool.wait_ge(S["proj_out0"], 16 * (CHUNKS // 2))
                            pool.wait_ge(S["proj_out1"], 16 * (CHUNKS // 2))
                        if not (isinstance(p, int) and p == -1 and k < U_RING):
                            hold(pool, S["dots"], PICKS * u + k - U_RING + 1, S["held_pool"])
                        nc.gpsimd.indirect_dma_start(
                            u_rows[:, k % U_RING, :], None, a["peer_u"],
                            bass.IndirectOffsetOnAxis(ap=idx_u[:, k:k + 1], axis=0), engine_sem=S["u_written"])\
                            .then_inc(u_row[k % U_RING], 16)
                    kv = k - V_LAG
                    if v is not None and 0 <= kv < steps_of(v):
                        if isinstance(p, int) or kv >= V_RING:
                            hold(pool, S["vsum"], summed(PICKS * v + kv - V_RING + 1), S["held_pool"])
                        else:
                            hold(pool, S["vsum"], summed(PICKS * v), S["held_pool"])
                        nc.gpsimd.indirect_dma_start(
                            v_rows[:, kv % V_RING, :], None, a["peer_v"],
                            bass.IndirectOffsetOnAxis(ap=idx_v[:, kv:kv + 1], axis=0), engine_sem=S["v_written"])\
                            .then_inc(v_row[kv % V_RING], 16)
                if f is not None or u is not None:
                    if u is not None:
                        pool.wait_ge(S["dots"], PICKS * u + steps_of(u))
                        if v is not None:
                            hold(pool, S["vsum"], summed(PICKS * v + steps_of(v)), S["held_pool"])
                        nc.gpsimd.tensor_copy(idx_v[:, :], idx_u[:, :]).then_inc(S["idx_moved"], 1)
                        hold(pool, S["idx_moved"], u + 1, S["held_pool"])
                    if f is not None:
                        hold(pool, S["topk_done"], f + 1, S["held_pool"])
                        nc.gpsimd.tensor_copy(idx_u[:, :], idx_f[:, :]).then_inc(S["idx_taken"], 1)
                        hold(pool, S["idx_taken"], f + 1, S["held_pool"])

            periods(pool, None, body)

        @block.scalar
        def _(act):
            own = Own(act, S["own_act"], ACT_PER)
            act.wait_ge(S["consts_in"], 16 * 12)

            act.wait_ge(S["set_up"], 1)
            act.wait_ge(S["lb_shifted"], 1)
            nc.scalar.activation(lb_in, lb_in, ACT.Exp).then_inc(S["lb_exp"], 1)
            for i in range(TILES + 1):
                n = P if i < TILES else NS
                act.wait_ge(S[f"x_a{i % 2}"], 16 * (i // 2 + 1))
                if i >= 1:
                    act.wait_ge(S["a_scaled"], i)
                own.settle() if i else None
                own.mark(nc.scalar.activation(r3[0:n, :], x_a[i % 2][0:n, :], ACT.Square, accum_out=ssq[0:n, :]))
                own.settle()
                nc.scalar.activation(rstd[0:n, :], ssq[0:n, :], ACT.Sqrt, bias=eps[0:n, :], scale=1.0 / D)\
                  .then_inc(S["a_root"], 1)
            def keep_low(it, first):
                for j in range(2):
                    act.wait_ge(S["wp_done"], 2 * it + j + 1)
                    if not first:
                        act.wait_ge(S[f"proj_out{j}"], 16 * it)
                    nc.scalar.activation(staged[j][:, 0:512], ps[:, 3 * j, :], ACT.Copy).then_inc(S["kept_lo"], 1)
            keep_low(0, True)
            with act.Fori(1, CHUNKS // 2) as it:
                keep_low(it, False)

            def exps(f, kv, lo):
                act.wait_ge(S["s_masked"], 2 * f + kv + 1)
                for j in range(GRP):
                    h = GRP * kv + j
                    own.mark(nc.scalar.activation(probs[:, j, lo:2 * P], probs[:, j, lo:2 * P], ACT.Exp,
                                                  bias=nmax[:, h:h + 1], accum_out=den[:, h:h + 1]))
                nc.scalar.activation(esink[:, GRP * kv:GRP * (kv + 1)], esink[:, GRP * kv:GRP * (kv + 1)], ACT.Exp)\
                  .then_inc(S["p_ready"], 1)

            def keep_probs(f, kv, first):
                act.wait_ge(S["p_turned"], 2 * f + kv + 1)
                act.wait_ge(S["pv"], 2 * f + kv)
                for j in range(2):
                    bank = F[(3 if kv == 0 else 0) + j].rearrange("p (h b t) -> p h b t", h=2, b=2)
                    lo = 1 if first else 0
                    last = nc.scalar.activation(probs_t[:, 2 * j:2 * j + 2, lo:2, :], bank[:, :, lo:2, :], ACT.Copy)
                last.then_inc(S["p_kept"], 1)

            def front(k, f):
                first = isinstance(f, int) and f == 0
                n = NS if is_sample(f) else P
                if not is_sample(f):
                    if k == 1 and not first:
                        act.wait_ge(S["pv"], 2 * f)
                        nc.scalar.activation(v_n[:, 0, :], v_n[:, 1, :], ACT.Copy)
                        nc.scalar.activation(k_t[:, 0, :], k_t[:, 1, :], ACT.Copy).then_inc(S["kv_shifted"], 1)
                    if k == 1 and first:
                        nc.scalar.activation(k_t[:, 0, 0:1], eps, ACT.Copy).then_inc(S["kv_shifted"], 1)
                    if k == 6:
                        act.wait_ge(S["turned"], f + 1)
                        act.wait_ge(S["proj_in"], 48 * f + 48)
                        nc.scalar.activation(slots(C_I, 4), F[0].rearrange("p (c t) -> p c t", c=4), ACT.Copy)
                        nc.scalar.activation(slots(C_G, 4), F[1].rearrange("p (c t) -> p c t", c=4), ACT.Silu)
                        nc.scalar.activation(v_n[:, 1, :], F[2][:, 0:P], ACT.Copy).then_inc(S["v_kept"], 1)
                        nc.scalar.activation(slots(C_QH, 4), slots(C_QH, 4), ACT.Silu)
                        nc.scalar.activation(slots(C_F, 4), slots(C_F, 4), ACT.Sigmoid).then_inc(S["kept_ig"], 1)
                    for kv in range(KV):
                        if k == 12 + 7 * kv:
                            exps(f, kv, P if first else 0)
                        if k == 16 + 7 * kv:
                            keep_probs(f, kv, first)
                    if k == 29:
                        act.wait_ge(S["hg_f"], f + 1)
                        act.wait_ge(S["pv"], 2 * f + 2)
                        nc.scalar.activation(cum.rearrange("p (c t) -> p c t", c=4), slots(C_F, 4), ACT.Ln)\
                          .then_inc(S["hg_ln"], 1)
                    for l in range(NL - 1):
                        if k == 33 + 3 * l:
                            act.wait_ge(S["lev_d"], (NL - 1) * f + l + 1)
                            nc.scalar.activation(lev[l % 2], lev[l % 2], ACT.Exp).then_inc(S["lev_e"], 1)
                    if k == 37:
                        act.wait_ge(S["hg_k"], f + 1)
                        nc.scalar.activation(slots(C_Q, 4), cum.rearrange("p (c t) -> p c t", c=4), ACT.Exp)\
                          .then_inc(S["qe_exp"], 1)
                    if k == 55:
                        act.wait_ge(S["kd_d"], f + 1)
                        nc.scalar.activation(lev[1], lev[1], ACT.Exp).then_inc(S["kd_exp"], 1)
                    if k == 59:
                        act.wait_ge(S["kd_turned"], f + 1)
                        nc.scalar.activation(kd_n, F[2], ACT.Copy).then_inc(S["kd_kept"], 1)
                    if k == 63:
                        act.wait_ge(S["hg_out"], f + 1)
                        nc.scalar.activation(mix[:, 512:1024], F[3], ACT.Copy)
                        for h in range(HG):
                            own.mark(nc.scalar.activation(lev[0][:, P * h:P * (h + 1)], F[3][:, P * h:P * (h + 1)],
                                                          ACT.Square, accum_out=ssq4[:, h:h + 1]))
                        own.settle()
                        nc.scalar.activation(ssq4, ssq4, ACT.Sqrt, bias=eps, scale=1.0 / P).then_inc(S["rms_root"], 1)
                else:
                    sample_front(k, f)
                if k == 81:
                    act.wait_ge(S["h_ready"], f + 1)
                    own.mark(nc.scalar.activation(r2[0:n, 0:D], hx[0:n, :], ACT.Square, accum_out=ssq[0:n, :]))
                    own.settle()
                    nc.scalar.activation(rstd[0:n, :], ssq[0:n, :], ACT.Sqrt, bias=eps[0:n, :], scale=1.0 / D)\
                      .then_inc(S["ssq_root"], 1)
                if k == 84:
                    act.wait_ge(S["hn_turned"], f + 1)
                    for j in range(2):
                        last = nc.scalar.activation(hn_t[:, 4 * j:4 * j + 4, 0:n],
                                                    F[4 + j][:, 0:4 * n].rearrange("p (c t) -> p c t", c=4), ACT.Copy)
                    last.then_inc(S["hn_kept"], 1)
                for g in range(4):
                    if k == 87 + 3 * g:
                        act.wait_ge(S["qry_mm"], 4 * f + g + 1)
                        if g >= 2:
                            act.wait_ge(S["sc_mm"], 4 * f + g - 1)
                        nc.scalar.activation(qry[g % 2][:, :, 0:n], F[g % 2][:, 0:4 * n].rearrange("p (c t) -> p c t", c=4),
                                             ACT.Copy).then_inc(S["qry_kept"], 1)
                    if k == 89 + 3 * g:
                        act.wait_ge(S["sc_mm"], 4 * f + g + 1)
                        nc.scalar.activation(sc[0:n, 4 * g:4 * g + 4, :], F[2 + g % 2][0:n, :].rearrange("p (c t) -> p c t", c=4),
                                             ACT.Copy).then_inc(S["sc_kept"], 1)
                if k == 114:
                    act.wait_ge(S["gate_d"], f + 1)
                    nc.scalar.activation(fv[0:n], gate_f[0:n, :].rearrange("p (h k) -> p h k", h=PH), ACT.Exp).then_inc(S["gate_exp"], 1)

            def sample_front(k, f):
                if k == 1:
                    act.wait_ge(S["k7_turned"], 1)
                    act.wait_ge(S["y_ready"], f - 2)
                    nc.scalar.activation(r3[:, 896:1024], F[5][:, 0:P], ACT.Copy).then_inc(S["k7_kept"], 1)
                if k == 6:
                    act.wait_ge(S["turned"], f + 1)
                    act.wait_ge(S["out_kv"], 16 * 5)
                    nc.scalar.activation(v_n[0:NS, 1, :], F[2][0:NS, 0:P], ACT.Copy).then_inc(S["v_kept"], 1)
                    nc.scalar.activation(r3[0:NS, 896:1024], F[2][0:NS, P:2 * P], ACT.Copy).then_inc(S["v_kept"], 1)
                if k == 9:
                    act.wait_ge(S["s_bias_mm"], 1)
                    nc.scalar.activation(s_bias, F[5][:, 0:264].rearrange("p (g j) -> p g j", g=KV), ACT.Copy)\
                      .then_inc(S["s_bias_kept"], 1)
                for kv in range(KV):
                    if k == 14 + 14 * kv:
                        act.wait_ge(S["s_masked"], 2 * f + kv + 1)
                        own.mark(nc.scalar.activation(s_probs, s_probs, ACT.Exp, bias=nmax[:, kv:kv + 1],
                                                      accum_out=den[:, kv:kv + 1]))
                        nc.scalar.activation(esink[:, kv:kv + 1], esink[:, kv:kv + 1], ACT.Exp).then_inc(S["p_ready"], 1)
                    if k == 18 + 14 * kv:
                        act.wait_ge(S["p_turned"], 2 * f + kv + 1)
                        for c in range(9):
                            m = P if c < 8 else NS
                            src = F[3 + c // 4][0:m, P * (c % 4):P * (c % 4 + 1)]
                            last = nc.scalar.activation(s_probs_t[c][0:m, :], src, ACT.Copy)
                        last.then_inc(S["p_kept"], 1)
                if k == 42:
                    act.wait_ge(S["s_turned"], 1)
                    nc.scalar.activation(s_nat[:, 0:512], F[0][0:NS, :], ACT.Copy)
                    nc.scalar.activation(s_nat[:, 512:1024], F[1][0:NS, :], ACT.Silu)
                    nc.scalar.activation(slots(C_QH, 4, spj), slots(C_QH, 4, spj), ACT.Silu)
                    nc.scalar.activation(slots(C_F, 4, spj), slots(C_F, 4, spj), ACT.Sigmoid).then_inc(S["kept_ig"], 1)
                if k == 44:
                    act.wait_ge(S["hg_f"], f + 1)
                    nc.scalar.activation(s_cum.rearrange("p (c t) -> p c t", c=4), slots(C_F, 4, spj), ACT.Ln)\
                      .then_inc(S["hg_ln"], 1)
                for l in range(2):
                    if k == 48 + 2 * l:
                        act.wait_ge(S["lev_d"], (NL - 1) * f + l + 1)
                        nc.scalar.activation(s_lev[l], s_lev[l], ACT.Exp).then_inc(S["lev_e"], 1)
                if k == 50:
                    nc.scalar.activation(s_qe, s_cum, ACT.Exp).then_inc(S["qe_exp"], 1)
                if k == 54:
                    act.wait_ge(S["kd_d"], f + 1)
                    nc.scalar.activation(s_lev[0], s_lev[0], ACT.Exp).then_inc(S["kd_exp"], 1)
                if k == 58:
                    act.wait_ge(S["kd_turned"], f + 1)
                    nc.scalar.activation(s_kdn, F[2][0:NS, :], ACT.Copy).then_inc(S["kd_kept"], 1)
                if k == 69:
                    act.wait_ge(S["st_mm"], DEC_B)
                    nc.scalar.activation(s_ot, F[4][:, 0:P], ACT.Copy).then_inc(S["ot_kept"], 1)
                if k == 71:
                    act.wait_ge(S["ot_turned"], 1)
                    act.wait_ge(S["out_kv"], 16 * (5 + 2 * DEC_B))
                    nc.scalar.activation(mix[0:NS, 512:1024], F[5][0:NS, :], ACT.Copy).then_inc(S["o_kept"], 1)
                if k == 73:
                    act.wait_ge(S["o_kept"], 2)
                    for h in range(HG):
                        own.mark(nc.scalar.activation(r2[0:NS, P * h:P * (h + 1)], mix[0:NS, 512 + P * h:512 + P * (h + 1)],
                                                      ACT.Square, accum_out=ssq4[0:NS, h:h + 1]))
                    own.settle()
                    nc.scalar.activation(ssq4[0:NS, :], ssq4[0:NS, :], ACT.Sqrt, bias=eps[0:NS, :], scale=1.0 / P)\
                      .then_inc(S["rms_root"], 1)

            def body(p):
                v, u, f = parts(p)
                for k in range(PICKS):
                    if v is not None and k < steps_of(v):
                        if k == 0:
                            act.wait_ge(S["wv_ready"], v + 1)
                        act.wait_ge(S["vsum"], summed(PICKS * v + k - 1))
                        m = NS if is_sample(v) else P
                        nc.scalar.activation(diag[:, k % 2, 0:m], fold if is_sample(v) else ident[:, :], ACT.Copy,
                                             scale=w_v[:, k:k + 1]).then_inc(S["diag_ready"], 1)
                    if f is not None:
                        front(k, f)
                if u is not None:
                    act.wait_ge(S["dots"], PICKS * u + steps_of(u))
                    nc.scalar.activation(act_u[:, 0:steps_of(u)], act_u[:, 0:steps_of(u)], ACT.Gelu)\
                      .then_inc(S["act_ready"], 1)
                if v is not None:
                    m = ntok(v)
                    act.wait_ge(S["y_taken"], v + 1)
                    own.mark(nc.scalar.activation(r2[0:m, 0:D], hx[0:m, :], ACT.Square, accum_out=ssq_y[0:m, :]))
                    own.settle()
                    nc.scalar.activation(rstd_y[0:m, :], ssq_y[0:m, :], ACT.Sqrt, bias=eps[0:m, :], scale=1.0 / D)\
                      .then_inc(S["y_root"], 1)

            periods(act, own, body)

        @block.tensor
        def _(pe):
            pe.wait_ge(S["consts_in"], 16 * 12)
            for i in range(TILES + 1):
                n = P if i < TILES else NS
                pe.wait_ge(S["a_scaled"], i + 1)
                for j in range(2):
                    if i >= 1:
                        pe.wait_ge(S["a_kept"], 2 * i - 1 + j)
                    for c in range(4):
                        cc = 4 * j + c
                        last = nc.tensor.transpose(ps[:, j, c * P:c * P + n], x_a[i % 2][0:n, cc * P:(cc + 1) * P],
                                                   ident[0:n, 0:n])
                last.then_inc(S["a_turned"], 1)
            pe.wait_ge(S["table_in"], 32)
            pe.wait_ge(S["set_up"], 1)
            bias_ps = ps[:, 2:6, :].rearrange("p b (k h) -> p (b k) h", h=HEADS)
            for key in range(2 * P):
                off = 2 * P - 1 - key
                last = nc.tensor.matmul(bias_ps[:, key, :], bucket_of[:, off:off + P], table, start=True, stop=True)
            last.then_inc(S["bias_mm"], 1)
            pe.wait_ge(S["a_kept"], 2 * (TILES + 1))
            pe.wait_ge(S["bias_kept"], 1)
            def project(it, first):
                for j in range(2):
                    pe.wait_ge(S[f"w_a{j}"], 16 * it + 16)
                    if not first:
                        pe.wait_ge(S["kept_lo"], 2 * it - 1 + j)
                        pe.wait_ge(S["kept_hi"], 2 * it - 1 + j)
                    for b, (lo, hi) in enumerate(((0, 512), (512, 1024), (1024, TOK))):
                        for c in range(DC):
                            last = nc.tensor.matmul(ps[:, 3 * j + b, 0:hi - lo], wp[j][:, c, :], xn_t[:, c, lo:hi],
                                                    start=(c == 0), stop=(c == DC - 1))
                    last.then_inc(S["wp_done"], 1)
            project(0, True)
            with pe.Fori(1, CHUNKS // 2) as it:
                project(it, False)

            def turn(bank, src, count, n=P, m=P):
                for c in range(count):
                    last = nc.tensor.transpose(bank[0:m, c * n:(c + 1) * n], src[0:n, c * m:(c + 1) * m], ident[0:n, 0:n])
                return last

            def front(k, f):
                first = isinstance(f, int) and f == 0
                lo = 1 if first else 0
                n = NS if is_sample(f) else P
                if is_sample(f):
                    sample_front(k, f)
                else:
                    if k == 4:
                        if first:
                            pe.wait_ge(S["kept_lo"], CHUNKS)
                            pe.wait_ge(S["kept_hi"], CHUNKS)
                            pe.wait_ge(S["weights_in"], 48)
                        pe.wait_ge(S["proj_in"], 48 * f + 48)
                        for c in range(4):
                            nc.tensor.transpose(F[0][:, P * c:P * (c + 1)], slots(C_I + c, 1)[:, 0, :], ident[:, :])
                        for c in range(4):
                            nc.tensor.transpose(F[1][:, P * c:P * (c + 1)], slots(C_G + c, 1)[:, 0, :], ident[:, :])
                        nc.tensor.transpose(F[2][:, 0:P], slots(C_V, 1)[:, 0, :], ident[:, :]).then_inc(S["turned"], 1)
                    for kv in range(KV):
                        part = slice(DH * kv, DH * (kv + 1))
                        base = 3 if kv == 0 else 0
                        if k == 8 + 4 * kv:
                            pe.wait_ge(S["kept_ig"], f + 1)
                            pe.wait_ge(S["kv_shifted"], f + 1)
                            for j in range(GRP):
                                last = nc.tensor.matmul(F[base + j // 2][:, 256 * (j % 2) + P * lo:256 * (j % 2) + 256],
                                                        slots(C_Q + j, 1)[part, 0, :], k_t[part, lo:2, :],
                                                        start=True, stop=True)
                            last.then_inc(S["scores"], 1)
                        if k == 14 + 7 * kv:
                            pe.wait_ge(S["p_ready"], 2 * f + kv + 1)
                            for j in range(GRP):
                                for b in range(lo, 2):
                                    last = nc.tensor.transpose(F[base + j // 2][:, 256 * (j % 2) + P * b:256 * (j % 2) + P * (b + 1)],
                                                               probs[:, j, P * b:P * (b + 1)], ident[:, :])
                            last.then_inc(S["p_turned"], 1)
                        if k == 18 + 7 * kv:
                            pe.wait_ge(S["p_kept"], 2 * f + kv + 1)
                            pe.wait_ge(S["v_kept"], f + 1)
                            for j in range(GRP):
                                h = GRP * kv + j
                                for b in range(lo, 2):
                                    last = nc.tensor.matmul(F[5][:, DH * h:DH * (h + 1)], probs_t[:, j, b, :],
                                                            v_n[:, b, part], start=(b == lo), stop=(b == 1))
                            last.then_inc(S["pv"], 1)
                    for l in range(NL):
                        if k == 35 + 3 * l:
                            if l < NL - 1:
                                pe.wait_ge(S["lev_q"], (NL - 1) * f + l + 1)
                                lhs = rhs = lev[l % 2].rearrange("p (c t) -> p c t", c=4)
                            else:
                                lhs, rhs = slots(C_F, 4), slots(C_QH, 4)
                            if l >= 2:
                                pe.wait_ge(S["lev_kept"], NL * f + l - 1)
                            for h in range(HG):
                                last = nc.tensor.matmul(F[l % 2][:, P * h:P * (h + 1)], lhs[:, h, :], rhs[:, h, :],
                                                        start=True, stop=True)
                            last.then_inc(S["lev_mm"], 1)
                    if k == 58:
                        pe.wait_ge(S["kd_ready"], f + 1)
                        turn(F[2], lev[1], HG).then_inc(S["kd_turned"], 1)
                    if k == 61:
                        pe.wait_ge(S["lev_kept"], NL * f + NL)
                        pe.wait_ge(S["kd_kept"], f + 1)
                        pe.wait_ge(S["qe_ready"], f + 1)
                        pe.wait_ge(S["s_new"], f)
                        for h in range(HG):
                            cols = slice(P * h, P * (h + 1))
                            nc.tensor.matmul(F[3][:, cols], a_t[:, h, :], slots(C_I, 4)[:, h, :], start=True, stop=False)
                            nc.tensor.matmul(F[3][:, cols], slots(C_Q, 4)[:, h, :], state[:, h, :], start=False, stop=True)
                        for h in range(HG):
                            cols = slice(P * h, P * (h + 1))
                            last = nc.tensor.matmul(F[4][:, cols], kd_n[:, cols], slots(C_I, 4)[:, h, :], start=True, stop=True)
                        last.then_inc(S["hg_out"], 1)
                if k == 75:
                    pe.wait_ge(S["mix_ready"], f + 1)
                    turn(F[0], mix[:, 0:512], 4, n)
                    turn(F[1], mix[:, 512:1024], 4, n).then_inc(S["mix_turned"], 1)
                if k in (77, 79):
                    j = (k - 77) // 2
                    pe.wait_ge(S["mix_kept"], f + 1)
                    for c in range(DC):
                        last = nc.tensor.matmul(F[2 + j][0:n, :], mix_t[:, c, 0:n], w_o[:, c, 512 * j:512 * (j + 1)],
                                                start=(c == 0), stop=(c == DC - 1))
                    last.then_inc(S["h_mm"], 1)
                if k == 83:
                    pe.wait_ge(S["hn_ready"], f + 1)
                    turn(F[4], hn[:, 0:512], 4, n)
                    turn(F[5], hn[:, 512:1024], 4, n).then_inc(S["hn_turned"], 1)
                for g in range(4):
                    if k == 86 + 3 * g:
                        pe.wait_ge(S["hn_kept"], f + 1)
                        if g >= 2:
                            pe.wait_ge(S["qry_kept"], 4 * f + g - 1)
                        for c in range(4):
                            cc = 4 * g + c
                            for d in range(DC):
                                last = nc.tensor.matmul(F[g % 2][:, c * n:(c + 1) * n], w_q[:, d, P * cc:P * (cc + 1)],
                                                        hn_t[:, d, 0:n], start=(d == 0), stop=(d == DC - 1))
                        last.then_inc(S["qry_mm"], 1)
                    if k == 88 + 3 * g:
                        pe.wait_ge(S["qry_kept"], 4 * f + g + 1)
                        if g >= 2:
                            pe.wait_ge(S["sc_kept"], 4 * f + g - 1)
                        for c in range(4):
                            last = nc.tensor.matmul(F[2 + g % 2][0:n, P * c:P * (c + 1)], qry[g % 2][:, c, 0:n],
                                                    keys[:, 4 * g + c, :], start=True, stop=True)
                        last.then_inc(S["sc_mm"], 1)

            def sample_front(k, f):
                if k == 1:
                    nc.tensor.transpose(F[5][:, 0:P], k_t[:, 1, :], ident[:, :]).then_inc(S["k7_turned"], 1)
                if k == 4:
                    pe.wait_ge(S["proj_in"], 48 * f + 48)
                    nc.tensor.transpose(F[2][0:NS, 0:P], slots(C_V, 1, spj)[:, 0, :], ident[:, :])
                    nc.tensor.transpose(F[2][0:NS, P:2 * P], k_t[:, 1, 0:NS], ident[:, :]).then_inc(S["turned"], 1)
                if k == 7:
                    pe.wait_ge(S["s_tab_ready"], 2)
                    pe.wait_ge(S["caches_in"], 64)
                    pe.wait_ge(S["k7_kept"], 1)
                    for g in range(KV):
                        last = nc.tensor.matmul(F[5][:, 132 * g:132 * (g + 1)], s_tab[:, P * g:P * (g + 1)], s_oh,
                                                start=True, stop=True)
                    last.then_inc(S["s_bias_mm"], 1)
                for kv in range(KV):
                    part = slice(DH * kv, DH * (kv + 1))
                    if k == 10 + 14 * kv:
                        if kv == 0:
                            pe.wait_ge(S["v_kept"], f + 2)
                        else:
                            pe.wait_ge(S["mix_attn"], f + kv)
                        for j in range(GRP):
                            q = slots(C_Q + j, 1, spj)[part, 0, :]
                            out_rows = slice(NS * j, NS * (j + 1))
                            nc.tensor.matmul(F[0][out_rows, :], q, kc_t[part, 0:512], start=True, stop=True)
                            nc.tensor.matmul(F[1][out_rows, :], q, kc_t[part, 512:1024], start=True, stop=True)
                            last = nc.tensor.matmul(F[2][out_rows, 0:NS], q, k_t[part, 1, 0:NS], start=True, stop=True)
                        last.then_inc(S["scores"], 1)
                    if k == 16 + 14 * kv:
                        pe.wait_ge(S["p_ready"], 2 * f + kv + 1)
                        pe.wait_ge(S["s_bias_kept"], 1)
                        for c in range(9):
                            m = P if c < 8 else NS
                            last = nc.tensor.transpose(F[3 + c // 4][0:m, P * (c % 4):P * (c % 4 + 1)],
                                                       s_probs[:, P * c:P * c + m], ident[:, :])
                        last.then_inc(S["p_turned"], 1)
                    if k == 20 + 14 * kv:
                        pe.wait_ge(S["p_kept"], 2 * f + kv + 1)
                        for c in range(9):
                            m = P if c < 8 else NS
                            values = vc[:, c, part] if c < 8 else v_n[0:NS, 1, part]
                            last = nc.tensor.matmul(F[2][:, 64:128], s_probs_t[c][0:m, :], values,
                                                    start=(c == 0), stop=(c == 8))
                        last.then_inc(S["pv"], 1)
                if k == 40:
                    for c in range(4):
                        nc.tensor.transpose(F[0][0:NS, P * c:P * (c + 1)], slots(C_I + c, 1, spj)[:, 0, :], ident[:, :])
                    for c in range(4):
                        last = nc.tensor.transpose(F[1][0:NS, P * c:P * (c + 1)], slots(C_G + c, 1, spj)[:, 0, :], ident[:, :])
                    last.then_inc(S["s_turned"], 1)
                for l in range(3):
                    if k == 50 + 2 * l:
                        if l < 2:
                            pe.wait_ge(S["lev_q"], (NL - 1) * f + l + 1)
                            lhs = rhs = s_lev[l].rearrange("p (c t) -> p c t", c=4)
                        else:
                            lhs, rhs = slots(C_F, 4, spj), slots(C_QH, 4, spj)
                        if l == 0:
                            pe.wait_ge(S["kept_ig"], f + 1)
                        else:
                            pe.wait_ge(S["lev_kept"], NL * f + l)
                        for h in range(HG):
                            last = nc.tensor.matmul(F[0][0:NS, NS * h:NS * (h + 1)], lhs[:, h, :], rhs[:, h, :],
                                                    start=True, stop=True)
                        last.then_inc(S["lev_mm"], 1)
                if k == 57:
                    pe.wait_ge(S["kd_ready"], f + 1)
                    for h in range(HG):
                        last = nc.tensor.transpose(F[2][0:NS, P * h:P * (h + 1)], s_lev[0][:, NS * h:NS * (h + 1)], ident[:, :])
                    last.then_inc(S["kd_turned"], 1)
                if k == 59:
                    pe.wait_ge(S["lev_kept"], NL * f + 3)
                    for h in range(HG):
                        cols = slice(P * h, P * (h + 1))
                        nc.tensor.matmul(F[3][0:NS, cols], a_t[0:NS, h, 0:NS], s_nat[:, cols], start=True, stop=True)
                for b in range(DEC_B):
                    if k == 60 + b:
                        pe.wait_ge(S["qe_ready"], f + 1)
                        pe.wait_ge(S[f"st_in{b % 2}"], 16 * (b // 2 + 1))
                        pe.wait_ge(S["kdm_ready"], b + 1)
                        if b >= 2:
                            pe.wait_ge(S["st_new"], b - 1)
                        for h in range(HG):
                            col = NS * h + DEC_T * b
                            nc.tensor.matmul(F[4][:, col:col + DEC_T], s_st[b % 2][:, P * h:P * (h + 1)],
                                             s_qe[:, col:col + DEC_T], start=True, stop=True)
                        for h in range(HG):
                            cols = slice(P * h, P * (h + 1))
                            last = nc.tensor.matmul(F[b % 2][:, cols], s_kdm[b % 2][:, cols], s_nat[:, cols],
                                                    start=True, stop=True)
                        last.then_inc(S["st_mm"], 1)
                if k == 70:
                    pe.wait_ge(S["ot_kept"], 1)
                    for h in range(HG):
                        last = nc.tensor.transpose(F[5][0:NS, P * h:P * (h + 1)], s_ot[:, NS * h:NS * (h + 1)], ident[:, :])
                    last.then_inc(S["ot_turned"], 1)

            def body(p):
                v, u, f = parts(p)
                for k in range(PICKS):
                    if v is not None and k < steps_of(v):
                        pe.wait_ge(S["diag_ready"], PICKS * v + k + 1)
                        pe.wait_ge(v_row[k % V_RING], 16 * (PICKS // V_RING) * v + 16 * (k // V_RING + 1))
                        m = NS if is_sample(v) else P
                        for j in range(2):
                            last = nc.tensor.matmul(Y[j][0:m, :], diag[:, k % 2, 0:m], v_rows[:, k % V_RING, 512 * j:512 * (j + 1)],
                                                    start=(k == 0), stop=(k == steps_of(v) - 1))
                        last.then_inc(S["vsum"], 1)
                    if f is not None:
                        front(k, f)
                if v is not None:
                    pe.wait_ge(S["y_taken"], v + 1)

            pe.sem_inc(S["vsum"], summed(0))
            periods(pe, None, body)

        @block.vector
        def _(dve):
            own = Own(dve, S["own_dve"], DVE_PER)
            mark, settle = own.mark, own.settle
            V = nc.vector
            mark(V.memset(eps, EPS))
            mark(V.memset(one, 1.0))
            mark(V.memset(table[BUCKETS:BUCKETS + 1, :], NEG))
            mark(V.memset(state[:, :, :], 0.0))
            mark(V.memset(a_t[:, :, :], 0.0))
            V.memset(mix_scale[:, 0:4], 1.0).then_inc(S["set_up"], 1)
            dve.wait_ge(S["consts_in"], 16 * 12)
            mark(V.tensor_copy(level_masks[:, :, :], hn_u[:, :].rearrange("p (l t) -> p l t", l=NL)))
            lb_e = lb_in.rearrange("p (r h) -> p r h", r=2)
            mark(V.tensor_tensor(lb, lb_e[:, 0, :], lb_e[:, 1, :], ALU.max))
            settle()
            for r in range(2):
                last = V.tensor_tensor(lb_e[:, r, :], lb_e[:, r, :], lb, ALU.subtract)
            last.then_inc(S["lb_shifted"], 1)
            dve.wait_ge(S["lb_exp"], 1)
            mark(V.tensor_tensor(oml, lb_e[:, 0, :], lb_e[:, 1, :], ALU.add))
            settle()
            mark(V.reciprocal(oml, oml))
            settle()
            mark(V.tensor_tensor(lb, lb_e[:, 0, :], oml, ALU.mult))
            settle()
            mark(V.tensor_scalar(oml, lb, -1.0, 1.0, ALU.mult, ALU.add))
            settle()

            def keep(i):
                n = P if i < TILES else NS
                for j in range(2):
                    if j == 0:
                        dve.wait_ge(S["a_turned"], i + 1)
                    V.tensor_tensor(xn_t[:, 4 * j:4 * j + 4, P * i:P * i + n],
                                    ps[:, j, :].rearrange("p (c t) -> p c t", c=4)[:, :, 0:n],
                                    w_mix[:, 4 * j:4 * j + 4].unsqueeze(2).to_broadcast([P, 4, n]), ALU.mult)\
                        .then_inc(S["a_kept"], 1)
            for i in range(TILES + 1):
                n = P if i < TILES else NS
                dve.wait_ge(S["a_root"], i + 1)
                mark(V.reciprocal(rstd[0:n, :], rstd[0:n, :]))
                settle()
                V.tensor_scalar(x_a[i % 2][0:n, :], x_a[i % 2][0:n, :], rstd[0:n, :], None, ALU.mult)\
                    .then_inc(S["a_scaled"], 1)
                keep(i)
            dve.wait_ge(S["bias_mm"], 1)
            V.tensor_copy(bias_v.rearrange("p h k -> p k h"),
                          ps[:, 2:6, :].rearrange("p b (k h) -> p (b k) h", h=HEADS)).then_inc(S["bias_kept"], 1)
            def keep_high(it, first):
                for j in range(2):
                    dve.wait_ge(S["wp_done"], 2 * it + j + 1)
                    if not first:
                        dve.wait_ge(S[f"proj_out{j}"], 16 * it)
                    V.tensor_copy(staged[j][:, 512:1024], ps[:, 3 * j + 1, :])
                    V.tensor_copy(staged[j][:, 1024:TOK], ps[:, 3 * j + 2, 0:NS]).then_inc(S["kept_hi"], 1)
            keep_high(0, True)
            with dve.Fori(1, CHUNKS // 2) as it:
                keep_high(it, False)

            def mask_scores(f, kv, lo):
                dve.wait_ge(S["scores"], 2 * f + kv + 1)
                if kv:
                    dve.wait_ge(S["p_turned"], 2 * f + kv)
                for j in range(2):
                    h = GRP * kv + 2 * j
                    bank = F[(3 if kv == 0 else 0) + j].rearrange("p (h s) -> p h s", h=2)
                    mark(V.scalar_tensor_tensor(probs[:, 2 * j:2 * j + 2, lo:2 * P], bank[:, :, lo:2 * P], SCALE,
                                                bias_v[:, h:h + 2, lo:2 * P], ALU.mult, ALU.add))
                settle()
                heads = slice(GRP * kv, GRP * (kv + 1))
                mark(V.tensor_reduce(rmax, probs[:, :, lo:2 * P], AX.X, ALU.max))
                settle()
                mark(V.tensor_tensor(rmax, rmax, sinks[:, heads], ALU.max))
                settle()
                V.tensor_tensor(esink[:, heads], sinks[:, heads], rmax, ALU.subtract)
                V.tensor_scalar(nmax[:, heads], rmax, -1.0, None, ALU.mult).then_inc(S["s_masked"], 1)

            def level_exponents(l, m, cum_v, out):
                b = cum_v.rearrange("p (x two m) -> p x two m", two=2, m=m)
                o = out.rearrange("p (x two m) -> p x two m", two=2, m=m)
                ref = b[:, :, 0, m - 1:m].to_broadcast([P, b.shape[1], m])
                V.tensor_tensor(o[:, :, 1, :], b[:, :, 1, :], ref, ALU.subtract)
                V.tensor_tensor(o[:, :, 0, :], ref, b[:, :, 0, :], ALU.subtract).then_inc(S["lev_d"], 1)

            def level_factors(l, m, e, q, kk):
                o = e.rearrange("p (x two m) -> p x two m", two=2, m=m)
                q = q.rearrange("p (x two m) -> p x two m", two=2, m=m)
                kk = kk.rearrange("p (x two m) -> p x two m", two=2, m=m)
                V.tensor_tensor(o[:, :, 1, :], o[:, :, 1, :], q[:, :, 1, :], ALU.mult)
                V.tensor_tensor(o[:, :, 0, :], o[:, :, 0, :], kk[:, :, 0, :], ALU.mult).then_inc(S["lev_q"], 1)

            flat = "p c t -> p (c t)"

            def front(k, f):
                first = isinstance(f, int) and f == 0
                n = NS if is_sample(f) else P
                lo = P if first else 0
                if is_sample(f):
                    sample_front(k, f)
                else:
                    q_s, k_s = slots(C_QH, 4).rearrange(flat), slots(C_F, 4).rearrange(flat)
                    for kv in range(KV):
                        if k == 10 + 7 * kv:
                            mask_scores(f, kv, lo)
                    if k == 20:
                        dve.wait_ge(S["kept_ig"], f + 1)
                        for h in range(HG):
                            last = V.tensor_scalar(slots(C_F, 4)[:, h, :], slots(C_F, 4)[:, h, :], oml[:, h:h + 1],
                                                   lb[:, h:h + 1], ALU.mult, ALU.add)
                        last.then_inc(S["hg_f"], 1)
                    if k == 27:
                        dve.wait_ge(S["pv"], 2 * f + 2)
                        dve.wait_ge(S["p_ready"], 2 * f + 2)
                        mark(V.tensor_tensor(den, den, esink, ALU.add))
                        settle()
                        mark(V.reciprocal(den, den))
                        settle()
                        V.tensor_tensor(mix[:, 0:512].rearrange("p (h d) -> p h d", h=HEADS),
                                        F[5].rearrange("p (h d) -> p h d", h=HEADS),
                                        den.unsqueeze(2).to_broadcast([P, HEADS, DH]), ALU.mult).then_inc(S["mix_attn"], 1)
                    if k == 30:
                        dve.wait_ge(S["hg_ln"], f + 1)
                        V.tensor_scalar(k_s, k_s, -1.0, 1.0, ALU.mult, ALU.add)
                        for h in range(HG):
                            last = V.tensor_tensor_scan(cum[:, P * h:P * (h + 1)], one.to_broadcast([P, P]),
                                                        cum[:, P * h:P * (h + 1)], 0.0, ALU.mult, ALU.add)
                        last.then_inc(S["hg_k"], 1)
                        dve.wait_ge(S["hg_k"], f + 1)
                    for l in range(NL):
                        if k == 32 + 3 * l and l < NL - 1:
                            if l >= 2:
                                dve.wait_ge(S["lev_mm"], NL * f + l - 1)
                            level_exponents(l, LEVELS[l], cum, lev[l % 2])
                        if k == 34 + 3 * l and l < NL - 1:
                            dve.wait_ge(S["lev_e"], (NL - 1) * f + l + 1)
                            level_factors(l, LEVELS[l], lev[l % 2], q_s, k_s)
                        if k == 36 + 3 * l:
                            hold(dve, S["lev_mm"], NL * f + l + 1, S["held_dve"])
                            if l:
                                hold(dve, S["lev_kept"], NL * f + l, S["held_dve"])
                            V.copy_predicated(a_t[:, :, :], level_masks[:, l:l + 1, :].to_broadcast([P, HG, P]),
                                              F[l % 2].rearrange("p (c t) -> p c t", c=4)).then_inc(S["lev_kept"], 1)
                    if k == 40:
                        dve.wait_ge(S["qe_exp"], f + 1)
                        mark(V.tensor_copy(decay, slots(C_Q, 4)[:, :, P - 1]))
                        settle()
                        V.tensor_tensor(slots(C_Q, 4), slots(C_Q, 4), slots(C_QH, 4), ALU.mult).then_inc(S["qe_ready"], 1)
                    if k == 54:
                        dve.wait_ge(S["lev_mm"], NL * f + 6)
                        c3 = cum.rearrange("p (c t) -> p c t", c=4)
                        V.tensor_tensor(lev[1].rearrange("p (c t) -> p c t", c=4),
                                        c3[:, :, P - 1:P].to_broadcast([P, HG, P]), c3, ALU.subtract).then_inc(S["kd_d"], 1)
                    if k == 57:
                        dve.wait_ge(S["kd_exp"], f + 1)
                        V.tensor_tensor(lev[1], lev[1], k_s, ALU.mult).then_inc(S["kd_ready"], 1)
                    if k == 63:
                        dve.wait_ge(S["hg_out"], f + 1)
                        settle()
                        for h in range(HG):
                            last = V.scalar_tensor_tensor(state[:, h, :], state[:, h, :], decay[:, h:h + 1],
                                                          F[4][:, P * h:P * (h + 1)], ALU.mult, ALU.add)
                        last.then_inc(S["s_new"], 1)
                if k == 74:
                    dve.wait_ge(S["rms_root"], f + 1)
                    mark(V.reciprocal(ssq4[0:n, :], ssq4[0:n, :]))
                    settle()
                    m3 = mix[0:n, 512:1024].rearrange("p (h d) -> p h d", h=HG)
                    mark(V.tensor_tensor(m3, m3, ssq4[0:n, :].unsqueeze(2).to_broadcast([n, HG, P]), ALU.mult))
                    settle()
                    g_s = s_nat[:, 512:1024].rearrange("p (h d) -> p h d", h=HG) if is_sample(f) else slots(C_G, 4)
                    V.tensor_tensor(m3, m3, g_s, ALU.mult).then_inc(S["mix_ready"], 1)
                if k == 76:
                    dve.wait_ge(S["mix_turned"], f + 1)
                    for j in range(2):
                        last = V.tensor_tensor(mix_t[:, 4 * j:4 * j + 4, 0:n],
                                               F[j][:, 0:4 * n].rearrange("p (c t) -> p c t", c=4),
                                               mix_scale[:, 4 * j:4 * j + 4].unsqueeze(2).to_broadcast([P, 4, n]), ALU.mult)
                    last.then_inc(S["mix_kept"], 1)
                if k == 80:
                    dve.wait_ge(S["h_mm"], 2 * f + 2)
                    dve.wait_ge(S["x_in"], 16 * f + 16)
                    for j in range(2):
                        cols = slice(512 * j, 512 * (j + 1))
                        last = V.tensor_tensor(hx[0:n, cols], F[2 + j][0:n, :], hx[0:n, cols], ALU.add)
                    last.then_inc(S["h_ready"], 1)
                if k == 82:
                    dve.wait_ge(S["ssq_root"], f + 1)
                    dve.wait_ge(S["wffn_in"], 16 * f + 16)
                    mark(V.reciprocal(rstd[0:n, :], rstd[0:n, :]))
                    settle()
                    V.scalar_tensor_tensor(hn[0:n, :], hx[0:n, :], rstd[0:n, :], r3[0:n, :], ALU.mult, ALU.mult)\
                        .then_inc(S["hn_ready"], 1)
                    dve.wait_ge(S["hn_ready"], f + 1)
                for g in range(4):
                    if k == 90 + 3 * g:
                        hold(dve, S["sc_kept"], 4 * f + g + 1, S["held_dve"])
                        top16([sc[0:n, c, :] for c in range(4 * g, 4 * g + 4)], [sv[0:n, c, :] for c in range(4 * g, 4 * g + 4)],
                              [si[0:n, c, :] for c in range(4 * g, 4 * g + 4)])
                if k == 101:
                    settle()
                    sv4 = sv[0:n].rearrange("p (h two) k -> p h two k", two=2)
                    for j in range(2):
                        hs = slice(4 * j, 4 * j + 4)
                        mark(V.tensor_tensor(cand[0:n, hs, :].rearrange("p h (x y) -> p h x y", x=TOPK),
                                             sv4[:, hs, 0, :].unsqueeze(3).to_broadcast([n, 4, TOPK, TOPK]),
                                             sv4[:, hs, 1, :].unsqueeze(2).to_broadcast([n, 4, TOPK, TOPK]), ALU.add))
                    mark(V.tensor_copy(si_f[0:n], si[0:n]))
                    settle()
                for j in range(4):
                    if k == 103 + 2 * j:
                        top16([cand[0:n, h, :] for h in (2 * j, 2 * j + 1)], [fv[0:n, h, :] for h in (2 * j, 2 * j + 1)],
                              [fi[0:n, h, :] for h in (2 * j, 2 * j + 1)])
                if k == 111:
                    settle()
                    fi_x = r3[0:n, 896:1024].bitcast(U32)
                    mark(V.tensor_scalar(pos[0][0:n].bitcast(U32), fi_x, 4, None, ALU.logical_shift_right))
                    mark(V.tensor_scalar(pos[1][0:n].bitcast(U32), fi_x, 15, None, ALU.bitwise_and))
                    V.tensor_tensor(gate_f[0:n, :].rearrange("p (h k) -> p h k", h=PH), fv[0:n],
                                    fv[0:n, :, 0:1].to_broadcast([n, PH, TOPK]), ALU.subtract)\
                        .then_inc(S["gate_d"], 1)
                    settle()
                    for j in range(2):
                        mark(V.tensor_copy(pos[2 + j][0:n], pos[j][0:n].bitcast(U32)))
                    settle()
                for j in range(2):
                    if k == 113 + 2 * j:
                        oh = onehot[0:n]
                        settle()
                        mark(V.tensor_tensor(oh, pos[2 + j][0:n].unsqueeze(2).to_broadcast([n, PICKS, TOPK]),
                                             iota16[0:n].unsqueeze(1).to_broadcast([n, PICKS, TOPK]), ALU.is_equal))
                        settle()
                        si4 = si_f[0:n].rearrange("p (h two) k -> p h two k", two=2)[:, :, j, :]
                        oh4 = oh.rearrange("p (h k) x -> p h k x", h=PH)
                        mark(V.tensor_tensor(oh4, oh4, si4.unsqueeze(2).to_broadcast([n, PH, TOPK, TOPK]), ALU.mult))
                        settle()
                        mark(V.tensor_reduce(pos[j][0:n], oh, AX.X, ALU.add))
                if k == 118:
                    settle()
                    if not first:
                        dve.wait_ge(S["idx_taken"], f)
                    dve.wait_ge(S["gate_exp"], f + 1)
                    g3 = gate_f[0:n].rearrange("p (h k) -> p h k", h=PH)
                    mark(V.tensor_reduce(gsum[0:n], fv[0:n], AX.X, ALU.add))
                    settle()
                    mark(V.reciprocal(gsum[0:n], gsum[0:n]))
                    settle()
                    if not is_sample(f):
                        mark(V.scalar_tensor_tensor(idx_f[:, :], pos[0], float(P), pos[1], ALU.mult, ALU.add))
                        V.tensor_tensor(g3, fv[:], gsum.unsqueeze(2).to_broadcast([P, PH, TOPK]), ALU.mult)\
                            .then_inc(S["topk_done"], 1)
                        mark(V.memset(rmax[:, 0:1], 0.0))
                        settle()
                    else:
                        for g in range(SGRP):
                            cols, part = slice(NS * g, NS * (g + 1)), slice(NS * g, NS * (g + 1))
                            V.scalar_tensor_tensor(idx_f[part, 0:NS], pos[0][0:NS, cols], float(P), pos[1][0:NS, cols],
                                                   ALU.mult, ALU.add)
                            hs = slice(2 * g, 2 * g + 2)
                            last = V.tensor_tensor(gate_f[part, 0:NS].rearrange("p (h k) -> p h k", h=2), fv[0:NS, hs, :],
                                                   gsum[0:NS, hs].unsqueeze(2).to_broadcast([NS, 2, TOPK]), ALU.mult)
                        last.then_inc(S["topk_done"], 1)
                        dve.wait_ge(S["topk_done"], f + 1)

            def top16(values, best, places):
                for x, b in zip(values, best):
                    mark(V.max(b[:, 0:8], x))
                own.settle_held(S["held_dve"])
                for x, b, i in zip(values, best, places):
                    mark(V.max_index(i[:, 0:8], b[:, 0:8], x))
                    mark(V.match_replace(x, b[:, 0:8], x, LOWEST))
                own.settle_held(S["held_dve"])
                for x, b in zip(values, best):
                    mark(V.max(b[:, 8:16], x))
                own.settle_held(S["held_dve"])
                for x, b, i in zip(values, best, places):
                    mark(V.max_index(i[:, 8:16], b[:, 8:16], x))

            def sample_front(k, f):
                q_s, k_s = slots(C_QH, 4, spj).rearrange(flat), slots(C_F, 4, spj).rearrange(flat)
                if k == 2:
                    for g in range(KV):
                        V.tensor_tensor(s_tab[:, P * g:P * (g + 1)].rearrange("p (h b t) -> p h b t", h=GRP, b=DEC_B),
                                        tab_rep[:, GRP * g:GRP * (g + 1)].unsqueeze(2).unsqueeze(3).to_broadcast([P, GRP, DEC_B, DEC_T]),
                                        tsel.unsqueeze(1).unsqueeze(1).to_broadcast([P, GRP, DEC_B, DEC_T]), ALU.mult)\
                            .then_inc(S["s_tab_ready"], 1)
                for kv in range(KV):
                    if k == 12 + 14 * kv:
                        dve.wait_ge(S["scores"], 2 * f + kv + 1)
                        dve.wait_ge(S["s_bias_kept"], 1)
                        dve.wait_ge(S["caches_in"], 64)
                        if kv:
                            dve.wait_ge(S["p_turned"], 2 * f + 1)
                        for b, (x, y) in enumerate(((0, 512), (512, 1024), (1024, 1024 + NS))):
                            mark(V.scalar_tensor_tensor(s_probs[:, x:y], F[b][:, 0:y - x], SCALE, s_mask[:, x:y], ALU.mult, ALU.add))
                        settle()
                        old = s_probs[:, 0:D].rearrange("p (b j) -> p b j", b=DEC_B)
                        new = s_probs[:, D:D + NS].rearrange("p (b j) -> p b j", b=DEC_B)
                        mark(V.tensor_tensor(old, old, s_bias[:, kv:kv + 1, 0:P].to_broadcast([P, DEC_B, P]), ALU.add))
                        mark(V.tensor_tensor(new, new, s_bias[:, kv:kv + 1, P:P + DEC_T].to_broadcast([P, DEC_B, DEC_T]), ALU.add))
                        settle()
                        mark(V.tensor_reduce(rmax[:, 0:1], s_probs, AX.X, ALU.max))
                        settle()
                        mark(V.tensor_tensor(rmax[:, 0:1], rmax[:, 0:1], sinks_s[:, kv:kv + 1], ALU.max))
                        settle()
                        V.tensor_tensor(esink[:, kv:kv + 1], sinks_s[:, kv:kv + 1], rmax[:, 0:1], ALU.subtract)
                        V.tensor_scalar(nmax[:, kv:kv + 1], rmax[:, 0:1], -1.0, None, ALU.mult).then_inc(S["s_masked"], 1)
                    if k == 22 + 14 * kv:
                        dve.wait_ge(S["pv"], 2 * f + kv + 1)
                        mark(V.tensor_tensor(den[:, kv:kv + 1], den[:, kv:kv + 1], esink[:, kv:kv + 1], ALU.add))
                        settle()
                        mark(V.reciprocal(den[:, kv:kv + 1], den[:, kv:kv + 1]))
                        settle()
                        for j in range(GRP):
                            part, h = slice(NS * j, NS * (j + 1)), GRP * kv + j
                            last = V.tensor_scalar(mix[0:NS, DH * h:DH * (h + 1)], F[2][part, 64:128], den[part, kv:kv + 1],
                                                   None, ALU.mult)
                        last.then_inc(S["mix_attn"], 1)
                if k == 43:
                    dve.wait_ge(S["kept_ig"], f + 1)
                    for h in range(HG):
                        last = V.tensor_scalar(slots(C_F, 4, spj)[:, h, :], slots(C_F, 4, spj)[:, h, :], oml[:, h:h + 1],
                                               lb[:, h:h + 1], ALU.mult, ALU.add)
                    last.then_inc(S["hg_f"], 1)
                    dve.wait_ge(S["hg_out"], f)
                    mark(V.memset(a_t[0:NS, :, 0:NS], 0.0))
                    mark(V.memset(s_reset, 1.0))
                    settle()
                    mark(V.memset(s_reset.rearrange("p (x t) -> p x t", t=DEC_T)[:, :, 0:1], 0.0))
                if k == 45:
                    dve.wait_ge(S["hg_ln"], f + 1)
                    settle()
                    V.tensor_scalar(k_s, k_s, -1.0, 1.0, ALU.mult, ALU.add)
                    V.tensor_tensor_scan(s_cum, s_reset, s_cum, 0.0, ALU.mult, ALU.add).then_inc(S["hg_k"], 1)
                    dve.wait_ge(S["hg_k"], f + 1)
                for l in range(3):
                    if k == 47 + 2 * l and l < 2:
                        level_exponents(l, LEVELS[5 + l], s_cum, s_lev[l])
                    if k == 49 + 2 * l and l < 2:
                        dve.wait_ge(S["lev_e"], (NL - 1) * f + l + 1)
                        level_factors(l, LEVELS[5 + l], s_lev[l], q_s, k_s)
                    if k == 51 + 2 * l:
                        dve.wait_ge(S["lev_mm"], NL * f + l + 1)
                        if l:
                            dve.wait_ge(S["lev_kept"], NL * f + l)
                        V.copy_predicated(a_t[0:NS, :, 0:NS], level_masks[0:NS, 5 + l:6 + l, 0:NS].to_broadcast([NS, HG, NS]),
                                          F[0][0:NS, 0:P].rearrange("p (c t) -> p c t", c=4)).then_inc(S["lev_kept"], 1)
                if k == 52:
                    dve.wait_ge(S["qe_exp"], f + 1)
                    mark(V.tensor_copy(s_dec, s_qe.rearrange("p (x t) -> p x t", t=DEC_T)[:, :, last_pos]))
                    settle()
                    V.tensor_tensor(s_qe, s_qe, q_s, ALU.mult).then_inc(S["qe_ready"], 1)
                    dve.wait_ge(S["lev_mm"], NL * f + 1)
                    c3 = s_cum.rearrange("p (x t) -> p x t", t=DEC_T)
                    V.tensor_tensor(s_lev[0].rearrange("p (x t) -> p x t", t=DEC_T),
                                    c3[:, :, last_pos:DEC_T].to_broadcast([P, HG * DEC_B, DEC_T]), c3, ALU.subtract)\
                        .then_inc(S["kd_d"], 1)
                if k == 56:
                    dve.wait_ge(S["kd_exp"], f + 1)
                    V.tensor_tensor(s_lev[0], s_lev[0], k_s, ALU.mult).then_inc(S["kd_ready"], 1)
                for b in range(DEC_B):
                    if k == 59 + b:
                        dve.wait_ge(S["kd_kept"], f + 1)
                        if b >= 2:
                            dve.wait_ge(S["st_mm"], b - 1)
                        V.tensor_scalar(s_kdm[b % 2], s_kdn, bsel[0:NS, b:b + 1], None, ALU.mult).then_inc(S["kdm_ready"], 1)
                    if k == 61 + b:
                        dve.wait_ge(S["st_mm"], b + 1)
                        settle()
                        for h in range(HG):
                            cols = slice(P * h, P * (h + 1))
                            last = V.scalar_tensor_tensor(s_st[b % 2][:, cols], s_st[b % 2][:, cols],
                                                          s_dec[:, DEC_B * h + b:DEC_B * h + b + 1], F[b % 2][:, cols],
                                                          ALU.mult, ALU.add)
                        last.then_inc(S["st_new"], 1)
                if k == 72:
                    dve.wait_ge(S["o_kept"], 1)
                    V.tensor_tensor(mix[0:NS, 512:1024], mix[0:NS, 512:1024], F[3][0:NS, :], ALU.add).then_inc(S["o_kept"], 1)

            def body(p):
                v, u, f = parts(p)
                for k in range(PICKS):
                    if u is not None and k < steps_of(u):
                        dve.wait_ge(u_row[k % U_RING], 16 * (PICKS // U_RING) * u + 16 * (k // U_RING + 1))
                        V.tensor_tensor_reduce(u_rows[:, k % U_RING, :], u_rows[:, k % U_RING, :], hn_u[:, :], 1.0, 0.0,
                                               ALU.mult, ALU.add, act_u[:, k:k + 1]).then_inc(S["dots"], 1)
                    if f is not None:
                        front(k, f)
                if u is not None:
                    dve.wait_ge(S["act_ready"], u + 1)
                    if v is not None:
                        dve.wait_ge(S["diag_ready"], PICKS * v + steps_of(v))
                    V.tensor_tensor(w_v[:, 0:steps_of(u)], act_u[:, 0:steps_of(u)], gate_u[:, 0:steps_of(u)], ALU.mult)\
                        .then_inc(S["wv_ready"], 1)
                    dve.wait_ge(S["wv_ready"], u + 1)
                if f is not None:
                    if is_sample(f):
                        mark(V.tensor_copy(gate_u[:, 0:NS], gate_f[:, 0:NS]))
                        for g in range(SGRP):
                            mark(V.tensor_copy(hn_u[NS * g:NS * (g + 1), :], hn[0:NS, :]))
                    else:
                        mark(V.tensor_copy(gate_u[:, :], gate_f[:, :]))
                        V.tensor_copy(hn_u[:, :], hn[:, :]).then_inc(S["hn_taken"], 1)
                        dve.wait_ge(S["hn_taken"], f + 1)
                    settle()
                if v is not None:
                    m = ntok(v)
                    dve.wait_ge(S["vsum"], summed(PICKS * v + steps_of(v)))
                    dve.wait_ge(S["h_back"], 16 * v + 16)
                    for j in range(2):
                        cols = slice(512 * j, 512 * (j + 1))
                        last = V.tensor_tensor(hx[0:m, cols], Y[j][0:m, :], hx[0:m, cols], ALU.add)
                    last.then_inc(S["y_taken"], 1)
                    dve.wait_ge(S["y_root"], v + 1)
                    dve.wait_ge(S["wfin_in"], 16 * v + 16)
                    mark(V.reciprocal(rstd_y[0:m, :], rstd_y[0:m, :]))
                    settle()
                    V.scalar_tensor_tensor(hx[0:m, :], hx[0:m, :], rstd_y[0:m, :], r3[0:m, :], ALU.mult, ALU.mult)\
                        .then_inc(S["y_ready"], 1)

            periods(dve, own, body)



def bucket(dist):
    exact = BUCKETS // 2
    n = np.maximum(dist, 0)
    nf = np.maximum(n, 1).astype(np.float32)
    step = np.log(nf / np.float32(exact)) / np.float32(np.log(WINDOW / exact)) * np.float32(BUCKETS - exact)
    return np.where(n < exact, n, np.minimum(exact + step.astype(np.int32), BUCKETS - 1))


def constants():
    dist = np.arange(3 * P - 1) - (P - 1)
    valid = (dist >= 0) & (dist <= WINDOW)
    bucket_of = np.zeros((BUCKETS + 1, 3 * P - 1), np.float32)
    bucket_of[np.where(valid, bucket(dist), BUCKETS), np.arange(3 * P - 1)] = 1.0
    s, t = np.arange(P)[:, None], np.arange(P)[None, :]
    masks = np.zeros((P, NL, P), np.float32)
    for l, m in enumerate(LEVELS):
        masks[:, l] = (s // (2 * m) == t // (2 * m)) & (s % (2 * m) < m) & (t % (2 * m) >= m)
    masks[:, NL - 1] = s == t
    d_s = (WINDOW + np.arange(DEC_T))[:, None] - np.arange(WINDOW + DEC_T)[None, :]
    ok = (d_s >= 0) & (d_s <= WINDOW)
    onehot = (bucket(d_s)[:, None, :] == np.arange(BUCKETS)[None, :, None]) & ok[:, None, :]
    same = np.arange(DEC_B)[:, None] == np.arange(DEC_B)[None, :]
    allowed = same[:, None, :, None] & ok[None, :, None, :]
    flat = np.concatenate([allowed[..., :WINDOW].reshape(NS, -1), allowed[..., WINDOW:].reshape(NS, -1)], axis=1)
    p = np.arange(P)
    return {
        "ident": np.eye(P, dtype=np.float32),
        "bucket_of": bucket_of,
        "level_masks": masks.reshape(P, NL * P),
        "iota16": np.tile(np.arange(TOPK, dtype=np.float32), (P, 1)),
        "tsel": (p[:, None] // BUCKETS == np.arange(DEC_T)[None]).astype(np.float32),
        "bsel": (p[:, None] // DEC_T == np.arange(DEC_B)[None]).astype(np.float32),
        "fold": (p[:, None] % NS == np.arange(NS)[None]).astype(np.float32),
        "s_onehot": onehot.reshape(DEC_T * BUCKETS, -1).astype(np.float32),
        "s_mask": np.tile(np.where(flat, 0.0, NEG).astype(np.float32), (GRP, 1)),
    }


def layout(i):
    w_in = i["w_in"][0]
    aw = HEADS * DH
    q = w_in[:, :aw].reshape(D, KV, GRP, DH).transpose(0, 2, 1, 3).reshape(D, aw)
    w_in = np.concatenate([q, w_in[:, aw:]], axis=1)
    sinks = i["attn_sinks"][0]
    return {
        "x_prompt": i["x_prompt"][0],
        "x_sample": i["x_sample"].reshape(NS, D),
        "w_in": w_in.reshape(DC, P, CHUNKS, P).transpose(2, 1, 0, 3),
        "w_o": i["w_o"][0],
        "w_q": i["peer_w_q"][0],
        "keys_t": i["peer_sub_keys"][0].reshape(2 * PH, P, P).transpose(2, 0, 1),
        "peer_u": i["peer_u"][0],
        "peer_v": i["peer_v"][0],
        "norm_mix_t": i["norm_mix_w"][0].reshape(DC, P).T,
        "hg_norm_t": i["hg_norm_w"][0].reshape(HG, P).T,
        "hg_lb_t": i["hg_lb"].reshape(2 * HG, P).T,
        "norm_ffn": np.tile(i["norm_ffn_w"], (P, 1)),
        "norm_final": np.tile(i["norm_final_w"], (P, 1)),
        "sinks": np.tile(sinks, (P, 1)),
        "sinks_s": np.repeat(sinks.reshape(KV, GRP).T, NS, axis=0),
        "table": i["rel_bias_table"],
        "table_rep": np.tile(i["rel_bias_table"], (DEC_T, 1)),
        "cache_k": i["cache_k_win"][0].reshape(DEC_B, WINDOW, P),
        "cache_v": i["cache_v_win"][0].reshape(DEC_B, WINDOW, P),
        "cache_k_t": i["cache_k_win"][0].reshape(DEC_B, WINDOW, P).transpose(0, 2, 1),
        "state_in": i["state_hgrn"][0].transpose(0, 2, 1, 3),
    }


OUTS = {"y_prompt": (SEQ, D), "y_sample": (NS, D), "k_win_prompt": (WINDOW, P), "v_win_prompt": (WINDOW, P),
        "state_prompt": (P, HG, P), "k_win_sample": (DEC_B, WINDOW, P), "v_win_sample": (DEC_B, WINDOW, P),
        "state_out": (DEC_B, P, HG * P)}


def kernel(**inputs):
    import concourse.bacc as _bacc
    from concourse.bass_utils import run_bass_kernel_spmd as _run

    nc = _bacc.Bacc("TRN2", target_bir_lowering=False, num_devices=1)
    given = {k: np.asarray(v) for k, v in inputs.items()}
    arrays, aps = {}, {}
    for name, array in (layout(given) | constants()).items():
        array = np.ascontiguousarray(array)
        arrays[f"in_{name}"] = array
        aps[name] = nc.dram_tensor(f"in_{name}", array.shape, mybir.dt.from_np(array.dtype), kind="ExternalInput").ap()
    for name, shape in OUTS.items():
        aps[name] = nc.dram_tensor(f"out_{name}", shape, F32, kind="ExternalOutput").ap()
    build(nc, aps)
    r = _run(nc, [arrays], core_ids=[0]).results[0]
    o = {name: r[f"out_{name}"] for name in OUTS}
    win = (1, -1, WINDOW, KV, DH)
    return (o["y_prompt"].reshape(1, SEQ, D), o["y_sample"].reshape(DEC_B, DEC_T, D),
            o["k_win_prompt"].reshape(win), o["v_win_prompt"].reshape(win),
            np.ascontiguousarray(o["state_prompt"].transpose(1, 0, 2)).reshape(1, 1, HG, P, P),
            o["k_win_sample"].reshape(win), o["v_win_sample"].reshape(win),
            np.ascontiguousarray(o["state_out"].reshape(DEC_B, P, HG, P).transpose(0, 2, 1, 3)).reshape(1, DEC_B, HG, P, P))
```

```python
from contextlib import ExitStack

import numpy as np
import concourse.bass as bass
from concourse import mybir

F32 = mybir.dt.float32
I32 = mybir.dt.int32
U32 = mybir.dt.uint32
U8 = mybir.dt.uint8
ALU = mybir.AluOpType
ACT = mybir.ActivationFunctionType
AX = mybir.AxisListType

P = 128
D = 1024
DC = D // P
SEQ, DEC_B, DEC_T = 1024, 8, 4
NS = DEC_B * DEC_T
TILES = SEQ // P
TOK = SEQ + NS
HEADS, KV, DH = 8, 2, 64
GRP = HEADS // KV
SCALE = DH ** -0.5
HG = 4
BUCKETS, WINDOW = 32, 128
NEG = -1.0e30
CHUNKS = 22
C_Q, C_K, C_V, C_QH, C_F, C_I, C_G = 0, 4, 5, 6, 10, 14, 18
PH, TOPK = 8, 16
PICKS = PH * TOPK
LEVELS = [64, 32, 16, 8, 4, 2, 1]
NL = len(LEVELS) + 1
LOWEST = -3.0e38
EPS = 1e-6
U_RING, V_RING = 8, 4
V_LAG = 3
SGRP = P // NS
S_OFF = (C_G + 4 - 1) * NS
SPLIT = SEQ // 2
BLOCK_EVERY = 5
SKEW = 3 * P
ORDER = [0, 1, 2, 3, TILES, 4, 5, 6, 7]
FIRST = 5
OUT_1, OUT_2 = 32 * (CHUNKS // 2), 48 * (CHUNKS // 2)
LOOP = (1, TILES - 2)
SKIP = 10
HEAD = 104
HEAD_AT, TAIL_AT = 121, 12
DVE_PER, ACT_PER = 153, 14


def steps_of(tile):
    return PICKS // SGRP if isinstance(tile, int) and tile == TILES else PICKS


def hold(eng, semaphore, value, held):
    eng.wait_ge(semaphore, value)
    if not isinstance(value, int):
        eng.sem_inc(held, 1)


def summed(n):
    return n + 2


class Own:

    def __init__(self, eng, semaphore, per_turn):
        self.eng, self.semaphore, self.per_turn = eng, semaphore, per_turn
        self.count, self.turn, self.at_start = 0, None, 0

    def mark(self, instruction):
        self.count += 1
        instruction.then_inc(self.semaphore, 1)

    def settle(self):
        value = self.count
        if self.turn is not None:
            value = self.turn * self.per_turn + (self.count - LOOP[0] * self.per_turn)
        self.eng.wait_ge(self.semaphore, value)

    def settle_held(self, held):
        self.settle()
        if self.turn is not None:
            self.eng.sem_inc(held, 1)

    def begin(self, turn):
        self.turn, self.at_start = turn, self.count

    def end(self, first, last):
        assert self.count - self.at_start == self.per_turn, (self.semaphore, self.count - self.at_start)
        self.count = self.at_start + (last - first) * self.per_turn
        self.turn = None


def build(nc, a):
    proj = nc.dram_tensor("proj", (CHUNKS, P, TOK), F32, kind="Internal").ap()
    skewed = nc.dram_tensor("skewed", (HEADS * P * SKEW,), F32, kind="Internal").ap()
    h_dram = nc.dram_tensor("h_dram", (TOK, D), F32, kind="Internal").ap()

    ctx = ExitStack()
    with ctx:
        def sb(name, shape, dt=F32):
            return ctx.enter_context(nc.sbuf_tensor(name, shape, dt))

        def sem(name):
            return ctx.enter_context(nc.semaphore(name))

        w_o = sb("w_o", [P, DC, D])
        w_sc = sb("w_sc", [P, 2 * PH, D])
        keys = sb("keys", [P, 2 * PH, P])
        rows = sb("rows", [P, (U_RING + V_RING) * D])
        hn_u = sb("hn_u", [P, D])
        hn = sb("hn", [P, D])
        hx = sb("hx", [P, D])
        bias = sb("bias", [P, HEADS * 2 * P])
        r1 = sb("r1", [P, (CHUNKS - 1) * P])
        r2 = sb("r2", [P, 2 * D])
        r3 = sb("r3", [P, D])
        state = sb("state", [P, HG, P])
        a_t = sb("a_t", [P, HG, P])
        diag = sb("diag", [P, 2, P])
        ident = sb("ident", [P, P])
        level_masks = sb("level_masks", [P, NL, P], U8)
        k_t = sb("k_t", [P, 2, P])
        v_n = sb("v_n", [P, 2, P])
        gate_f, gate_u, act_u, w_v = (sb(n, [P, PICKS]) for n in ("gate_f", "gate_u", "act_u", "w_v"))
        idx_f, idx_u, idx_v = (sb(n, [P, PICKS], I32) for n in ("idx_f", "idx_u", "idx_v"))
        small = sb("small", [P, 192])
        ps = ctx.enter_context(nc.psum_tensor("ps", [P, 8, 512], F32))
        Y = [ps[:, 0, :], ps[:, 1, :]]
        F = [ps[:, 2 + n, :] for n in range(6)]

        taken = [0]

        def vec(n):
            taken[0] += n
            return small[:, taken[0] - n:taken[0]]

        eps, one = vec(1), vec(1)
        w_mix = vec(DC)
        mix_scale = vec(DC)
        lb_in, lb, oml = vec(2 * HG), vec(HG), vec(HG)
        sinks, sinks_s = vec(HEADS), vec(KV)
        rmax, nmax, den, esink = vec(GRP), vec(HEADS), vec(HEADS), vec(HEADS)
        decay, ssq4 = vec(HG), vec(HG)
        ssq, rstd = vec(1), vec(1)
        ssq_y, rstd_y = vec(1), vec(1)
        gsum, iota16 = vec(PH), vec(TOPK)
        tsel, tab_rep, bsel = vec(DEC_T), vec(HEADS), vec(DEC_B)
        fold = vec(NS)
        assert taken[0] <= 192

        names = """consts_in w_o_in w_q_in0 w_q_in1 w_q_in2 w_q_in3 x_a0 x_a1 a_root a_scaled a_turned a_kept w_a0 w_a1
            keys_in m_mm m_kept bias_mm bias_kept bias_out bias_in wp_done kept proj_out0 proj_out1 table_in
            x_in proj_in wffn_in kv_shifted turned kept_ig v_kept
            scores s_masked p_ready p_turned p_kept pv mix_attn
            hg_f hg_ln hg_k lev_d lev_e lev_q lev_mm lev_kept
            qe_exp qe_ready kd_d kd_exp kd_ready kd_turned kd_kept hg_out s_new rms_root mix_ready
            mix_turned mix_kept h_mm h_ready h_stored ssq_root hn_ready hn_turned hn_kept hn_taken
            sc_mm sc_kept gate_d gate_exp topk_done idx_taken
            h_back wfin_in y_taken y_root y_ready y_out
            dots act_ready wv_ready diag_ready vsum
            own_dve own_act held_sp held_pool held_dve u_written v_written idx_moved
            caches_in out_kv k7_turned k7_kept set_up lb_shifted lb_exp s_turned s_tab_ready s_bias_mm s_bias_kept
            st_in0 st_in1 st_out0 st_out1 kdm_ready st_mm st_new ot_kept ot_turned o_kept""".split()
        S = {n: sem(n) for n in names}
        u_row = [sem(f"u_row{n}") for n in range(U_RING)]
        v_row = [sem(f"v_row{n}") for n in range(V_RING)]

        u_rows = rows[:, 0:U_RING * D].rearrange("p (r d) -> p r d", d=D)
        v_rows = rows[:, U_RING * D:].rearrange("p (r d) -> p r d", d=D)
        pj = r1[:, :].rearrange("p (c t) -> p c t", t=P)
        spj = r1[:, 0:S_OFF].rearrange("p (c t) -> p c t", t=NS)

        def slots(c, n, view=pj):
            c = c if c < C_K else c - 1
            return view[:, c:c + n, :]

        bias_v = bias[:, :].rearrange("p (h s) -> p h s", h=HEADS)
        probs = r2[:, 0:D].rearrange("p (h s) -> p h s", h=GRP)
        probs_t = r2[:, D:2 * D].rearrange("p (h b t) -> p h b t", h=GRP, b=2)
        lev = [r2[:, 0:512], r2[:, 512:1024]]
        kd_n, cum = r2[:, 1024:1536], r2[:, 1536:2048]
        mix = r3
        mix_t = r2[:, 0:D].rearrange("p (c t) -> p c t", c=DC)
        hn_t = r2[:, D:2 * D].rearrange("p (c t) -> p c t", c=DC)
        sc = r1[:, 0:2 * D].rearrange("p (c n) -> p c n", c=2 * PH)
        cand = r2[:, :].rearrange("p (h x) -> p h x", h=PH)
        sv = r3[:, 0:256].rearrange("p (c k) -> p c k", c=2 * PH)
        si = r3[:, 256:512].bitcast(U32).rearrange("p (c k) -> p c k", c=2 * PH)
        si_f = r3[:, 512:768].rearrange("p (c k) -> p c k", c=2 * PH)
        fv = r3[:, 768:896].rearrange("p (h k) -> p h k", h=PH)
        fi = r3[:, 896:1024].bitcast(U32).rearrange("p (h k) -> p h k", h=PH)
        onehot = r1[:, 0:2 * D].rearrange("p (x k) -> p x k", k=TOPK)
        pos = [r1[:, 2048 + n * PICKS:2048 + (n + 1) * PICKS] for n in range(4)]

        x_a = [r1[:, 0:D], r1[:, D:2 * D]]
        xn_t = rows[:, 0:DC * TOK].rearrange("p (c t) -> p c t", c=DC)
        wp = [rows[:, DC * TOK + n * D:DC * TOK + (n + 1) * D].rearrange("p (c n) -> p c n", c=DC) for n in range(2)]
        staged = [rows[:, DC * TOK + 2 * D + n * (SPLIT + NS):DC * TOK + 2 * D + (n + 1) * (SPLIT + NS)] for n in range(2)]
        table = hn[0:BUCKETS + 1, :].rearrange("p (h q) -> p h q", h=HEADS)
        bucket_of = hx[0:BUCKETS + 1, 0:SKEW]
        replicated = [r2[:, 0:4 * SKEW], bias[:, 0:4 * SKEW]]

        kc_t = bias[:, 0:D]
        vc = bias[:, D:2 * D].rearrange("p (b x) -> p b x", b=DEC_B)
        s_probs = r2[:, 0:D + NS]
        s_probs_t = [r2[:, D + NS + c * P:D + NS + (c + 1) * P] if c < 7 else
                     hn[:, 660 + (c - 7) * P:660 + (c - 6) * P] for c in range(9)]
        s_mask = r1[:, S_OFF:S_OFF + D + NS]
        s_bias = hn[:, 0:264].rearrange("p (g j) -> p g j", g=KV)
        s_oh = hn[:, 264:396]
        s_tab = hn[:, 396:652]
        s_nat = r1[0:NS, S_OFF:S_OFF + D]
        s_st = [bias[:, 0:512], bias[:, 512:1024]]
        s_cum, s_reset = bias[:, 1024:1152], bias[:, 1152:1280]
        s_lev = [bias[:, 1280:1408], bias[:, 1408:1536]]
        s_qe, s_dec, s_ot = bias[:, 1536:1664], bias[:, 1664:1696], bias[:, 1696:1824]
        s_kdn, s_kdm = r2[0:NS, 1024:1536], [r2[0:NS, 0:512], r2[0:NS, 512:1024]]
        last_pos = DEC_T - 1

        x_tiles = a["x_prompt"].rearrange("(i p) d -> i p d", p=P)
        proj_tiles = proj[:, :, 0:SEQ].rearrange("c p (i t) -> i p c t", t=P)
        proj_s = proj[:, :, SEQ:TOK].rearrange("c p t -> p c t")
        h_tiles = h_dram[0:SEQ, :].rearrange("(i p) d -> i p d", p=P)
        y_tiles = a["y_prompt"].rearrange("(i p) d -> i p d", p=P)

        def ntok(f):
            return NS if isinstance(f, int) and f == TILES else P

        def is_sample(f):
            return isinstance(f, int) and f == TILES

        def periods(eng, own, body):
            for q in range(-2, LOOP[0]):
                body(q)
            with eng.Fori(*LOOP) as p:
                if own:
                    own.begin(p)
                body(p)
                if own:
                    own.end(*LOOP)
            for q in range(LOOP[1], TILES + 2):
                body(q)

        def parts(p):
            if isinstance(p, int):
                return [t if 0 <= t <= TILES else None for t in range(p - 1, p + 3)]
            return p - 1, p, p + 1, p + 2

        block = ctx.enter_context(nc.Block())

        @block.sync
        def _(sp):
            def token_tile(n):
                i = ORDER[n]
                if n >= 2:
                    sp.wait_ge(S["a_turned"], n - 1)
                sp.dma_start(x_a[n % 2][0:ntok(i), :], x_tiles[i] if i < TILES else a["x_sample"])\
                  .then_inc(S[f"x_a{n % 2}"], 16)

            token_tile(0)
            for dst, src in ((ident[:, :], "ident"), (w_mix, "norm_mix_t"), (mix_scale[:, 4:8], "hg_norm_t"),
                             (lb_in, "hg_lb_t"), (sinks, "sinks"), (sinks_s, "sinks_s"), (iota16, "iota16"),
                             (tsel, "tsel"), (tab_rep, "table_rep"), (bsel, "bsel"), (fold, "fold")):
                sp.dma_start(dst, a[src]).then_inc(S["consts_in"], 16)
            sp.dma_start(hn_u[:, :], a["level_masks"]).then_inc(S["consts_in"], 16)
            token_tile(1)
            sp.dma_start(keys[:, :, :], a["keys_t"]).then_inc(S["keys_in"], 16)
            w_q_t = a["w_q_t"].rearrange("(c p) d -> p c d", p=P)
            for part in range(4):
                sp.dma_start(w_sc[:, 4 * part:4 * part + 4, :], w_q_t[:, 4 * part:4 * part + 4, :])\
                  .then_inc(S[f"w_q_in{part}"], 16)
                if part >= 1:
                    token_tile(part + 1)
                if part == 1:
                    sp.dma_start(table[0:BUCKETS, :, :], a["table"]).then_inc(S["table_in"], 16)
                    sp.dma_start(bucket_of, a["bucket_of"]).then_inc(S["table_in"], 16)
            for half in range(2):
                sp.wait_ge(S["bias_kept"], half + 1)
                sp.dma_start(skewed.rearrange("(h q s) -> q h s", h=HEADS, q=P)[:, 4 * half:4 * half + 4, :],
                             replicated[half].rearrange("p (h s) -> p h s", h=4)).then_inc(S["bias_out"], 16)
            for n in range(FIRST, TILES + 1):
                token_tile(n)
            sp.dma_start(w_o[:, :, :], a["w_o"].rearrange("(c p) n -> p c n", p=P)).then_inc(S["w_o_in"], 16)
            sp.wait_ge(S["bias_out"], 32)
            for h in range(HEADS):
                one_head = skewed[h * P * SKEW + P - 1:h * P * SKEW + P - 1 + P * (SKEW - 1)]
                sp.dma_start(bias_v[:, h, :], one_head.rearrange("(q s) -> q s", q=P)[:, 0:2 * P])\
                  .then_inc(S["bias_in"], 16)
            for j in range(2):
                sp.wait_ge(S[f"proj_out{j}"], OUT_1)
            sp.wait_ge(S["a_turned"], TILES + 1)

            def finish(w):
                if w is not None:
                    hold(sp, S["y_ready"], w + 1, S["held_sp"])
                    sp.dma_start(a["y_sample"] if is_sample(w) else y_tiles[w], hx[0:ntok(w), :]).then_inc(S["y_out"], 16)
                    hold(sp, S["y_out"], 16 * w + 16, S["held_sp"])

            def body(p):
                w, v, u, f = parts(p)
                if f is not None:
                    sample = is_sample(f)
                    first = isinstance(f, int) and f == 0
                    n = ntok(f)
                    if not first:
                        hold(sp, S["topk_done"], f, S["held_sp"])
                    if isinstance(p, int) and p == 0:
                        for j in range(2):
                            sp.wait_ge(S[f"proj_out{j}"], OUT_2)
                    if sample:
                        finish(w)
                        sp.dma_start(a["v_win_prompt"], v_n[:, 1, :]).then_inc(S["out_kv"], 16)
                        sp.dma_start(a["state_prompt"], state[:, :, :]).then_inc(S["out_kv"], 16)
                        sp.wait_ge(S["k7_kept"], 1)
                        sp.dma_start(a["k_win_prompt"], r3[:, 896:1024]).then_inc(S["out_kv"], 16)
                        for out_name, in_name in (("k_win_sample", "cache_k"), ("v_win_sample", "cache_v")):
                            sp.dma_start(a[out_name][:, 0:WINDOW - DEC_T, :], a[in_name][:, DEC_T:WINDOW, :])\
                              .then_inc(S["out_kv"], 16)
                        sp.dma_start(kc_t.rearrange("p (b j) -> p b j", b=DEC_B), a["cache_k_t"].rearrange("b p j -> p b j"))\
                          .then_inc(S["caches_in"], 16)
                        sp.dma_start(vc, a["cache_v"].rearrange("b j x -> j b x")).then_inc(S["caches_in"], 16)
                        sp.dma_start(s_mask, a["s_mask"]).then_inc(S["caches_in"], 16)
                        sp.wait_ge(S["hn_taken"], TILES)
                        sp.dma_start(s_oh, a["s_onehot"]).then_inc(S["caches_in"], 16)
                        sp.dma_start(k_t[:, 1, 0:NS], proj_s[:, C_K, :]).then_inc(S["proj_in"], 16)
                        sp.dma_start(spj[:, 0:C_K, :], proj_s[:, 0:C_K, :]).then_inc(S["proj_in"], 16)
                        sp.dma_start(spj[:, C_K:, :], proj_s[:, C_V:, :]).then_inc(S["proj_in"], 16)
                    else:
                        if not first:
                            sp.wait_ge(S["kv_shifted"], f + 1)
                        sp.dma_start(k_t[:, 1, :], proj_tiles[f, :, C_K, :]).then_inc(S["proj_in"], 16)
                        sp.dma_start(pj[:, 0:C_K, :], proj_tiles[f, :, 0:C_K, :]).then_inc(S["proj_in"], 16)
                        sp.dma_start(pj[:, C_K:, :], proj_tiles[f, :, C_V:, :]).then_inc(S["proj_in"], 16)
                        finish(w)
                    if first:
                        sp.wait_ge(S["bias_mm"], 2)
                    else:
                        hold(sp, S["hn_ready"], f, S["held_sp"])
                    sp.dma_start(hx[0:n, :], a["x_sample"] if sample else x_tiles[f]).then_inc(S["x_in"], 16)
                    if sample:
                        sp.wait_ge(S["v_kept"], f + 2)
                        for b in range(DEC_B):
                            sp.dma_start(a["k_win_sample"][b, WINDOW - DEC_T:WINDOW, :],
                                         r3[DEC_T * b:DEC_T * (b + 1), 896:1024]).then_inc(S["out_kv"], 16)
                            sp.dma_start(a["v_win_sample"][b, WINDOW - DEC_T:WINDOW, :],
                                         v_n[DEC_T * b:DEC_T * (b + 1), 1, :]).then_inc(S["out_kv"], 16)
                        sp.wait_ge(S["pv"], 2 * f + 2)
                        for b in range(DEC_B):
                            if b >= 2:
                                sp.wait_ge(S["st_new"], b - 1)
                                sp.dma_start(a["state_out"][b - 2], s_st[b % 2]).then_inc(S[f"st_out{b % 2}"], 16)
                                sp.wait_ge(S[f"st_out{b % 2}"], 16 * (b // 2))
                            sp.dma_start(s_st[b % 2].rearrange("p (h x) -> p h x", h=HG), a["state_in"][b])\
                              .then_inc(S[f"st_in{b % 2}"], 16)
                        for b in range(DEC_B - 2, DEC_B):
                            sp.wait_ge(S["st_new"], b + 1)
                            sp.dma_start(a["state_out"][b], s_st[b % 2]).then_inc(S[f"st_out{b % 2}"], 16)
                            sp.wait_ge(S[f"st_out{b % 2}"], 16 * (DEC_B // 2))
                    sp.wait_ge(S["mix_turned"], f + 1)
                    sp.dma_start(r3[:, :], a["norm_ffn"]).then_inc(S["wffn_in"], 16)
                    hold(sp, S["h_ready"], f + 1, S["held_sp"])
                    h_at = h_dram[SEQ:TOK, :] if sample else h_tiles[f]
                    sp.dma_start(h_at, hx[0:n, :]).then_inc(S["h_stored"], 16)
                    sp.wait_ge(S["h_stored"], 16 * f + 16)
                if f is None:
                    finish(w)
                if v is not None:
                    if f is not None:
                        sp.wait_ge(S["hn_ready"], f + 1)
                        hold(sp, S["topk_done"], f + 1, S["held_sp"])
                    nv = ntok(v)
                    sp.dma_start(hx[0:nv, :], h_dram[SEQ:TOK, :] if is_sample(v) else h_tiles[v])\
                      .then_inc(S["h_back"], 16)
                    sp.dma_start(r3[:, :], a["norm_final"]).then_inc(S["wfin_in"], 16)

            periods(sp, None, body)
            sp.wait_ge(S["y_out"], 16 * (TILES + 1))
            sp.wait_ge(S["out_kv"], 16 * (3 + 2 + 2 * DEC_B))

        @block.gpsimd
        def _(pool):
            def block_io(n, base, nxt, store):
                j = n[1]
                done = base + n[0] + j + 1
                hold(pool, S["wp_done"], done, S["held_pool"])
                if nxt is not None:
                    nc.gpsimd.dma_start(wp[j], a["w_in"][nxt]).then_inc(S[f"w_a{j}"], 16)
                hold(pool, S["kept"], done, S["held_pool"])
                store(n[0] + j, j)

            def store_1(c, j):
                nc.gpsimd.dma_start(proj[c, :, 0:SPLIT], staged[j][:, 0:SPLIT]).then_inc(S[f"proj_out{j}"], 16)
                nc.gpsimd.dma_start(proj[c, :, SEQ:TOK], staged[j][:, SPLIT:SPLIT + NS]).then_inc(S[f"proj_out{j}"], 16)

            def store_2(c, j):
                nc.gpsimd.dma_start(proj[c, :, SPLIT:SEQ], staged[j][:, 0:SPLIT]).then_inc(S[f"proj_out{j}"], 16)

            for j in range(2):
                nc.gpsimd.dma_start(wp[j], a["w_in"][j]).then_inc(S[f"w_a{j}"], 16)
            for base, store in ((0, store_1), (CHUNKS, store_2)):
                with pool.Fori(0, CHUNKS // 2 - 1) as it:
                    for j in range(2):
                        block_io((2 * it, j), base, 2 * it + j + 2, store)
                for j in range(2):
                    block_io((CHUNKS - 2, j), base, j if base == 0 else None, store)

            def body(p):
                w, v, u, f = parts(p)
                for k in range(PICKS + V_LAG):
                    if u is not None and k < steps_of(u):
                        if k == 0 and isinstance(p, int) and p == -1:
                            pool.wait_ge(S["proj_out0"], OUT_2)
                            pool.wait_ge(S["proj_out1"], OUT_2)
                        if not (isinstance(p, int) and p == -1 and k < U_RING):
                            hold(pool, S["dots"], PICKS * u + k - U_RING + 1, S["held_pool"])
                        nc.gpsimd.indirect_dma_start(
                            u_rows[:, k % U_RING, :], None, a["peer_u"],
                            bass.IndirectOffsetOnAxis(ap=idx_u[:, k:k + 1], axis=0), engine_sem=S["u_written"])\
                            .then_inc(u_row[k % U_RING], 16)
                    kv = k - V_LAG
                    if v is not None and 0 <= kv < steps_of(v):
                        if not (isinstance(v, int) and v == 0 and kv < V_RING):
                            hold(pool, S["vsum"], summed(PICKS * v + kv - V_RING + 1), S["held_pool"])
                        nc.gpsimd.indirect_dma_start(
                            v_rows[:, kv % V_RING, :], None, a["peer_v"],
                            bass.IndirectOffsetOnAxis(ap=idx_v[:, kv:kv + 1], axis=0), engine_sem=S["v_written"])\
                            .then_inc(v_row[kv % V_RING], 16)
                    if k == HEAD_AT:
                        move(slice(0, HEAD), u, f, 1)
                    if k == TAIL_AT:
                        move(slice(HEAD, PICKS), None if is_sample(v) else v, None if is_sample(u) else u, 2)

            def move(cols, to_v, to_u, part):
                if to_v is not None:
                    if part == 1:
                        hold(pool, S["dots"], PICKS * to_v + min(steps_of(to_v), HEAD), S["held_pool"])
                        if not (isinstance(to_v, int) and to_v == 0):
                            hold(pool, S["vsum"], summed(PICKS * (to_v - 1) + HEAD), S["held_pool"])
                    else:
                        hold(pool, S["dots"], PICKS * to_v + PICKS, S["held_pool"])
                        if not (isinstance(to_v, int) and to_v == 0):
                            hold(pool, S["vsum"], summed(PICKS * to_v), S["held_pool"])
                    nc.gpsimd.tensor_copy(idx_v[:, cols], idx_u[:, cols]).then_inc(S["idx_moved"], 1)
                    hold(pool, S["idx_moved"], 2 * to_v + part, S["held_pool"])
                if to_u is not None:
                    hold(pool, S["topk_done"], to_u + 1, S["held_pool"])
                    nc.gpsimd.tensor_copy(idx_u[:, cols], idx_f[:, cols]).then_inc(S["idx_taken"], 1)
                    hold(pool, S["idx_taken"], 2 * to_u + part, S["held_pool"])

            periods(pool, None, body)

        @block.scalar
        def _(act):
            own = Own(act, S["own_act"], ACT_PER)
            act.wait_ge(S["consts_in"], 16 * 12)

            act.wait_ge(S["set_up"], 1)
            act.wait_ge(S["lb_shifted"], 1)
            nc.scalar.activation(lb_in, lb_in, ACT.Exp).then_inc(S["lb_exp"], 1)
            def root(i):
                n = ntok(ORDER[i])
                act.wait_ge(S[f"x_a{i % 2}"], 16 * (i // 2 + 1))
                if i >= 1:
                    act.wait_ge(S["a_scaled"], i)
                    own.settle()
                own.mark(nc.scalar.activation(r3[0:n, :], x_a[i % 2][0:n, :], ACT.Square, accum_out=ssq[0:n, :]))
                own.settle()
                nc.scalar.activation(rstd[0:n, :], ssq[0:n, :], ACT.Sqrt, bias=eps[0:n, :], scale=1.0 / D)\
                  .then_inc(S["a_root"], 1)
            for i in range(FIRST):
                root(i)
            for half in range(2):
                act.wait_ge(S["bias_mm"], half + 1)
                nc.scalar.activation(replicated[half].rearrange("p (h s) -> p h s", h=4), ps[:, 4:8, 0:SKEW], ACT.Copy)\
                  .then_inc(S["bias_kept"], 1)

            def keep_block(it, j):
                act.wait_ge(S["wp_done"], 2 * it + j + 1)
                if not (isinstance(it, int) and it == 0):
                    act.wait_ge(S[f"proj_out{j}"], 32 * it)
                nc.scalar.activation(staged[j][:, 0:SPLIT], ps[:, 2 + j, :], ACT.Copy)
                nc.scalar.activation(staged[j][:, SPLIT:SPLIT + NS], ps[:, 4 + j, 0:NS], ACT.Copy).then_inc(S["kept"], 1)
            for n in range(4):
                root(FIRST + n)
                keep_block(n // 2, n % 2)
            with act.Fori(2, CHUNKS // 2) as it:
                for j in range(2):
                    keep_block(it, j)

            def keep_second(b):
                j = b % 2
                act.wait_ge(S["wp_done"], CHUNKS + b + 1)
                act.wait_ge(S[f"proj_out{j}"], OUT_1 + 16 * (b // 2))
                nc.scalar.activation(staged[j][:, 0:SPLIT], ps[:, j, :], ACT.Copy).then_inc(S["kept"], 1)

            def exps(f, kv, lo):
                act.wait_ge(S["s_masked"], 2 * f + kv + 1)
                for j in range(GRP):
                    h = GRP * kv + j
                    own.mark(nc.scalar.activation(probs[:, j, lo:2 * P], probs[:, j, lo:2 * P], ACT.Exp,
                                                  bias=nmax[:, h:h + 1], accum_out=den[:, h:h + 1]))
                nc.scalar.activation(esink[:, GRP * kv:GRP * (kv + 1)], esink[:, GRP * kv:GRP * (kv + 1)], ACT.Exp)\
                  .then_inc(S["p_ready"], 1)

            def keep_probs(f, kv, first):
                act.wait_ge(S["p_turned"], 2 * f + kv + 1)
                act.wait_ge(S["pv"], 2 * f + kv)
                for j in range(2):
                    bank = F[(3 if kv == 0 else 0) + j].rearrange("p (h b t) -> p h b t", h=2, b=2)
                    lo = 1 if first else 0
                    last = nc.scalar.activation(probs_t[:, 2 * j:2 * j + 2, lo:2, :], bank[:, :, lo:2, :], ACT.Copy)
                last.then_inc(S["p_kept"], 1)

            def front(k, f):
                q = k if is_sample(f) else k + SKIP
                first = isinstance(f, int) and f == 0
                n = NS if is_sample(f) else P
                if not is_sample(f):
                    if k == 1 and not first:
                        act.wait_ge(S["pv"], 2 * f)
                        nc.scalar.activation(v_n[:, 0, :], v_n[:, 1, :], ACT.Copy)
                        nc.scalar.activation(k_t[:, 0, :], k_t[:, 1, :], ACT.Copy).then_inc(S["kv_shifted"], 1)
                    if k == 1 and first:
                        nc.scalar.activation(k_t[:, 0, 0:1], eps, ACT.Copy).then_inc(S["kv_shifted"], 1)
                    if k == 6:
                        act.wait_ge(S["turned"], f + 1)
                        act.wait_ge(S["proj_in"], 48 * f + 48)
                        nc.scalar.activation(slots(C_I, 4), F[0].rearrange("p (c t) -> p c t", c=4), ACT.Copy)
                        nc.scalar.activation(slots(C_G, 4), F[1].rearrange("p (c t) -> p c t", c=4), ACT.Silu)
                        nc.scalar.activation(v_n[:, 1, :], F[2][:, 0:P], ACT.Copy).then_inc(S["v_kept"], 1)
                        nc.scalar.activation(slots(C_QH, 4), slots(C_QH, 4), ACT.Silu)
                        nc.scalar.activation(slots(C_F, 4), slots(C_F, 4), ACT.Sigmoid).then_inc(S["kept_ig"], 1)
                    for kv in range(KV):
                        if k == 12 + 7 * kv:
                            exps(f, kv, P if first else 0)
                        if k == 16 + 7 * kv:
                            keep_probs(f, kv, first)
                    if k == 29:
                        act.wait_ge(S["hg_f"], f + 1)
                        act.wait_ge(S["pv"], 2 * f + 2)
                        nc.scalar.activation(cum.rearrange("p (c t) -> p c t", c=4), slots(C_F, 4), ACT.Ln)\
                          .then_inc(S["hg_ln"], 1)
                    for l in range(NL - 1):
                        if k == 33 + 3 * l:
                            act.wait_ge(S["lev_d"], (NL - 1) * f + l + 1)
                            nc.scalar.activation(lev[l % 2], lev[l % 2], ACT.Exp).then_inc(S["lev_e"], 1)
                    if k == 37:
                        act.wait_ge(S["hg_k"], f + 1)
                        nc.scalar.activation(slots(C_Q, 4), cum.rearrange("p (c t) -> p c t", c=4), ACT.Exp)\
                          .then_inc(S["qe_exp"], 1)
                    if k == 55:
                        act.wait_ge(S["kd_d"], f + 1)
                        nc.scalar.activation(lev[1], lev[1], ACT.Exp).then_inc(S["kd_exp"], 1)
                    if k == 59:
                        act.wait_ge(S["kd_turned"], f + 1)
                        nc.scalar.activation(kd_n, F[2], ACT.Copy).then_inc(S["kd_kept"], 1)
                    if k == 63:
                        act.wait_ge(S["hg_out"], f + 1)
                        nc.scalar.activation(mix[:, 512:1024], F[3], ACT.Copy)
                        for h in range(HG):
                            own.mark(nc.scalar.activation(lev[0][:, P * h:P * (h + 1)], F[3][:, P * h:P * (h + 1)],
                                                          ACT.Square, accum_out=ssq4[:, h:h + 1]))
                        own.settle()
                        nc.scalar.activation(ssq4, ssq4, ACT.Sqrt, bias=eps, scale=1.0 / P).then_inc(S["rms_root"], 1)
                else:
                    sample_front(k, f)
                if q == 81:
                    act.wait_ge(S["h_ready"], f + 1)
                    own.mark(nc.scalar.activation(r2[0:n, 0:D], hx[0:n, :], ACT.Square, accum_out=ssq[0:n, :]))
                    own.settle()
                    nc.scalar.activation(rstd[0:n, :], ssq[0:n, :], ACT.Sqrt, bias=eps[0:n, :], scale=1.0 / D)\
                      .then_inc(S["ssq_root"], 1)
                if q == 84:
                    act.wait_ge(S["hn_turned"], f + 1)
                    for j in range(2):
                        last = nc.scalar.activation(hn_t[:, 4 * j:4 * j + 4, 0:n],
                                                    F[4 + j][:, 0:4 * n].rearrange("p (c t) -> p c t", c=4), ACT.Copy)
                    last.then_inc(S["hn_kept"], 1)
                for g in range(4):
                    if q == 88 + 3 * g:
                        act.wait_ge(S["sc_mm"], 4 * f + g + 1)
                        nc.scalar.activation(sc[0:n, 4 * g:4 * g + 4, :], F[g][0:n, :].rearrange("p (c t) -> p c t", c=4),
                                             ACT.Copy).then_inc(S["sc_kept"], 1)
                if q == 114:
                    act.wait_ge(S["gate_d"], f + 1)
                    nc.scalar.activation(fv[0:n], gate_f[0:n, :].rearrange("p (h k) -> p h k", h=PH), ACT.Exp).then_inc(S["gate_exp"], 1)

            def sample_front(k, f):
                if k == 5:
                    act.wait_ge(S["k7_turned"], 1)
                    act.wait_ge(S["y_ready"], f - 2)
                    nc.scalar.activation(r3[:, 896:1024], F[5][:, 0:P], ACT.Copy).then_inc(S["k7_kept"], 1)
                if k == 6:
                    act.wait_ge(S["turned"], f + 1)
                    act.wait_ge(S["out_kv"], 16 * 5)
                    nc.scalar.activation(v_n[0:NS, 1, :], F[2][0:NS, 0:P], ACT.Copy).then_inc(S["v_kept"], 1)
                    nc.scalar.activation(r3[0:NS, 896:1024], F[2][0:NS, P:2 * P], ACT.Copy).then_inc(S["v_kept"], 1)
                if k == 9:
                    act.wait_ge(S["s_bias_mm"], 1)
                    nc.scalar.activation(s_bias, F[5][:, 0:264].rearrange("p (g j) -> p g j", g=KV), ACT.Copy)\
                      .then_inc(S["s_bias_kept"], 1)
                for kv in range(KV):
                    if k == 14 + 14 * kv:
                        act.wait_ge(S["s_masked"], 2 * f + kv + 1)
                        own.mark(nc.scalar.activation(s_probs, s_probs, ACT.Exp, bias=nmax[:, kv:kv + 1],
                                                      accum_out=den[:, kv:kv + 1]))
                        nc.scalar.activation(esink[:, kv:kv + 1], esink[:, kv:kv + 1], ACT.Exp).then_inc(S["p_ready"], 1)
                    if k == 18 + 14 * kv:
                        act.wait_ge(S["p_turned"], 2 * f + kv + 1)
                        for c in range(9):
                            m = P if c < 8 else NS
                            src = F[3 + c // 4][0:m, P * (c % 4):P * (c % 4 + 1)]
                            last = nc.scalar.activation(s_probs_t[c][0:m, :], src, ACT.Copy)
                        last.then_inc(S["p_kept"], 1)
                if k == 42:
                    act.wait_ge(S["s_turned"], 1)
                    nc.scalar.activation(s_nat[:, 0:512], F[0][0:NS, :], ACT.Copy)
                    nc.scalar.activation(s_nat[:, 512:1024], F[1][0:NS, :], ACT.Silu)
                    nc.scalar.activation(slots(C_QH, 4, spj), slots(C_QH, 4, spj), ACT.Silu)
                    nc.scalar.activation(slots(C_F, 4, spj), slots(C_F, 4, spj), ACT.Sigmoid).then_inc(S["kept_ig"], 1)
                if k == 44:
                    act.wait_ge(S["hg_f"], f + 1)
                    nc.scalar.activation(s_cum.rearrange("p (c t) -> p c t", c=4), slots(C_F, 4, spj), ACT.Ln)\
                      .then_inc(S["hg_ln"], 1)
                for l in range(2):
                    if k == 48 + 2 * l:
                        act.wait_ge(S["lev_d"], (NL - 1) * f + l + 1)
                        nc.scalar.activation(s_lev[l], s_lev[l], ACT.Exp).then_inc(S["lev_e"], 1)
                if k == 50:
                    nc.scalar.activation(s_qe, s_cum, ACT.Exp).then_inc(S["qe_exp"], 1)
                if k == 54:
                    act.wait_ge(S["kd_d"], f + 1)
                    nc.scalar.activation(s_lev[0], s_lev[0], ACT.Exp).then_inc(S["kd_exp"], 1)
                if k == 58:
                    act.wait_ge(S["kd_turned"], f + 1)
                    nc.scalar.activation(s_kdn, F[2][0:NS, :], ACT.Copy).then_inc(S["kd_kept"], 1)
                if k == 69:
                    act.wait_ge(S["st_mm"], DEC_B)
                    nc.scalar.activation(s_ot, F[4][:, 0:P], ACT.Copy).then_inc(S["ot_kept"], 1)
                if k == 71:
                    act.wait_ge(S["ot_turned"], 1)
                    act.wait_ge(S["out_kv"], 16 * (5 + 2 * DEC_B))
                    nc.scalar.activation(mix[0:NS, 512:1024], F[5][0:NS, :], ACT.Copy).then_inc(S["o_kept"], 1)
                if k == 73:
                    act.wait_ge(S["o_kept"], 2)
                    for h in range(HG):
                        own.mark(nc.scalar.activation(r2[0:NS, P * h:P * (h + 1)], mix[0:NS, 512 + P * h:512 + P * (h + 1)],
                                                      ACT.Square, accum_out=ssq4[0:NS, h:h + 1]))
                    own.settle()
                    nc.scalar.activation(ssq4[0:NS, :], ssq4[0:NS, :], ACT.Sqrt, bias=eps[0:NS, :], scale=1.0 / P)\
                      .then_inc(S["rms_root"], 1)

            def body(p):
                w, v, u, f = parts(p)
                for k in range(PICKS):
                    if v is not None and k < steps_of(v):
                        if k == 0:
                            act.wait_ge(S["wv_ready"], v + 1)
                        act.wait_ge(S["vsum"], summed(PICKS * v + k - 1))
                        m = NS if is_sample(v) else P
                        nc.scalar.activation(diag[:, k % 2, 0:m], fold if is_sample(v) else ident[:, :], ACT.Copy,
                                             scale=w_v[:, k:k + 1]).then_inc(S["diag_ready"], 1)
                    if isinstance(p, int) and p == -2 and k % BLOCK_EVERY == 3 and k // BLOCK_EVERY < CHUNKS:
                        keep_second(k // BLOCK_EVERY)
                    if k == 2 and w is not None:
                        m = ntok(w)
                        act.wait_ge(S["y_taken"], w + 1)
                        own.mark(nc.scalar.activation(r2[0:m, 0:D], hx[0:m, :], ACT.Square, accum_out=ssq_y[0:m, :]))
                        own.settle()
                        nc.scalar.activation(rstd_y[0:m, :], ssq_y[0:m, :], ACT.Sqrt, bias=eps[0:m, :], scale=1.0 / D)\
                          .then_inc(S["y_root"], 1)
                    if f is not None:
                        front(k, f)
                if u is not None:
                    act.wait_ge(S["dots"], PICKS * u + steps_of(u))
                    nc.scalar.activation(act_u[:, 0:steps_of(u)], act_u[:, 0:steps_of(u)], ACT.Gelu)\
                      .then_inc(S["act_ready"], 1)

            periods(act, own, body)

        @block.tensor
        def _(pe):
            pe.wait_ge(S["consts_in"], 16 * 12)
            def turn_tile(i):
                n = ntok(ORDER[i])
                pe.wait_ge(S["a_scaled"], i + 1)
                for j in range(2):
                    if i >= 1:
                        pe.wait_ge(S["a_kept"], 2 * i - 1 + j)
                    for c in range(4):
                        cc = 4 * j + c
                        last = nc.tensor.transpose(ps[:, j, c * P:c * P + n], x_a[i % 2][0:n, cc * P:(cc + 1) * P],
                                                   ident[0:n, 0:n])
                last.then_inc(S["a_turned"], 1)

            for i in range(FIRST):
                turn_tile(i)
                if i < 4:
                    pe.wait_ge(S["keys_in"], 16)
                    pe.wait_ge(S[f"w_q_in{i}"], 16)
                    for c in range(4 * i, 4 * i + 4):
                        if c >= 2:
                            pe.wait_ge(S["m_kept"], c - 1)
                        for d in range(DC):
                            last = nc.tensor.matmul(ps[:, 4 + 2 * (c % 2) + d // 4, P * (d % 4):P * (d % 4 + 1)],
                                                    w_sc[:, c, P * d:P * (d + 1)], keys[:, c, :], start=True, stop=True)
                        last.then_inc(S["m_mm"], 1)
            pe.wait_ge(S["table_in"], 32)
            pe.wait_ge(S["set_up"], 1)
            pe.wait_ge(S["m_kept"], 2 * PH)
            for half in range(2):
                if half:
                    pe.wait_ge(S["bias_kept"], 1)
                for h in range(4):
                    last = nc.tensor.matmul(ps[:, 4 + h, 0:SKEW], table[:, 4 * half + h, :], bucket_of, start=True, stop=True)
                last.then_inc(S["bias_mm"], 1)
            pe.wait_ge(S["a_kept"], 2 * FIRST)
            pe.wait_ge(S["bias_kept"], 2)

            def project(it, j, first):
                pe.wait_ge(S[f"w_a{j}"], 16 * it + 16)
                if not first:
                    pe.wait_ge(S["kept"], 2 * it - 1 + j)
                for c in range(DC):
                    nc.tensor.matmul(ps[:, 2 + j, :], wp[j][:, c, :], xn_t[:, c, 0:SPLIT], start=(c == 0), stop=(c == DC - 1))
                for c in range(DC):
                    last = nc.tensor.matmul(ps[:, 4 + j, 0:NS], wp[j][:, c, :], xn_t[:, c, SEQ:TOK],
                                            start=(c == 0), stop=(c == DC - 1))
                last.then_inc(S["wp_done"], 1)
            for n in range(4):
                project(n // 2, n % 2, n < 2)
                turn_tile(FIRST + n)
            with pe.Fori(2, CHUNKS // 2) as it:
                for j in range(2):
                    project(it, j, False)

            def project_second(b):
                j = b % 2
                if b == 0:
                    pe.wait_ge(S["a_kept"], 2 * (TILES + 1))
                pe.wait_ge(S[f"w_a{j}"], 16 * (CHUNKS // 2 + b // 2 + 1))
                if b >= 2:
                    pe.wait_ge(S["kept"], CHUNKS + b - 1)
                for c in range(DC):
                    last = nc.tensor.matmul(ps[:, j, :], wp[j][:, c, :], xn_t[:, c, SPLIT:SEQ],
                                            start=(c == 0), stop=(c == DC - 1))
                last.then_inc(S["wp_done"], 1)

            def turn(bank, src, count, n=P, m=P):
                for c in range(count):
                    last = nc.tensor.transpose(bank[0:m, c * n:(c + 1) * n], src[0:n, c * m:(c + 1) * m], ident[0:n, 0:n])
                return last

            def front(k, f):
                q = k if is_sample(f) else k + SKIP
                first = isinstance(f, int) and f == 0
                lo = 1 if first else 0
                n = NS if is_sample(f) else P
                if is_sample(f):
                    sample_front(k, f)
                else:
                    if k == 4:
                        if first:
                            pe.wait_ge(S["kept"], CHUNKS)
                            pe.wait_ge(S["w_o_in"], 16)
                        pe.wait_ge(S["proj_in"], 48 * f + 48)
                        for c in range(4):
                            nc.tensor.transpose(F[0][:, P * c:P * (c + 1)], slots(C_I + c, 1)[:, 0, :], ident[:, :])
                        for c in range(4):
                            nc.tensor.transpose(F[1][:, P * c:P * (c + 1)], slots(C_G + c, 1)[:, 0, :], ident[:, :])
                        nc.tensor.transpose(F[2][:, 0:P], slots(C_V, 1)[:, 0, :], ident[:, :]).then_inc(S["turned"], 1)
                    for kv in range(KV):
                        part = slice(DH * kv, DH * (kv + 1))
                        base = 3 if kv == 0 else 0
                        if k == 8 + 4 * kv:
                            pe.wait_ge(S["kept_ig"], f + 1)
                            pe.wait_ge(S["kv_shifted"], f + 1)
                            for j in range(GRP):
                                last = nc.tensor.matmul(F[base + j // 2][:, 256 * (j % 2) + P * lo:256 * (j % 2) + 256],
                                                        slots(C_Q + j, 1)[part, 0, :], k_t[part, lo:2, :],
                                                        start=True, stop=True)
                            last.then_inc(S["scores"], 1)
                        if k == 14 + 7 * kv:
                            pe.wait_ge(S["p_ready"], 2 * f + kv + 1)
                            for j in range(GRP):
                                for b in range(lo, 2):
                                    last = nc.tensor.transpose(F[base + j // 2][:, 256 * (j % 2) + P * b:256 * (j % 2) + P * (b + 1)],
                                                               probs[:, j, P * b:P * (b + 1)], ident[:, :])
                            last.then_inc(S["p_turned"], 1)
                        if k == 18 + 7 * kv:
                            pe.wait_ge(S["p_kept"], 2 * f + kv + 1)
                            pe.wait_ge(S["v_kept"], f + 1)
                            for j in range(GRP):
                                h = GRP * kv + j
                                for b in range(lo, 2):
                                    last = nc.tensor.matmul(F[5][:, DH * h:DH * (h + 1)], probs_t[:, j, b, :],
                                                            v_n[:, b, part], start=(b == lo), stop=(b == 1))
                            last.then_inc(S["pv"], 1)
                    for l in range(NL):
                        if k == 35 + 3 * l:
                            if l < NL - 1:
                                pe.wait_ge(S["lev_q"], (NL - 1) * f + l + 1)
                                lhs = rhs = lev[l % 2].rearrange("p (c t) -> p c t", c=4)
                            else:
                                lhs, rhs = slots(C_F, 4), slots(C_QH, 4)
                            if l >= 2:
                                pe.wait_ge(S["lev_kept"], NL * f + l - 1)
                            for h in range(HG):
                                last = nc.tensor.matmul(F[l % 2][:, P * h:P * (h + 1)], lhs[:, h, :], rhs[:, h, :],
                                                        start=True, stop=True)
                            last.then_inc(S["lev_mm"], 1)
                    if k == 58:
                        pe.wait_ge(S["kd_ready"], f + 1)
                        turn(F[2], lev[1], HG).then_inc(S["kd_turned"], 1)
                    if k == 61:
                        pe.wait_ge(S["lev_kept"], NL * f + NL)
                        pe.wait_ge(S["kd_kept"], f + 1)
                        pe.wait_ge(S["qe_ready"], f + 1)
                        pe.wait_ge(S["s_new"], f)
                        for h in range(HG):
                            cols = slice(P * h, P * (h + 1))
                            nc.tensor.matmul(F[3][:, cols], a_t[:, h, :], slots(C_I, 4)[:, h, :], start=True, stop=False)
                            nc.tensor.matmul(F[3][:, cols], slots(C_Q, 4)[:, h, :], state[:, h, :], start=False, stop=True)
                        for h in range(HG):
                            cols = slice(P * h, P * (h + 1))
                            last = nc.tensor.matmul(F[4][:, cols], kd_n[:, cols], slots(C_I, 4)[:, h, :], start=True, stop=True)
                        last.then_inc(S["hg_out"], 1)
                if q == 75:
                    pe.wait_ge(S["mix_ready"], f + 1)
                    turn(F[0], mix[:, 0:512], 4, n)
                    turn(F[1], mix[:, 512:1024], 4, n).then_inc(S["mix_turned"], 1)
                if q in (77, 79):
                    j = (q - 77) // 2
                    pe.wait_ge(S["mix_kept"], f + 1)
                    for c in range(DC):
                        last = nc.tensor.matmul(F[2 + j][0:n, :], mix_t[:, c, 0:n], w_o[:, c, 512 * j:512 * (j + 1)],
                                                start=(c == 0), stop=(c == DC - 1))
                    last.then_inc(S["h_mm"], 1)
                if q == 83:
                    pe.wait_ge(S["hn_ready"], f + 1)
                    turn(F[4], hn[:, 0:512], 4, n)
                    turn(F[5], hn[:, 512:1024], 4, n).then_inc(S["hn_turned"], 1)
                for g in range(4):
                    if q == 86 + 3 * g:
                        pe.wait_ge(S["hn_kept"], f + 1)
                        for d in range(DC):
                            last = nc.tensor.matmul(F[g][0:n, :], hn_t[:, d, 0:n],
                                                    w_sc[:, 4 * g:4 * g + 4, P * d:P * (d + 1)],
                                                    start=(d == 0), stop=(d == DC - 1))
                        last.then_inc(S["sc_mm"], 1)

            def sample_front(k, f):
                if k == 1:
                    nc.tensor.transpose(F[5][:, 0:P], k_t[:, 1, :], ident[:, :]).then_inc(S["k7_turned"], 1)
                if k == 4:
                    pe.wait_ge(S["proj_in"], 48 * f + 48)
                    nc.tensor.transpose(F[2][0:NS, 0:P], slots(C_V, 1, spj)[:, 0, :], ident[:, :])
                    nc.tensor.transpose(F[2][0:NS, P:2 * P], k_t[:, 1, 0:NS], ident[:, :]).then_inc(S["turned"], 1)
                if k == 7:
                    pe.wait_ge(S["s_tab_ready"], 2)
                    pe.wait_ge(S["caches_in"], 64)
                    pe.wait_ge(S["k7_kept"], 1)
                    for g in range(KV):
                        last = nc.tensor.matmul(F[5][:, 132 * g:132 * (g + 1)], s_tab[:, P * g:P * (g + 1)], s_oh,
                                                start=True, stop=True)
                    last.then_inc(S["s_bias_mm"], 1)
                for kv in range(KV):
                    part = slice(DH * kv, DH * (kv + 1))
                    if k == 10 + 14 * kv:
                        if kv == 0:
                            pe.wait_ge(S["v_kept"], f + 2)
                        else:
                            pe.wait_ge(S["mix_attn"], f + kv)
                        for j in range(GRP):
                            q = slots(C_Q + j, 1, spj)[part, 0, :]
                            out_rows = slice(NS * j, NS * (j + 1))
                            nc.tensor.matmul(F[0][out_rows, :], q, kc_t[part, 0:512], start=True, stop=True)
                            nc.tensor.matmul(F[1][out_rows, :], q, kc_t[part, 512:1024], start=True, stop=True)
                            last = nc.tensor.matmul(F[2][out_rows, 0:NS], q, k_t[part, 1, 0:NS], start=True, stop=True)
                        last.then_inc(S["scores"], 1)
                    if k == 16 + 14 * kv:
                        pe.wait_ge(S["p_ready"], 2 * f + kv + 1)
                        pe.wait_ge(S["s_bias_kept"], 1)
                        for c in range(9):
                            m = P if c < 8 else NS
                            last = nc.tensor.transpose(F[3 + c // 4][0:m, P * (c % 4):P * (c % 4 + 1)],
                                                       s_probs[:, P * c:P * c + m], ident[:, :])
                        last.then_inc(S["p_turned"], 1)
                    if k == 20 + 14 * kv:
                        pe.wait_ge(S["p_kept"], 2 * f + kv + 1)
                        for c in range(9):
                            m = P if c < 8 else NS
                            values = vc[:, c, part] if c < 8 else v_n[0:NS, 1, part]
                            last = nc.tensor.matmul(F[2][:, 64:128], s_probs_t[c][0:m, :], values,
                                                    start=(c == 0), stop=(c == 8))
                        last.then_inc(S["pv"], 1)
                if k == 40:
                    for c in range(4):
                        nc.tensor.transpose(F[0][0:NS, P * c:P * (c + 1)], slots(C_I + c, 1, spj)[:, 0, :], ident[:, :])
                    for c in range(4):
                        last = nc.tensor.transpose(F[1][0:NS, P * c:P * (c + 1)], slots(C_G + c, 1, spj)[:, 0, :], ident[:, :])
                    last.then_inc(S["s_turned"], 1)
                for l in range(3):
                    if k == 50 + 2 * l:
                        if l < 2:
                            pe.wait_ge(S["lev_q"], (NL - 1) * f + l + 1)
                            lhs = rhs = s_lev[l].rearrange("p (c t) -> p c t", c=4)
                        else:
                            lhs, rhs = slots(C_F, 4, spj), slots(C_QH, 4, spj)
                        if l == 0:
                            pe.wait_ge(S["kept_ig"], f + 1)
                        else:
                            pe.wait_ge(S["lev_kept"], NL * f + l)
                        for h in range(HG):
                            last = nc.tensor.matmul(F[0][0:NS, NS * h:NS * (h + 1)], lhs[:, h, :], rhs[:, h, :],
                                                    start=True, stop=True)
                        last.then_inc(S["lev_mm"], 1)
                if k == 57:
                    pe.wait_ge(S["kd_ready"], f + 1)
                    for h in range(HG):
                        last = nc.tensor.transpose(F[2][0:NS, P * h:P * (h + 1)], s_lev[0][:, NS * h:NS * (h + 1)], ident[:, :])
                    last.then_inc(S["kd_turned"], 1)
                if k == 59:
                    pe.wait_ge(S["lev_kept"], NL * f + 3)
                    for h in range(HG):
                        cols = slice(P * h, P * (h + 1))
                        nc.tensor.matmul(F[3][0:NS, cols], a_t[0:NS, h, 0:NS], s_nat[:, cols], start=True, stop=True)
                for b in range(DEC_B):
                    if k == 60 + b:
                        pe.wait_ge(S["qe_ready"], f + 1)
                        pe.wait_ge(S[f"st_in{b % 2}"], 16 * (b // 2 + 1))
                        pe.wait_ge(S["kdm_ready"], b + 1)
                        if b >= 2:
                            pe.wait_ge(S["st_new"], b - 1)
                        for h in range(HG):
                            col = NS * h + DEC_T * b
                            nc.tensor.matmul(F[4][:, col:col + DEC_T], s_st[b % 2][:, P * h:P * (h + 1)],
                                             s_qe[:, col:col + DEC_T], start=True, stop=True)
                        for h in range(HG):
                            cols = slice(P * h, P * (h + 1))
                            last = nc.tensor.matmul(F[b % 2][:, cols], s_kdm[b % 2][:, cols], s_nat[:, cols],
                                                    start=True, stop=True)
                        last.then_inc(S["st_mm"], 1)
                if k == 70:
                    pe.wait_ge(S["ot_kept"], 1)
                    for h in range(HG):
                        last = nc.tensor.transpose(F[5][0:NS, P * h:P * (h + 1)], s_ot[:, NS * h:NS * (h + 1)], ident[:, :])
                    last.then_inc(S["ot_turned"], 1)

            def body(p):
                w, v, u, f = parts(p)
                for k in range(PICKS):
                    if v is not None and k < steps_of(v):
                        if k == 0 and w is not None:
                            pe.wait_ge(S["y_taken"], v)
                        pe.wait_ge(S["diag_ready"], PICKS * v + k + 1)
                        pe.wait_ge(v_row[k % V_RING], 16 * (PICKS // V_RING) * v + 16 * (k // V_RING + 1))
                        m = NS if is_sample(v) else P
                        for j in range(2):
                            last = nc.tensor.matmul(Y[j][0:m, :], diag[:, k % 2, 0:m], v_rows[:, k % V_RING, 512 * j:512 * (j + 1)],
                                                    start=(k == 0), stop=(k == steps_of(v) - 1))
                        last.then_inc(S["vsum"], 1)
                    if isinstance(p, int) and p == -2 and k % BLOCK_EVERY == 2 and k // BLOCK_EVERY < CHUNKS:
                        project_second(k // BLOCK_EVERY)
                    if f is not None:
                        front(k, f)

            pe.sem_inc(S["vsum"], summed(0))
            periods(pe, None, body)

        @block.vector
        def _(dve):
            own = Own(dve, S["own_dve"], DVE_PER)
            mark, settle = own.mark, own.settle
            V = nc.vector
            mark(V.memset(eps, EPS))
            mark(V.memset(one, 1.0))
            mark(V.memset(hn[BUCKETS:BUCKETS + 1, :], NEG))
            mark(V.memset(state[:, :, :], 0.0))
            mark(V.memset(a_t[:, :, :], 0.0))
            V.memset(mix_scale[:, 0:4], 1.0).then_inc(S["set_up"], 1)
            dve.wait_ge(S["consts_in"], 16 * 12)
            mark(V.tensor_copy(level_masks[:, :, :], hn_u[:, :].rearrange("p (l t) -> p l t", l=NL)))
            lb_e = lb_in.rearrange("p (r h) -> p r h", r=2)
            mark(V.tensor_tensor(lb, lb_e[:, 0, :], lb_e[:, 1, :], ALU.max))
            settle()
            for r in range(2):
                last = V.tensor_tensor(lb_e[:, r, :], lb_e[:, r, :], lb, ALU.subtract)
            last.then_inc(S["lb_shifted"], 1)
            dve.wait_ge(S["lb_exp"], 1)
            mark(V.tensor_tensor(oml, lb_e[:, 0, :], lb_e[:, 1, :], ALU.add))
            settle()
            mark(V.reciprocal(oml, oml))
            settle()
            mark(V.tensor_tensor(lb, lb_e[:, 0, :], oml, ALU.mult))
            settle()
            mark(V.tensor_scalar(oml, lb, -1.0, 1.0, ALU.mult, ALU.add))
            settle()

            def scale_and_keep(i):
                tile = ORDER[i]
                n = ntok(tile)
                dve.wait_ge(S["a_root"], i + 1)
                mark(V.reciprocal(rstd[0:n, :], rstd[0:n, :]))
                settle()
                V.tensor_scalar(x_a[i % 2][0:n, :], x_a[i % 2][0:n, :], rstd[0:n, :], None, ALU.mult)\
                    .then_inc(S["a_scaled"], 1)
                dve.wait_ge(S["a_turned"], i + 1)
                for j in range(2):
                    V.tensor_tensor(xn_t[:, 4 * j:4 * j + 4, P * tile:P * tile + n],
                                    ps[:, j, :].rearrange("p (c t) -> p c t", c=4)[:, :, 0:n],
                                    w_mix[:, 4 * j:4 * j + 4].unsqueeze(2).to_broadcast([P, 4, n]), ALU.mult)\
                        .then_inc(S["a_kept"], 1)
            for i in range(TILES + 1):
                scale_and_keep(i)
                if i < 4:
                    for c in range(4 * i, 4 * i + 4):
                        dve.wait_ge(S["m_mm"], c + 1)
                        bank = 4 + 2 * (c % 2)
                        V.tensor_copy(w_sc[:, c, :].rearrange("p (b x) -> p b x", b=2), ps[:, bank:bank + 2, :])\
                            .then_inc(S["m_kept"], 1)

            def mask_scores(f, kv, lo):
                dve.wait_ge(S["scores"], 2 * f + kv + 1)
                if isinstance(f, int) and f == 0:
                    dve.wait_ge(S["bias_in"], 16 * HEADS)
                if kv:
                    dve.wait_ge(S["p_turned"], 2 * f + kv)
                for j in range(2):
                    h = GRP * kv + 2 * j
                    bank = F[(3 if kv == 0 else 0) + j].rearrange("p (h s) -> p h s", h=2)
                    mark(V.scalar_tensor_tensor(probs[:, 2 * j:2 * j + 2, lo:2 * P], bank[:, :, lo:2 * P], SCALE,
                                                bias_v[:, h:h + 2, lo:2 * P], ALU.mult, ALU.add))
                settle()
                heads = slice(GRP * kv, GRP * (kv + 1))
                mark(V.tensor_reduce(rmax, probs[:, :, lo:2 * P], AX.X, ALU.max))
                settle()
                mark(V.tensor_tensor(rmax, rmax, sinks[:, heads], ALU.max))
                settle()
                V.tensor_tensor(esink[:, heads], sinks[:, heads], rmax, ALU.subtract)
                V.tensor_scalar(nmax[:, heads], rmax, -1.0, None, ALU.mult).then_inc(S["s_masked"], 1)

            def level_exponents(l, m, cum_v, out):
                b = cum_v.rearrange("p (x two m) -> p x two m", two=2, m=m)
                o = out.rearrange("p (x two m) -> p x two m", two=2, m=m)
                ref = b[:, :, 0, m - 1:m].to_broadcast([P, b.shape[1], m])
                V.tensor_tensor(o[:, :, 1, :], b[:, :, 1, :], ref, ALU.subtract)
                V.tensor_tensor(o[:, :, 0, :], ref, b[:, :, 0, :], ALU.subtract).then_inc(S["lev_d"], 1)

            def level_factors(l, m, e, q, kk):
                o = e.rearrange("p (x two m) -> p x two m", two=2, m=m)
                q = q.rearrange("p (x two m) -> p x two m", two=2, m=m)
                kk = kk.rearrange("p (x two m) -> p x two m", two=2, m=m)
                V.tensor_tensor(o[:, :, 1, :], o[:, :, 1, :], q[:, :, 1, :], ALU.mult)
                V.tensor_tensor(o[:, :, 0, :], o[:, :, 0, :], kk[:, :, 0, :], ALU.mult).then_inc(S["lev_q"], 1)

            flat = "p c t -> p (c t)"

            def front(k, f):
                q = k if is_sample(f) else k + SKIP
                first = isinstance(f, int) and f == 0
                n = NS if is_sample(f) else P
                lo = P if first else 0
                if is_sample(f):
                    sample_front(k, f)
                else:
                    q_s, k_s = slots(C_QH, 4).rearrange(flat), slots(C_F, 4).rearrange(flat)
                    for kv in range(KV):
                        if k == 10 + 7 * kv:
                            mask_scores(f, kv, lo)
                    if k == 20:
                        dve.wait_ge(S["kept_ig"], f + 1)
                        for h in range(HG):
                            last = V.tensor_scalar(slots(C_F, 4)[:, h, :], slots(C_F, 4)[:, h, :], oml[:, h:h + 1],
                                                   lb[:, h:h + 1], ALU.mult, ALU.add)
                        last.then_inc(S["hg_f"], 1)
                    if k == 27:
                        dve.wait_ge(S["pv"], 2 * f + 2)
                        dve.wait_ge(S["p_ready"], 2 * f + 2)
                        mark(V.tensor_tensor(den, den, esink, ALU.add))
                        settle()
                        mark(V.reciprocal(den, den))
                        settle()
                        V.tensor_tensor(mix[:, 0:512].rearrange("p (h d) -> p h d", h=HEADS),
                                        F[5].rearrange("p (h d) -> p h d", h=HEADS),
                                        den.unsqueeze(2).to_broadcast([P, HEADS, DH]), ALU.mult).then_inc(S["mix_attn"], 1)
                    if k == 30:
                        dve.wait_ge(S["hg_ln"], f + 1)
                        V.tensor_scalar(k_s, k_s, -1.0, 1.0, ALU.mult, ALU.add)
                        for h in range(HG):
                            last = V.tensor_tensor_scan(cum[:, P * h:P * (h + 1)], one.to_broadcast([P, P]),
                                                        cum[:, P * h:P * (h + 1)], 0.0, ALU.mult, ALU.add)
                        last.then_inc(S["hg_k"], 1)
                        dve.wait_ge(S["hg_k"], f + 1)
                    for l in range(NL):
                        if k == 32 + 3 * l and l < NL - 1:
                            if l >= 2:
                                dve.wait_ge(S["lev_mm"], NL * f + l - 1)
                            level_exponents(l, LEVELS[l], cum, lev[l % 2])
                        if k == 34 + 3 * l and l < NL - 1:
                            dve.wait_ge(S["lev_e"], (NL - 1) * f + l + 1)
                            level_factors(l, LEVELS[l], lev[l % 2], q_s, k_s)
                        if k == 36 + 3 * l:
                            hold(dve, S["lev_mm"], NL * f + l + 1, S["held_dve"])
                            if l:
                                hold(dve, S["lev_kept"], NL * f + l, S["held_dve"])
                            V.copy_predicated(a_t[:, :, :], level_masks[:, l:l + 1, :].to_broadcast([P, HG, P]),
                                              F[l % 2].rearrange("p (c t) -> p c t", c=4)).then_inc(S["lev_kept"], 1)
                    if k == 40:
                        dve.wait_ge(S["qe_exp"], f + 1)
                        mark(V.tensor_copy(decay, slots(C_Q, 4)[:, :, P - 1]))
                        settle()
                        V.tensor_tensor(slots(C_Q, 4), slots(C_Q, 4), slots(C_QH, 4), ALU.mult).then_inc(S["qe_ready"], 1)
                    if k == 54:
                        dve.wait_ge(S["lev_mm"], NL * f + 6)
                        c3 = cum.rearrange("p (c t) -> p c t", c=4)
                        V.tensor_tensor(lev[1].rearrange("p (c t) -> p c t", c=4),
                                        c3[:, :, P - 1:P].to_broadcast([P, HG, P]), c3, ALU.subtract).then_inc(S["kd_d"], 1)
                    if k == 57:
                        dve.wait_ge(S["kd_exp"], f + 1)
                        V.tensor_tensor(lev[1], lev[1], k_s, ALU.mult).then_inc(S["kd_ready"], 1)
                    if k == 63:
                        dve.wait_ge(S["hg_out"], f + 1)
                        settle()
                        for h in range(HG):
                            last = V.scalar_tensor_tensor(state[:, h, :], state[:, h, :], decay[:, h:h + 1],
                                                          F[4][:, P * h:P * (h + 1)], ALU.mult, ALU.add)
                        last.then_inc(S["s_new"], 1)
                if q == 74:
                    dve.wait_ge(S["rms_root"], f + 1)
                    mark(V.reciprocal(ssq4[0:n, :], ssq4[0:n, :]))
                    settle()
                    m3 = mix[0:n, 512:1024].rearrange("p (h d) -> p h d", h=HG)
                    mark(V.tensor_tensor(m3, m3, ssq4[0:n, :].unsqueeze(2).to_broadcast([n, HG, P]), ALU.mult))
                    settle()
                    g_s = s_nat[:, 512:1024].rearrange("p (h d) -> p h d", h=HG) if is_sample(f) else slots(C_G, 4)
                    V.tensor_tensor(m3, m3, g_s, ALU.mult).then_inc(S["mix_ready"], 1)
                if q == 76:
                    dve.wait_ge(S["mix_turned"], f + 1)
                    for j in range(2):
                        last = V.tensor_tensor(mix_t[:, 4 * j:4 * j + 4, 0:n],
                                               F[j][:, 0:4 * n].rearrange("p (c t) -> p c t", c=4),
                                               mix_scale[:, 4 * j:4 * j + 4].unsqueeze(2).to_broadcast([P, 4, n]), ALU.mult)
                    last.then_inc(S["mix_kept"], 1)
                if q == 80:
                    dve.wait_ge(S["h_mm"], 2 * f + 2)
                    dve.wait_ge(S["x_in"], 16 * f + 16)
                    for j in range(2):
                        cols = slice(512 * j, 512 * (j + 1))
                        last = V.tensor_tensor(hx[0:n, cols], F[2 + j][0:n, :], hx[0:n, cols], ALU.add)
                    last.then_inc(S["h_ready"], 1)
                if q == 82:
                    dve.wait_ge(S["ssq_root"], f + 1)
                    dve.wait_ge(S["wffn_in"], 16 * f + 16)
                    mark(V.reciprocal(rstd[0:n, :], rstd[0:n, :]))
                    settle()
                    V.scalar_tensor_tensor(hn[0:n, :], hx[0:n, :], rstd[0:n, :], r3[0:n, :], ALU.mult, ALU.mult)\
                        .then_inc(S["hn_ready"], 1)
                    dve.wait_ge(S["hn_ready"], f + 1)
                for g in range(4):
                    if q == 90 + 3 * g:
                        hold(dve, S["sc_kept"], 4 * f + g + 1, S["held_dve"])
                        top16([sc[0:n, c, :] for c in range(4 * g, 4 * g + 4)], [sv[0:n, c, :] for c in range(4 * g, 4 * g + 4)],
                              [si[0:n, c, :] for c in range(4 * g, 4 * g + 4)])
                if q == 101:
                    settle()
                    sv4 = sv[0:n].rearrange("p (h two) k -> p h two k", two=2)
                    for j in range(2):
                        hs = slice(4 * j, 4 * j + 4)
                        mark(V.tensor_tensor(cand[0:n, hs, :].rearrange("p h (x y) -> p h x y", x=TOPK),
                                             sv4[:, hs, 0, :].unsqueeze(3).to_broadcast([n, 4, TOPK, TOPK]),
                                             sv4[:, hs, 1, :].unsqueeze(2).to_broadcast([n, 4, TOPK, TOPK]), ALU.add))
                    mark(V.tensor_copy(si_f[0:n], si[0:n]))
                    settle()
                for j in range(4):
                    if q == 103 + 2 * j:
                        top16([cand[0:n, h, :] for h in (2 * j, 2 * j + 1)], [fv[0:n, h, :] for h in (2 * j, 2 * j + 1)],
                              [fi[0:n, h, :] for h in (2 * j, 2 * j + 1)])
                if q == 111:
                    settle()
                    fi_x = r3[0:n, 896:1024].bitcast(U32)
                    mark(V.tensor_scalar(pos[0][0:n].bitcast(U32), fi_x, 4, None, ALU.logical_shift_right))
                    mark(V.tensor_scalar(pos[1][0:n].bitcast(U32), fi_x, 15, None, ALU.bitwise_and))
                    V.tensor_tensor(gate_f[0:n, :].rearrange("p (h k) -> p h k", h=PH), fv[0:n],
                                    fv[0:n, :, 0:1].to_broadcast([n, PH, TOPK]), ALU.subtract)\
                        .then_inc(S["gate_d"], 1)
                    settle()
                    for j in range(2):
                        mark(V.tensor_copy(pos[2 + j][0:n], pos[j][0:n].bitcast(U32)))
                    settle()
                for j in range(2):
                    if q == 113 + 2 * j:
                        oh = onehot[0:n]
                        settle()
                        mark(V.tensor_tensor(oh, pos[2 + j][0:n].unsqueeze(2).to_broadcast([n, PICKS, TOPK]),
                                             iota16[0:n].unsqueeze(1).to_broadcast([n, PICKS, TOPK]), ALU.is_equal))
                        settle()
                        si4 = si_f[0:n].rearrange("p (h two) k -> p h two k", two=2)[:, :, j, :]
                        oh4 = oh.rearrange("p (h k) x -> p h k x", h=PH)
                        mark(V.tensor_tensor(oh4, oh4, si4.unsqueeze(2).to_broadcast([n, PH, TOPK, TOPK]), ALU.mult))
                        settle()
                        mark(V.tensor_reduce(pos[j][0:n], oh, AX.X, ALU.add))
                if q == 118:
                    settle()
                    if not first:
                        dve.wait_ge(S["idx_taken"], 2 * f)
                    dve.wait_ge(S["gate_exp"], f + 1)
                    g3 = gate_f[0:n].rearrange("p (h k) -> p h k", h=PH)
                    mark(V.tensor_reduce(gsum[0:n], fv[0:n], AX.X, ALU.add))
                    settle()
                    mark(V.reciprocal(gsum[0:n], gsum[0:n]))
                    settle()
                    if not is_sample(f):
                        mark(V.scalar_tensor_tensor(idx_f[:, :], pos[0], float(P), pos[1], ALU.mult, ALU.add))
                        V.tensor_tensor(g3, fv[:], gsum.unsqueeze(2).to_broadcast([P, PH, TOPK]), ALU.mult)\
                            .then_inc(S["topk_done"], 1)
                        mark(V.memset(rmax[:, 0:1], 0.0))
                        settle()
                    else:
                        for g in range(SGRP):
                            cols, part = slice(NS * g, NS * (g + 1)), slice(NS * g, NS * (g + 1))
                            V.scalar_tensor_tensor(idx_f[part, 0:NS], pos[0][0:NS, cols], float(P), pos[1][0:NS, cols],
                                                   ALU.mult, ALU.add)
                            hs = slice(2 * g, 2 * g + 2)
                            last = V.tensor_tensor(gate_f[part, 0:NS].rearrange("p (h k) -> p h k", h=2), fv[0:NS, hs, :],
                                                   gsum[0:NS, hs].unsqueeze(2).to_broadcast([NS, 2, TOPK]), ALU.mult)
                        last.then_inc(S["topk_done"], 1)
                        dve.wait_ge(S["topk_done"], f + 1)

            def top16(values, best, places):
                for x, b in zip(values, best):
                    mark(V.max(b[:, 0:8], x))
                own.settle_held(S["held_dve"])
                for x, b, i in zip(values, best, places):
                    mark(V.max_index(i[:, 0:8], b[:, 0:8], x))
                    mark(V.match_replace(x, b[:, 0:8], x, LOWEST))
                own.settle_held(S["held_dve"])
                for x, b in zip(values, best):
                    mark(V.max(b[:, 8:16], x))
                own.settle_held(S["held_dve"])
                for x, b, i in zip(values, best, places):
                    mark(V.max_index(i[:, 8:16], b[:, 8:16], x))

            def sample_front(k, f):
                q_s, k_s = slots(C_QH, 4, spj).rearrange(flat), slots(C_F, 4, spj).rearrange(flat)
                if k == 2:
                    for g in range(KV):
                        V.tensor_tensor(s_tab[:, P * g:P * (g + 1)].rearrange("p (h b t) -> p h b t", h=GRP, b=DEC_B),
                                        tab_rep[:, GRP * g:GRP * (g + 1)].unsqueeze(2).unsqueeze(3).to_broadcast([P, GRP, DEC_B, DEC_T]),
                                        tsel.unsqueeze(1).unsqueeze(1).to_broadcast([P, GRP, DEC_B, DEC_T]), ALU.mult)\
                            .then_inc(S["s_tab_ready"], 1)
                for kv in range(KV):
                    if k == 12 + 14 * kv:
                        dve.wait_ge(S["scores"], 2 * f + kv + 1)
                        dve.wait_ge(S["s_bias_kept"], 1)
                        dve.wait_ge(S["caches_in"], 64)
                        if kv:
                            dve.wait_ge(S["p_turned"], 2 * f + 1)
                        for b, (x, y) in enumerate(((0, 512), (512, 1024), (1024, 1024 + NS))):
                            mark(V.scalar_tensor_tensor(s_probs[:, x:y], F[b][:, 0:y - x], SCALE, s_mask[:, x:y], ALU.mult, ALU.add))
                        settle()
                        old = s_probs[:, 0:D].rearrange("p (b j) -> p b j", b=DEC_B)
                        new = s_probs[:, D:D + NS].rearrange("p (b j) -> p b j", b=DEC_B)
                        mark(V.tensor_tensor(old, old, s_bias[:, kv:kv + 1, 0:P].to_broadcast([P, DEC_B, P]), ALU.add))
                        mark(V.tensor_tensor(new, new, s_bias[:, kv:kv + 1, P:P + DEC_T].to_broadcast([P, DEC_B, DEC_T]), ALU.add))
                        settle()
                        mark(V.tensor_reduce(rmax[:, 0:1], s_probs, AX.X, ALU.max))
                        settle()
                        mark(V.tensor_tensor(rmax[:, 0:1], rmax[:, 0:1], sinks_s[:, kv:kv + 1], ALU.max))
                        settle()
                        V.tensor_tensor(esink[:, kv:kv + 1], sinks_s[:, kv:kv + 1], rmax[:, 0:1], ALU.subtract)
                        V.tensor_scalar(nmax[:, kv:kv + 1], rmax[:, 0:1], -1.0, None, ALU.mult).then_inc(S["s_masked"], 1)
                    if k == 22 + 14 * kv:
                        dve.wait_ge(S["pv"], 2 * f + kv + 1)
                        mark(V.tensor_tensor(den[:, kv:kv + 1], den[:, kv:kv + 1], esink[:, kv:kv + 1], ALU.add))
                        settle()
                        mark(V.reciprocal(den[:, kv:kv + 1], den[:, kv:kv + 1]))
                        settle()
                        for j in range(GRP):
                            part, h = slice(NS * j, NS * (j + 1)), GRP * kv + j
                            last = V.tensor_scalar(mix[0:NS, DH * h:DH * (h + 1)], F[2][part, 64:128], den[part, kv:kv + 1],
                                                   None, ALU.mult)
                        last.then_inc(S["mix_attn"], 1)
                if k == 43:
                    dve.wait_ge(S["kept_ig"], f + 1)
                    for h in range(HG):
                        last = V.tensor_scalar(slots(C_F, 4, spj)[:, h, :], slots(C_F, 4, spj)[:, h, :], oml[:, h:h + 1],
                                               lb[:, h:h + 1], ALU.mult, ALU.add)
                    last.then_inc(S["hg_f"], 1)
                    dve.wait_ge(S["hg_out"], f)
                    mark(V.memset(a_t[0:NS, :, 0:NS], 0.0))
                    mark(V.memset(s_reset, 1.0))
                    settle()
                    mark(V.memset(s_reset.rearrange("p (x t) -> p x t", t=DEC_T)[:, :, 0:1], 0.0))
                if k == 45:
                    dve.wait_ge(S["hg_ln"], f + 1)
                    settle()
                    V.tensor_scalar(k_s, k_s, -1.0, 1.0, ALU.mult, ALU.add)
                    V.tensor_tensor_scan(s_cum, s_reset, s_cum, 0.0, ALU.mult, ALU.add).then_inc(S["hg_k"], 1)
                    dve.wait_ge(S["hg_k"], f + 1)
                for l in range(3):
                    if k == 47 + 2 * l and l < 2:
                        level_exponents(l, LEVELS[5 + l], s_cum, s_lev[l])
                    if k == 49 + 2 * l and l < 2:
                        dve.wait_ge(S["lev_e"], (NL - 1) * f + l + 1)
                        level_factors(l, LEVELS[5 + l], s_lev[l], q_s, k_s)
                    if k == 51 + 2 * l:
                        dve.wait_ge(S["lev_mm"], NL * f + l + 1)
                        if l:
                            dve.wait_ge(S["lev_kept"], NL * f + l)
                        V.copy_predicated(a_t[0:NS, :, 0:NS], level_masks[0:NS, 5 + l:6 + l, 0:NS].to_broadcast([NS, HG, NS]),
                                          F[0][0:NS, 0:P].rearrange("p (c t) -> p c t", c=4)).then_inc(S["lev_kept"], 1)
                if k == 52:
                    dve.wait_ge(S["qe_exp"], f + 1)
                    mark(V.tensor_copy(s_dec, s_qe.rearrange("p (x t) -> p x t", t=DEC_T)[:, :, last_pos]))
                    settle()
                    V.tensor_tensor(s_qe, s_qe, q_s, ALU.mult).then_inc(S["qe_ready"], 1)
                    dve.wait_ge(S["lev_mm"], NL * f + 1)
                    c3 = s_cum.rearrange("p (x t) -> p x t", t=DEC_T)
                    V.tensor_tensor(s_lev[0].rearrange("p (x t) -> p x t", t=DEC_T),
                                    c3[:, :, last_pos:DEC_T].to_broadcast([P, HG * DEC_B, DEC_T]), c3, ALU.subtract)\
                        .then_inc(S["kd_d"], 1)
                if k == 56:
                    dve.wait_ge(S["kd_exp"], f + 1)
                    V.tensor_tensor(s_lev[0], s_lev[0], k_s, ALU.mult).then_inc(S["kd_ready"], 1)
                for b in range(DEC_B):
                    if k == 59 + b:
                        dve.wait_ge(S["kd_kept"], f + 1)
                        if b >= 2:
                            dve.wait_ge(S["st_mm"], b - 1)
                        V.tensor_scalar(s_kdm[b % 2], s_kdn, bsel[0:NS, b:b + 1], None, ALU.mult).then_inc(S["kdm_ready"], 1)
                    if k == 61 + b:
                        dve.wait_ge(S["st_mm"], b + 1)
                        settle()
                        for h in range(HG):
                            cols = slice(P * h, P * (h + 1))
                            last = V.scalar_tensor_tensor(s_st[b % 2][:, cols], s_st[b % 2][:, cols],
                                                          s_dec[:, DEC_B * h + b:DEC_B * h + b + 1], F[b % 2][:, cols],
                                                          ALU.mult, ALU.add)
                        last.then_inc(S["st_new"], 1)
                if k == 72:
                    dve.wait_ge(S["o_kept"], 1)
                    V.tensor_tensor(mix[0:NS, 512:1024], mix[0:NS, 512:1024], F[3][0:NS, :], ALU.add).then_inc(S["o_kept"], 1)

            def body(p):
                w, v, u, f = parts(p)
                for k in range(PICKS):
                    if u is not None and k < steps_of(u):
                        dve.wait_ge(u_row[k % U_RING], 16 * (PICKS // U_RING) * u + 16 * (k // U_RING + 1))
                        V.tensor_tensor_reduce(u_rows[:, k % U_RING, :], u_rows[:, k % U_RING, :], hn_u[:, :], 1.0, 0.0,
                                               ALU.mult, ALU.add, act_u[:, k:k + 1]).then_inc(S["dots"], 1)
                    if w is not None:
                        finish(k, w)
                    if f is not None:
                        front(k, f)
                if f is not None:
                    if u is not None:
                        dve.wait_ge(S["dots"], PICKS * u + steps_of(u))
                    if is_sample(f):
                        for g in range(SGRP):
                            mark(V.tensor_copy(hn_u[NS * g:NS * (g + 1), :], hn[0:NS, :]))
                    else:
                        V.tensor_copy(hn_u[:, :], hn[:, :]).then_inc(S["hn_taken"], 1)
                if u is not None:
                    n = steps_of(u)
                    dve.wait_ge(S["act_ready"], u + 1)
                    if v is not None:
                        dve.wait_ge(S["diag_ready"], PICKS * v + steps_of(v))
                    V.tensor_tensor(w_v[:, 0:n], act_u[:, 0:n], gate_u[:, 0:n], ALU.mult).then_inc(S["wv_ready"], 1)
                    dve.wait_ge(S["wv_ready"], u + 1)
                if f is not None:
                    n = NS if is_sample(f) else PICKS
                    mark(V.tensor_copy(gate_u[:, 0:n], gate_f[:, 0:n]))
                    settle()
                    if not is_sample(f):
                        dve.wait_ge(S["hn_taken"], f + 1)

            def finish(k, w):
                m = ntok(w)
                if k == 1:
                    dve.wait_ge(S["vsum"], summed(PICKS * w + steps_of(w)))
                    dve.wait_ge(S["h_back"], 16 * w + 16)
                    for j in range(2):
                        cols = slice(512 * j, 512 * (j + 1))
                        last = V.tensor_tensor(hx[0:m, cols], Y[j][0:m, :], hx[0:m, cols], ALU.add)
                    last.then_inc(S["y_taken"], 1)
                if k == 3:
                    dve.wait_ge(S["y_root"], w + 1)
                    dve.wait_ge(S["wfin_in"], 16 * w + 16)
                    mark(V.reciprocal(rstd_y[0:m, :], rstd_y[0:m, :]))
                    settle()
                    V.scalar_tensor_tensor(hx[0:m, :], hx[0:m, :], rstd_y[0:m, :], r3[0:m, :], ALU.mult, ALU.mult)\
                        .then_inc(S["y_ready"], 1)

            periods(dve, own, body)



def bucket(dist):
    exact = BUCKETS // 2
    n = np.maximum(dist, 0)
    nf = np.maximum(n, 1).astype(np.float32)
    step = np.log(nf / np.float32(exact)) / np.float32(np.log(WINDOW / exact)) * np.float32(BUCKETS - exact)
    return np.where(n < exact, n, np.minimum(exact + step.astype(np.int32), BUCKETS - 1))


def constants():
    dist = 2 * P - 1 - np.arange(SKEW)
    valid = (dist >= 0) & (dist <= WINDOW)
    bucket_of = np.zeros((BUCKETS + 1, SKEW), np.float32)
    bucket_of[np.where(valid, bucket(dist), BUCKETS), np.arange(SKEW)] = 1.0
    s, t = np.arange(P)[:, None], np.arange(P)[None, :]
    masks = np.zeros((P, NL, P), np.float32)
    for l, m in enumerate(LEVELS):
        masks[:, l] = (s // (2 * m) == t // (2 * m)) & (s % (2 * m) < m) & (t % (2 * m) >= m)
    masks[:, NL - 1] = s == t
    d_s = (WINDOW + np.arange(DEC_T))[:, None] - np.arange(WINDOW + DEC_T)[None, :]
    ok = (d_s >= 0) & (d_s <= WINDOW)
    onehot = (bucket(d_s)[:, None, :] == np.arange(BUCKETS)[None, :, None]) & ok[:, None, :]
    same = np.arange(DEC_B)[:, None] == np.arange(DEC_B)[None, :]
    allowed = same[:, None, :, None] & ok[None, :, None, :]
    flat = np.concatenate([allowed[..., :WINDOW].reshape(NS, -1), allowed[..., WINDOW:].reshape(NS, -1)], axis=1)
    p = np.arange(P)
    return {
        "ident": np.eye(P, dtype=np.float32),
        "bucket_of": bucket_of,
        "level_masks": masks.reshape(P, NL * P),
        "iota16": np.tile(np.arange(TOPK, dtype=np.float32), (P, 1)),
        "tsel": (p[:, None] // BUCKETS == np.arange(DEC_T)[None]).astype(np.float32),
        "bsel": (p[:, None] // DEC_T == np.arange(DEC_B)[None]).astype(np.float32),
        "fold": (p[:, None] % NS == np.arange(NS)[None]).astype(np.float32),
        "s_onehot": onehot.reshape(DEC_T * BUCKETS, -1).astype(np.float32),
        "s_mask": np.tile(np.where(flat, 0.0, NEG).astype(np.float32), (GRP, 1)),
    }


def layout(i):
    w_in = i["w_in"][0]
    aw = HEADS * DH
    q = w_in[:, :aw].reshape(D, KV, GRP, DH).transpose(0, 2, 1, 3).reshape(D, aw)
    w_in = np.concatenate([q, w_in[:, aw:]], axis=1)
    sinks = i["attn_sinks"][0]
    return {
        "x_prompt": i["x_prompt"][0],
        "x_sample": i["x_sample"].reshape(NS, D),
        "w_in": w_in.reshape(DC, P, CHUNKS, P).transpose(2, 1, 0, 3),
        "w_o": i["w_o"][0],
        "w_q_t": i["peer_w_q"][0].T,
        "keys_t": i["peer_sub_keys"][0].reshape(2 * PH, P, P).transpose(2, 0, 1),
        "peer_u": i["peer_u"][0],
        "peer_v": i["peer_v"][0],
        "norm_mix_t": i["norm_mix_w"][0].reshape(DC, P).T,
        "hg_norm_t": i["hg_norm_w"][0].reshape(HG, P).T,
        "hg_lb_t": i["hg_lb"].reshape(2 * HG, P).T,
        "norm_ffn": np.tile(i["norm_ffn_w"], (P, 1)),
        "norm_final": np.tile(i["norm_final_w"], (P, 1)),
        "sinks": np.tile(sinks, (P, 1)),
        "sinks_s": np.repeat(sinks.reshape(KV, GRP).T, NS, axis=0),
        "table": np.repeat(i["rel_bias_table"][:, :, None], P, axis=2),
        "table_rep": np.tile(i["rel_bias_table"], (DEC_T, 1)),
        "cache_k": i["cache_k_win"][0].reshape(DEC_B, WINDOW, P),
        "cache_v": i["cache_v_win"][0].reshape(DEC_B, WINDOW, P),
        "cache_k_t": i["cache_k_win"][0].reshape(DEC_B, WINDOW, P).transpose(0, 2, 1),
        "state_in": i["state_hgrn"][0].transpose(0, 2, 1, 3),
    }


OUTS = {"y_prompt": (SEQ, D), "y_sample": (NS, D), "k_win_prompt": (WINDOW, P), "v_win_prompt": (WINDOW, P),
        "state_prompt": (P, HG, P), "k_win_sample": (DEC_B, WINDOW, P), "v_win_sample": (DEC_B, WINDOW, P),
        "state_out": (DEC_B, P, HG * P)}


def kernel(**inputs):
    import concourse.bacc as _bacc
    from concourse.bass_utils import run_bass_kernel_spmd as _run

    nc = _bacc.Bacc("TRN2", target_bir_lowering=False, num_devices=1)
    given = {k: np.asarray(v) for k, v in inputs.items()}
    arrays, aps = {}, {}
    for name, array in (layout(given) | constants()).items():
        array = np.ascontiguousarray(array)
        arrays[f"in_{name}"] = array
        aps[name] = nc.dram_tensor(f"in_{name}", array.shape, mybir.dt.from_np(array.dtype), kind="ExternalInput").ap()
    for name, shape in OUTS.items():
        aps[name] = nc.dram_tensor(f"out_{name}", shape, F32, kind="ExternalOutput").ap()
    build(nc, aps)
    r = _run(nc, [arrays], core_ids=[0]).results[0]
    o = {name: r[f"out_{name}"] for name in OUTS}
    win = (1, -1, WINDOW, KV, DH)
    return (o["y_prompt"].reshape(1, SEQ, D), o["y_sample"].reshape(DEC_B, DEC_T, D),
            o["k_win_prompt"].reshape(win), o["v_win_prompt"].reshape(win),
            np.ascontiguousarray(o["state_prompt"].transpose(1, 0, 2)).reshape(1, 1, HG, P, P),
            o["k_win_sample"].reshape(win), o["v_win_sample"].reshape(win),
            np.ascontiguousarray(o["state_out"].reshape(DEC_B, P, HG, P).transpose(0, 2, 1, 3)).reshape(1, DEC_B, HG, P, P))
```

```python
from contextlib import ExitStack

import numpy as np
import concourse.bass as bass
from concourse import mybir

F32 = mybir.dt.float32
I32 = mybir.dt.int32
U32 = mybir.dt.uint32
U8 = mybir.dt.uint8
ALU = mybir.AluOpType
ACT = mybir.ActivationFunctionType
AX = mybir.AxisListType

P = 128
D = 1024
DC = D // P
SEQ, DEC_B, DEC_T = 1024, 8, 4
NS = DEC_B * DEC_T
TILES = SEQ // P
TOK = SEQ + NS
HEADS, KV, DH = 8, 2, 64
GRP = HEADS // KV
SCALE = DH ** -0.5
HG = 4
BUCKETS, WINDOW = 32, 128
NEG = -1.0e30
CHUNKS = 22
C_Q, C_K, C_V, C_QH, C_F, C_I, C_G = 0, 4, 5, 6, 10, 14, 18
PH, TOPK = 8, 16
PICKS = PH * TOPK
SIDE = 256
LEVELS = [64, 32, 16, 8, 4, 2, 1]
NL = len(LEVELS) + 1
LOWEST = -3.0e38
EPS = 1e-6
U_RING, V_RING = 8, 4
V_LAG = 3
SGRP = P // NS
S_OFF = (C_G + 4 - 1) * NS
PASS1 = 2 * P
PASS2 = 4 * P
PASS3 = SEQ - PASS1 - PASS2
BLOCKS_AT = {-2: (2, 5), -1: (38, 4)}
SKEW = 3 * P
ORDER = [0, 1, TILES, 2, 3, 4, 5, 6, 7]
FIRST = 3
OUT_1, OUT_2 = 32 * (CHUNKS // 2), 48 * (CHUNKS // 2)
LOOP = (1, TILES - 2)
SKIP = 18
SKIP_S, SKIP_M = 14, 14
HEAD = 104
HEAD_AT, TAIL_AT = 121, 12
DVE_PER, ACT_PER = 153, 14


def steps_of(tile):
    return PICKS // SGRP if isinstance(tile, int) and tile == TILES else PICKS


def block_at(p, k):
    if not isinstance(p, int) or p >= 0:
        return None
    first, every = BLOCKS_AT[p]
    b, rest = divmod(k - first, every)
    return b if rest == 0 and 0 <= b < CHUNKS else None


def side_sum(v, k):
    return isinstance(v, int) and v == TILES - 1 and k >= NS


def hold(eng, semaphore, value, held):
    eng.wait_ge(semaphore, value)
    if not isinstance(value, int):
        eng.sem_inc(held, 1)


def summed(n):
    return n + 2


class Own:

    def __init__(self, eng, semaphore, per_turn):
        self.eng, self.semaphore, self.per_turn = eng, semaphore, per_turn
        self.count, self.turn, self.at_start = 0, None, 0

    def mark(self, instruction):
        self.count += 1
        instruction.then_inc(self.semaphore, 1)

    def settle(self):
        value = self.count
        if self.turn is not None:
            value = self.turn * self.per_turn + (self.count - LOOP[0] * self.per_turn)
        self.eng.wait_ge(self.semaphore, value)

    def settle_held(self, held):
        self.settle()
        if self.turn is not None:
            self.eng.sem_inc(held, 1)

    def begin(self, turn):
        self.turn, self.at_start = turn, self.count

    def end(self, first, last):
        assert self.count - self.at_start == self.per_turn, (self.semaphore, self.count - self.at_start)
        self.count = self.at_start + (last - first) * self.per_turn
        self.turn = None


def build(nc, a):
    proj = nc.dram_tensor("proj", (CHUNKS, P, SEQ), F32, kind="Internal").ap()
    skewed = nc.dram_tensor("skewed", (HEADS * P * SKEW,), F32, kind="Internal").ap()
    proj_s = nc.dram_tensor("proj_s", (P, CHUNKS, NS), F32, kind="Internal").ap()
    h_dram = nc.dram_tensor("h_dram", (TOK, D), F32, kind="Internal").ap()

    ctx = ExitStack()
    with ctx:
        def sb(name, shape, dt=F32):
            return ctx.enter_context(nc.sbuf_tensor(name, shape, dt))

        def sem(name):
            return ctx.enter_context(nc.semaphore(name))

        w_o = sb("w_o", [P, DC, D])
        w_sc = sb("w_sc", [P, 2 * PH, D])
        keys = sb("keys", [P, 2 * PH, P])
        rows = sb("rows", [P, (U_RING + V_RING) * D])
        hn_u = sb("hn_u", [P, D])
        hn = sb("hn", [P, D])
        hx = sb("hx", [P, D])
        bias = sb("bias", [P, HEADS * 2 * P])
        r1 = sb("r1", [P, (CHUNKS - 1) * P])
        r2 = sb("r2", [P, 2 * D])
        r3 = sb("r3", [P, D])
        state = sb("state", [P, HG, P])
        a_t = sb("a_t", [P, HG, P])
        diag = sb("diag", [P, 2, P])
        ident = sb("ident", [P, P])
        level_masks = sb("level_masks", [P, NL, P], U8)
        k_t = sb("k_t", [P, 2, P])
        v_n = sb("v_n", [P, 2, P])
        gate_f, gate_u, act_u, w_v = (sb(n, [P, PICKS]) for n in ("gate_f", "gate_u", "act_u", "w_v"))
        idx_f, idx_u, idx_v = (sb(n, [P, PICKS], I32) for n in ("idx_f", "idx_u", "idx_v"))
        small = sb("small", [P, 192])
        ps = ctx.enter_context(nc.psum_tensor("ps", [P, 8, 512], F32))
        Y = [ps[:, 0, :], ps[:, 1, :]]
        F = [ps[:, 2 + n, :] for n in range(6)]

        taken = [0]

        def vec(n):
            taken[0] += n
            return small[:, taken[0] - n:taken[0]]

        eps, one = vec(1), vec(1)
        w_mix = vec(DC)
        mix_scale = vec(DC)
        lb_in, lb, oml = vec(2 * HG), vec(HG), vec(HG)
        sinks, sinks_s = vec(HEADS), vec(KV)
        rmax, nmax, den, esink = vec(GRP), vec(HEADS), vec(HEADS), vec(HEADS)
        decay, ssq4 = vec(HG), vec(HG)
        ssq, rstd = vec(1), vec(1)
        ssq_y, rstd_y = vec(1), vec(1)
        gsum, iota16 = vec(PH), vec(TOPK)
        tsel, tab_rep, bsel = vec(DEC_T), vec(HEADS), vec(DEC_B)
        fold = vec(NS)
        assert taken[0] <= 192

        names = """consts_in w_o_in w_q_in x_a0 x_a1 a_root a_scaled a_turned a_kept w_a0 w_a1 w_a2 w_a3 w_b0 w_b1
            keys_in m_mm m_kept bias_mm bias_kept bias_out bias_in wp_done kept proj_out0 proj_out1 block3 kept3 proj_out3 table_in
            x_in proj_in norms_in kv_shifted turned kept_ig v_kept
            scores s_masked p_ready p_turned p_kept pv mix_attn
            hg_f hg_ln hg_k lev_d lev_e lev_q lev_mm lev_kept
            qe_exp qe_ready kd_d kd_exp kd_ready kd_turned kd_kept hg_out s_new rms_root mix_ready
            mix_turned mix_kept h_mm h_ready h_stored ssq_root hn_ready hn_turned hn_kept hn_taken
            sc_mm sc_kept gate_d gate_exp topk_done idx_taken
            h_back y_taken y_root y_ready y_out
            dots act_ready wv_ready diag_ready vsum side_added
            own_dve own_act held_sp held_pool held_dve u_written v_written idx_moved
            caches_in out_kv k7_turned k7_kept set_up lb_shifted lb_exp s_turned s_tab_ready s_bias_mm s_bias_kept
            st_in0 st_in1 st_in2 st_out0 st_out1 st_out2 kdm_ready st_mm st_new ot_kept ot_turned o_kept""".split()
        S = {n: sem(n) for n in names}
        u_row = [sem(f"u_row{n}") for n in range(U_RING)]
        v_row = [sem(f"v_row{n}") for n in range(V_RING)]

        u_rows = rows[:, 0:U_RING * D].rearrange("p (r d) -> p r d", d=D)
        v_rows = rows[:, U_RING * D:].rearrange("p (r d) -> p r d", d=D)
        pj = r1[:, :].rearrange("p (c t) -> p c t", t=P)
        spj = r1[:, 0:S_OFF].rearrange("p (c t) -> p c t", t=NS)

        def slots(c, n, view=pj):
            c = c if c < C_K else c - 1
            return view[:, c:c + n, :]

        bias_v = bias[:, :].rearrange("p (h s) -> p h s", h=HEADS)
        probs = r2[:, 0:D].rearrange("p (h s) -> p h s", h=GRP)
        probs_t = r2[:, D:2 * D].rearrange("p (h b t) -> p h b t", h=GRP, b=2)
        lev = [r2[:, 0:512], r2[:, 512:1024]]
        kd_n, cum = r2[:, 1024:1536], r2[:, 1536:2048]
        mix = r3
        mix_t = r2[:, 0:D].rearrange("p (c t) -> p c t", c=DC)
        hn_t = r2[:, D:2 * D].rearrange("p (c t) -> p c t", c=DC)
        sc = r1[:, 0:2 * D].rearrange("p (c n) -> p c n", c=2 * PH)
        cand = r2[:, :].rearrange("p (h x) -> p h x", h=PH)
        sv = r3[:, 0:256].rearrange("p (c k) -> p c k", c=2 * PH)
        si = r3[:, 256:512].bitcast(U32).rearrange("p (c k) -> p c k", c=2 * PH)
        si_f = r3[:, 512:768].rearrange("p (c k) -> p c k", c=2 * PH)
        fv = r3[:, 768:896].rearrange("p (h k) -> p h k", h=PH)
        fi = r3[:, 896:1024].bitcast(U32).rearrange("p (h k) -> p h k", h=PH)
        onehot = r1[:, 0:2 * D].rearrange("p (x k) -> p x k", k=TOPK)
        pos = [r1[:, 2048 + n * PICKS:2048 + (n + 1) * PICKS] for n in range(4)]

        x_a = [r1[:, 0:D], r1[:, D:2 * D]]
        xn_t = rows[:, 0:DC * (PASS1 + NS + PASS2)].rearrange("p (c t) -> p c t", c=DC)
        staged = [rows[:, DC * (PASS1 + NS + PASS2) + n * PASS2:DC * (PASS1 + NS + PASS2) + (n + 1) * PASS2] for n in range(2)]
        last = U_RING * D
        xn_t3 = rows[:, last:last + DC * PASS3].rearrange("p (c t) -> p c t", c=DC)
        wp = [rows[:, last + DC * PASS3 + n * D:last + DC * PASS3 + (n + 1) * D].rearrange("p (c n) -> p c n", c=DC)
              for n in range(2)]
        w_first = wp + [w_o[:, n, :].rearrange("p (c n) -> p c n", c=DC) for n in range(2)]
        staged3 = diag[:, :, :].rearrange("p a b -> p (a b)")
        column = {0: 0, 1: P, TILES: 2 * P} | {i: i * P + NS for i in range(2, TILES - 2)}
        table = hn[0:BUCKETS + 1, :].rearrange("p (h q) -> p h q", h=HEADS)
        bucket_of = hx[0:BUCKETS + 1, 0:SKEW]
        replicated = [r2[:, 0:4 * SKEW], bias[:, 0:4 * SKEW]]

        w_ffn = keys[:, 0:PH, :].rearrange("p c n -> p (c n)")
        w_fin = keys[:, PH:2 * PH, :].rearrange("p c n -> p (c n)")

        kc_t = bias[:, 0:D]
        vc = bias[:, D:2 * D].rearrange("p (b x) -> p b x", b=DEC_B)
        s_probs = r2[:, 0:D + NS]
        s_probs_t = [r2[:, D + NS + c * P:D + NS + (c + 1) * P] if c < 7 else
                     hn[:, 660 + (c - 7) * P:660 + (c - 6) * P] for c in range(9)]
        s_mask = r1[:, S_OFF:S_OFF + D + NS]
        s_bias = hn[:, 0:264].rearrange("p (g j) -> p g j", g=KV)
        s_oh = hn[:, 264:396]
        s_tab = hn[:, 396:652]
        s_nat = r1[0:NS, S_OFF:S_OFF + D]
        s_st = [bias[:, 0:512], bias[:, 512:1024], r2[:, 1536:2048]]
        s_cum, s_reset = bias[:, 1024:1152], bias[:, 1152:1280]
        s_lev = [bias[:, 1280:1408], bias[:, 1408:1536]]
        s_qe, s_dec, s_ot = bias[:, 1536:1664], bias[:, 1664:1696], bias[:, 1696:1824]
        s_kdn, s_kdm = r2[0:NS, 1024:1536], [r2[0:NS, 0:512], r2[0:NS, 512:1024]]

        x_tiles = a["x_prompt"].rearrange("(i p) d -> i p d", p=P)
        proj_tiles = proj.rearrange("c p (i t) -> i p c t", t=P)
        h_tiles = h_dram[0:SEQ, :].rearrange("(i p) d -> i p d", p=P)
        y_tiles = a["y_prompt"].rearrange("(i p) d -> i p d", p=P)

        def ntok(f):
            return NS if isinstance(f, int) and f == TILES else P

        def is_sample(f):
            return isinstance(f, int) and f == TILES

        def periods(eng, own, body):
            for q in range(-2, LOOP[0]):
                body(q)
            with eng.Fori(*LOOP) as p:
                if own:
                    own.begin(p)
                body(p)
                if own:
                    own.end(*LOOP)
            for q in range(LOOP[1], TILES + 2):
                body(q)

        def parts(p):
            if isinstance(p, int):
                return [t if 0 <= t <= TILES else None for t in range(p - 1, p + 3)]
            return p - 1, p, p + 1, p + 2

        block = ctx.enter_context(nc.Block())

        @block.sync
        def _(sp):
            def token_tile(n):
                i = ORDER[n]
                if n >= 2:
                    sp.wait_ge(S["a_turned"], n - 1)
                sp.dma_start(x_a[n % 2][0:ntok(i), :], x_tiles[i] if i < TILES else a["x_sample"])\
                  .then_inc(S[f"x_a{n % 2}"], 16)

            token_tile(0)
            for dst, src in ((ident[:, :], "ident"), (w_mix, "norm_mix_t"), (mix_scale[:, 4:8], "hg_norm_t"),
                             (lb_in, "hg_lb_t"), (sinks, "sinks"), (sinks_s, "sinks_s"), (iota16, "iota16"),
                             (tsel, "tsel"), (tab_rep, "table_rep"), (bsel, "bsel"), (fold, "fold")):
                sp.dma_start(dst, a[src]).then_inc(S["consts_in"], 16)
            sp.dma_start(hn_u[:, :], a["level_masks"]).then_inc(S["consts_in"], 16)
            token_tile(1)
            w_q_t = a["w_q_t"].rearrange("(c p) d -> p c d", p=P)
            token_tile(2)
            sp.dma_start(table[0:BUCKETS, :, :], a["table"]).then_inc(S["table_in"], 16)
            sp.dma_start(bucket_of, a["bucket_of"]).then_inc(S["table_in"], 16)
            for half in range(2):
                sp.wait_ge(S["bias_kept"], half + 1)
                sp.dma_start(skewed.rearrange("(h q s) -> q h s", h=HEADS, q=P)[:, 4 * half:4 * half + 4, :],
                             replicated[half].rearrange("p (h s) -> p h s", h=4)).then_inc(S["bias_out"], 16)
            for n in range(FIRST, TILES + 1):
                token_tile(n)
            for part in range(8):
                sp.wait_ge(S["wp_done"], 5 + 2 * part)
                cs = slice(2 * part, 2 * part + 2)
                sp.dma_start(w_sc[:, cs, :], w_q_t[:, cs, :]).then_inc(S["w_q_in"], 16)
                if part == 1:
                    sp.dma_start(keys[:, :, :], a["keys_t"]).then_inc(S["keys_in"], 16)
            sp.wait_ge(S["wp_done"], CHUNKS)
            sp.dma_start(w_o[:, :, :], a["w_o"].rearrange("(c p) n -> p c n", p=P)).then_inc(S["w_o_in"], 16)
            sp.wait_ge(S["bias_out"], 32)
            for h in range(HEADS):
                one_head = skewed[h * P * SKEW + P - 1:h * P * SKEW + P - 1 + P * (SKEW - 1)]
                sp.dma_start(bias_v[:, h, :], one_head.rearrange("(q s) -> q s", q=P)[:, 0:2 * P])\
                  .then_inc(S["bias_in"], 16)
            sp.wait_ge(S["m_mm"], 2 * PH)
            sp.dma_start(w_ffn, a["norm_ffn"]).then_inc(S["norms_in"], 16)
            sp.dma_start(w_fin, a["norm_final"]).then_inc(S["norms_in"], 16)
            for j in range(2):
                sp.wait_ge(S[f"proj_out{j}"], OUT_1)
            sp.wait_ge(S["a_turned"], TILES + 1)

            def finish(w):
                if w is not None:
                    hold(sp, S["y_ready"], w + 1, S["held_sp"])
                    sp.dma_start(a["y_sample"] if is_sample(w) else y_tiles[w], hx[0:ntok(w), :]).then_inc(S["y_out"], 16)
                    hold(sp, S["y_out"], 16 * w + 16, S["held_sp"])

            def body(p):
                w, v, u, f = parts(p)
                if f is not None:
                    sample = is_sample(f)
                    first = isinstance(f, int) and f == 0
                    n = ntok(f)
                    if not first:
                        hold(sp, S["topk_done"], f, S["held_sp"])
                    if isinstance(p, int) and p == 0:
                        for j in range(2):
                            sp.wait_ge(S[f"proj_out{j}"], OUT_2)
                        sp.wait_ge(S["proj_out3"], 16 * CHUNKS)
                    if sample:
                        finish(w)
                        sp.dma_start(a["v_win_prompt"], v_n[:, 1, :]).then_inc(S["out_kv"], 16)
                        sp.dma_start(a["state_prompt"], state[:, :, :]).then_inc(S["out_kv"], 16)
                        sp.wait_ge(S["k7_kept"], 1)
                        sp.dma_start(a["k_win_prompt"], r3[:, 896:1024]).then_inc(S["out_kv"], 16)
                        for out_name, in_name in (("k_win_sample", "cache_k"), ("v_win_sample", "cache_v")):
                            sp.dma_start(a[out_name][:, 0:WINDOW - DEC_T, :], a[in_name][:, DEC_T:WINDOW, :])\
                              .then_inc(S["out_kv"], 16)
                        sp.dma_start(kc_t.rearrange("p (b j) -> p b j", b=DEC_B), a["cache_k_t"].rearrange("b p j -> p b j"))\
                          .then_inc(S["caches_in"], 16)
                        sp.dma_start(vc, a["cache_v"].rearrange("b j x -> j b x")).then_inc(S["caches_in"], 16)
                        sp.dma_start(s_mask, a["s_mask"]).then_inc(S["caches_in"], 16)
                        sp.wait_ge(S["hn_taken"], TILES)
                        sp.dma_start(s_oh, a["s_onehot"]).then_inc(S["caches_in"], 16)
                        sp.dma_start(k_t[:, 1, 0:NS], proj_s[:, C_K, :]).then_inc(S["proj_in"], 16)
                        sp.dma_start(spj[:, 0:C_K, :], proj_s[:, 0:C_K, :]).then_inc(S["proj_in"], 16)
                        sp.dma_start(spj[:, C_K:, :], proj_s[:, C_V:, :]).then_inc(S["proj_in"], 16)
                    else:
                        if not first:
                            sp.wait_ge(S["kv_shifted"], f + 1)
                        sp.dma_start(k_t[:, 1, :], proj_tiles[f, :, C_K, :]).then_inc(S["proj_in"], 16)
                        sp.dma_start(pj[:, 0:C_K, :], proj_tiles[f, :, 0:C_K, :]).then_inc(S["proj_in"], 16)
                        sp.dma_start(pj[:, C_K:, :], proj_tiles[f, :, C_V:, :]).then_inc(S["proj_in"], 16)
                        finish(w)
                    if first:
                        sp.wait_ge(S["bias_mm"], 2)
                    else:
                        hold(sp, S["hn_ready"], f, S["held_sp"])
                    sp.dma_start(hx[0:n, :], a["x_sample"] if sample else x_tiles[f]).then_inc(S["x_in"], 16)
                    if sample:
                        sp.wait_ge(S["v_kept"], f + 2)
                        for b in range(DEC_B):
                            sp.dma_start(a["k_win_sample"][b, WINDOW - DEC_T:WINDOW, :],
                                         r3[DEC_T * b:DEC_T * (b + 1), 896:1024]).then_inc(S["out_kv"], 16)
                            sp.dma_start(a["v_win_sample"][b, WINDOW - DEC_T:WINDOW, :],
                                         v_n[DEC_T * b:DEC_T * (b + 1), 1, :]).then_inc(S["out_kv"], 16)
                        sp.wait_ge(S["pv"], 2 * f + 2)
                        for b in range(DEC_B):
                            buf = b % 3
                            if b >= 3:
                                sp.wait_ge(S["st_new"], b - 2)
                                sp.dma_start(a["state_out"][b - 3], s_st[buf]).then_inc(S[f"st_out{buf}"], 16)
                                sp.wait_ge(S[f"st_out{buf}"], 16 * (b // 3))
                            sp.dma_start(s_st[buf].rearrange("p (h x) -> p h x", h=HG), a["state_in"][b])\
                              .then_inc(S[f"st_in{buf}"], 16)
                        for b in range(DEC_B - 3, DEC_B):
                            sp.wait_ge(S["st_new"], b + 1)
                            sp.dma_start(a["state_out"][b], s_st[b % 3]).then_inc(S[f"st_out{b % 3}"], 16)
                            sp.wait_ge(S[f"st_out{b % 3}"], 16 * (b // 3 + 1))
                    hold(sp, S["h_ready"], f + 1, S["held_sp"])
                    h_at = h_dram[SEQ:TOK, :] if sample else h_tiles[f]
                    sp.dma_start(h_at, hx[0:n, :]).then_inc(S["h_stored"], 16)
                    sp.wait_ge(S["h_stored"], 16 * f + 16)
                if f is None:
                    finish(w)
                if v is not None:
                    if f is not None:
                        sp.wait_ge(S["hn_ready"], f + 1)
                    nv = ntok(v)
                    sp.dma_start(hx[0:nv, :], h_dram[SEQ:TOK, :] if is_sample(v) else h_tiles[v])\
                      .then_inc(S["h_back"], 16)

            periods(sp, None, body)
            sp.wait_ge(S["y_out"], 16 * (TILES + 1))
            sp.wait_ge(S["out_kv"], 16 * (3 + 2 + 2 * DEC_B))

        @block.gpsimd
        def _(pool):
            def block_io(c, done, buffer, nxt, j, store):
                hold(pool, S["wp_done"], done, S["held_pool"])
                if nxt is not None:
                    nc.gpsimd.dma_start(w_first[buffer], a["w_in"][nxt]).then_inc(S[f"w_a{buffer}"], 16)
                hold(pool, S["kept"], done, S["held_pool"])
                store(c, j)

            def store_1(c, j):
                nc.gpsimd.dma_start(proj[c, :, 0:PASS1], staged[j][:, 0:PASS1]).then_inc(S[f"proj_out{j}"], 16)
                nc.gpsimd.dma_start(proj_s[:, c, :], staged[j][:, PASS1:PASS1 + NS]).then_inc(S[f"proj_out{j}"], 16)

            def store_2(c, j):
                nc.gpsimd.dma_start(proj[c, :, PASS1:PASS1 + PASS2], staged[j]).then_inc(S[f"proj_out{j}"], 16)

            for n in range(4):
                nc.gpsimd.dma_start(w_first[n], a["w_in"][n]).then_inc(S[f"w_a{n}"], 16)
            with pool.Fori(0, CHUNKS // 4 - 1) as it:
                for n in range(4):
                    block_io(4 * it + n, 4 * it + n + 1, n, 4 * it + n + 4, n % 2, store_1)
            for c in range(4 * (CHUNKS // 4 - 1), CHUNKS):
                nxt = c + 4 if c + 4 < CHUNKS else c - (CHUNKS - 2) if c >= CHUNKS - 2 else None
                block_io(c, c + 1, c % 4, nxt, c % 2, store_1)
            with pool.Fori(0, CHUNKS // 2 - 1) as it:
                for j in range(2):
                    block_io(2 * it + j, 2 * it + (CHUNKS + j + 1), j, 2 * it + j + 2, j, store_2)
            for j in range(2):
                c = CHUNKS - 2 + j
                block_io(c, CHUNKS + c + 1, j, j, j, store_2)

            def body(p):
                w, v, u, f = parts(p)
                for k in range(PICKS + V_LAG):
                    if u is not None and k < steps_of(u):
                        if k == 0 and isinstance(p, int) and p == -1:
                            pool.wait_ge(S["proj_out0"], OUT_2)
                            pool.wait_ge(S["proj_out1"], OUT_2)
                        if not (isinstance(p, int) and p == -1 and k < U_RING):
                            hold(pool, S["dots"], PICKS * u + k - U_RING + 1, S["held_pool"])
                        nc.gpsimd.indirect_dma_start(
                            u_rows[:, k % U_RING, :], None, a["peer_u"],
                            bass.IndirectOffsetOnAxis(ap=idx_u[:, k:k + 1], axis=0), engine_sem=S["u_written"])\
                            .then_inc(u_row[k % U_RING], 16)
                    kv = k - V_LAG
                    if v is not None and 0 <= kv < steps_of(v):
                        if isinstance(v, int) and v == 0 and kv == 0:
                            pool.wait_ge(S["kept3"], CHUNKS)
                        if not (isinstance(v, int) and v == 0 and kv < V_RING):
                            hold(pool, S["vsum"], summed(PICKS * v + kv - V_RING + 1), S["held_pool"])
                        if side_sum(v, kv - V_RING):
                            pool.wait_ge(S["side_added"], kv - V_RING - NS + 1)
                        if is_sample(v) and kv < V_RING:
                            pool.wait_ge(S["side_added"], PICKS - NS - V_RING + kv + 1)
                        nc.gpsimd.indirect_dma_start(
                            v_rows[:, kv % V_RING, :], None, a["peer_v"],
                            bass.IndirectOffsetOnAxis(ap=idx_v[:, kv:kv + 1], axis=0), engine_sem=S["v_written"])\
                            .then_inc(v_row[kv % V_RING], 16)
                    if k == HEAD_AT:
                        move(slice(0, HEAD), u, f, 1)
                    if k == TAIL_AT:
                        move(slice(HEAD, PICKS), None if is_sample(v) else v, None if is_sample(u) else u, 2)

            def move(cols, to_v, to_u, part):
                if to_v is not None:
                    if part == 1:
                        hold(pool, S["dots"], PICKS * to_v + min(steps_of(to_v), HEAD), S["held_pool"])
                        if not (isinstance(to_v, int) and to_v == 0):
                            hold(pool, S["vsum"], summed(PICKS * (to_v - 1) + HEAD), S["held_pool"])
                    else:
                        hold(pool, S["dots"], PICKS * to_v + PICKS, S["held_pool"])
                        if not (isinstance(to_v, int) and to_v == 0):
                            hold(pool, S["vsum"], summed(PICKS * to_v), S["held_pool"])
                    nc.gpsimd.tensor_copy(idx_v[:, cols], idx_u[:, cols]).then_inc(S["idx_moved"], 1)
                    hold(pool, S["idx_moved"], 2 * to_v + part, S["held_pool"])
                if to_u is not None:
                    hold(pool, S["topk_done"], to_u + 1, S["held_pool"])
                    nc.gpsimd.tensor_copy(idx_u[:, cols], idx_f[:, cols]).then_inc(S["idx_taken"], 1)
                    hold(pool, S["idx_taken"], 2 * to_u + part, S["held_pool"])

            periods(pool, None, body)

        @block.scalar
        def _(act):
            own = Own(act, S["own_act"], ACT_PER)
            act.wait_ge(S["consts_in"], 16 * 12)

            act.wait_ge(S["set_up"], 1)
            act.wait_ge(S["lb_shifted"], 1)
            nc.scalar.activation(lb_in, lb_in, ACT.Exp).then_inc(S["lb_exp"], 1)
            def root(i):
                n = ntok(ORDER[i])
                act.wait_ge(S[f"x_a{i % 2}"], 16 * (i // 2 + 1))
                if i >= 1:
                    act.wait_ge(S["a_scaled"], i)
                    own.settle()
                own.mark(nc.scalar.activation(r3[0:n, :], x_a[i % 2][0:n, :], ACT.Square, accum_out=ssq[0:n, :]))
                own.settle()
                nc.scalar.activation(rstd[0:n, :], ssq[0:n, :], ACT.Sqrt, bias=eps[0:n, :], scale=1.0 / D)\
                  .then_inc(S["a_root"], 1)
            for i in range(FIRST):
                root(i)
            for half in range(2):
                act.wait_ge(S["bias_mm"], half + 1)
                nc.scalar.activation(replicated[half].rearrange("p (h s) -> p h s", h=4), ps[:, 4:8, 0:SKEW], ACT.Copy)\
                  .then_inc(S["bias_kept"], 1)

            def keep_block(it, j):
                act.wait_ge(S["wp_done"], 2 * it + j + 1)
                if not (isinstance(it, int) and it == 0):
                    act.wait_ge(S[f"proj_out{j}"], 32 * it)
                nc.scalar.activation(staged[j][:, 0:PASS1 + NS], ps[:, 2 + j, 0:PASS1 + NS], ACT.Copy).then_inc(S["kept"], 1)
            for n in range(6):
                root(FIRST + n)
                keep_block(n // 2, n % 2)
            with act.Fori(3, CHUNKS // 2) as it:
                for j in range(2):
                    keep_block(it, j)

            def keep_second(b):
                j = b % 2
                act.wait_ge(S["wp_done"], CHUNKS + b + 1)
                act.wait_ge(S[f"proj_out{j}"], OUT_1 + 16 * (b // 2))
                nc.scalar.activation(staged[j], ps[:, j, :], ACT.Copy).then_inc(S["kept"], 1)

            def keep_third(b):
                act.wait_ge(S["block3"], b + 1)
                if b + 2 < CHUNKS:
                    act.dma_start(wp[b % 2], a["w_in"][b + 2]).then_inc(S[f"w_b{b % 2}"], 16)
                if b:
                    act.wait_ge(S["proj_out3"], 16 * b)
                nc.scalar.activation(staged3, ps[:, b % 2, 0:PASS3], ACT.Copy).then_inc(S["kept3"], 1)
                act.wait_ge(S["kept3"], b + 1)
                act.dma_start(proj[b, :, PASS1 + PASS2:SEQ], staged3).then_inc(S["proj_out3"], 16)

            def exps(f, kv, lo):
                act.wait_ge(S["s_masked"], 2 * f + kv + 1)
                for j in range(GRP):
                    h = GRP * kv + j
                    own.mark(nc.scalar.activation(probs[:, j, lo:2 * P], probs[:, j, lo:2 * P], ACT.Exp,
                                                  bias=nmax[:, h:h + 1], accum_out=den[:, h:h + 1]))
                nc.scalar.activation(esink[:, GRP * kv:GRP * (kv + 1)], esink[:, GRP * kv:GRP * (kv + 1)], ACT.Exp)\
                  .then_inc(S["p_ready"], 1)

            def keep_probs(f, kv, first):
                act.wait_ge(S["p_turned"], 2 * f + kv + 1)
                act.wait_ge(S["pv"], 2 * f + kv)
                for j in range(2):
                    bank = F[(3 if kv == 0 else 0) + j].rearrange("p (h b t) -> p h b t", h=2, b=2)
                    lo = 1 if first else 0
                    last = nc.scalar.activation(probs_t[:, 2 * j:2 * j + 2, lo:2, :], bank[:, :, lo:2, :], ACT.Copy)
                last.then_inc(S["p_kept"], 1)

            def front(k, f):
                q = k + (SKIP_S if is_sample(f) else SKIP)
                first = isinstance(f, int) and f == 0
                n = NS if is_sample(f) else P
                if not is_sample(f):
                    if k == 1 and not first:
                        act.wait_ge(S["pv"], 2 * f)
                        nc.scalar.activation(v_n[:, 0, :], v_n[:, 1, :], ACT.Copy)
                        nc.scalar.activation(k_t[:, 0, :], k_t[:, 1, :], ACT.Copy).then_inc(S["kv_shifted"], 1)
                    if k == 1 and first:
                        nc.scalar.activation(k_t[:, 0, 0:1], eps, ACT.Copy).then_inc(S["kv_shifted"], 1)
                    if k == 6:
                        act.wait_ge(S["turned"], f + 1)
                        act.wait_ge(S["proj_in"], 48 * f + 48)
                        nc.scalar.activation(slots(C_I, 4), F[0].rearrange("p (c t) -> p c t", c=4), ACT.Copy)
                        nc.scalar.activation(slots(C_G, 4), F[1].rearrange("p (c t) -> p c t", c=4), ACT.Silu)
                        nc.scalar.activation(v_n[:, 1, :], F[2][:, 0:P], ACT.Copy).then_inc(S["v_kept"], 1)
                        nc.scalar.activation(slots(C_QH, 4), slots(C_QH, 4), ACT.Silu)
                        nc.scalar.activation(slots(C_F, 4), slots(C_F, 4), ACT.Sigmoid).then_inc(S["kept_ig"], 1)
                    for kv in range(KV):
                        if k == 12 + 7 * kv:
                            exps(f, kv, P if first else 0)
                        if k == 16 + 7 * kv:
                            keep_probs(f, kv, first)
                    if k == 29:
                        act.wait_ge(S["hg_f"], f + 1)
                        act.wait_ge(S["pv"], 2 * f + 2)
                        nc.scalar.activation(cum.rearrange("p (c t) -> p c t", c=4), slots(C_F, 4), ACT.Ln)\
                          .then_inc(S["hg_ln"], 1)
                    for l in range(NL - 1):
                        if k == 33 + 2 * l:
                            act.wait_ge(S["lev_d"], (NL - 1) * f + l + 1)
                            nc.scalar.activation(lev[l % 2], lev[l % 2], ACT.Exp).then_inc(S["lev_e"], 1)
                    if k == 37:
                        act.wait_ge(S["hg_k"], f + 1)
                        nc.scalar.activation(slots(C_Q, 4), cum.rearrange("p (c t) -> p c t", c=4), ACT.Exp)\
                          .then_inc(S["qe_exp"], 1)
                    if k == 48:
                        act.wait_ge(S["kd_d"], f + 1)
                        nc.scalar.activation(lev[1], lev[1], ACT.Exp).then_inc(S["kd_exp"], 1)
                    if k == 51:
                        act.wait_ge(S["kd_turned"], f + 1)
                        nc.scalar.activation(kd_n, F[2], ACT.Copy).then_inc(S["kd_kept"], 1)
                    if k == 55:
                        act.wait_ge(S["hg_out"], f + 1)
                        nc.scalar.activation(mix[:, 512:1024], F[3], ACT.Copy)
                        for h in range(HG):
                            own.mark(nc.scalar.activation(lev[0][:, P * h:P * (h + 1)], F[3][:, P * h:P * (h + 1)],
                                                          ACT.Square, accum_out=ssq4[:, h:h + 1]))
                        own.settle()
                        nc.scalar.activation(ssq4, ssq4, ACT.Sqrt, bias=eps, scale=1.0 / P).then_inc(S["rms_root"], 1)
                else:
                    sample_front(k, f)
                if q == 86:
                    act.wait_ge(S["h_ready"], f + 1)
                    own.mark(nc.scalar.activation(r2[0:n, 0:D], hx[0:n, :], ACT.Square, accum_out=ssq[0:n, :]))
                    own.settle()
                    nc.scalar.activation(rstd[0:n, :], ssq[0:n, :], ACT.Sqrt, bias=eps[0:n, :], scale=1.0 / D)\
                      .then_inc(S["ssq_root"], 1)
                if q == 89:
                    act.wait_ge(S["hn_turned"], f + 1)
                    if is_sample(f):
                        act.wait_ge(S["st_out2"], 16 * 2)
                    for j in range(2):
                        last = nc.scalar.activation(hn_t[:, 4 * j:4 * j + 4, 0:n],
                                                    F[4 + j][:, 0:4 * n].rearrange("p (c t) -> p c t", c=4), ACT.Copy)
                    last.then_inc(S["hn_kept"], 1)
                for g in range(4):
                    if q == 96 + 6 * g:
                        act.wait_ge(S["sc_mm"], 4 * f + g + 1)
                        nc.scalar.activation(sc[0:n, 4 * g:4 * g + 4, :], F[g][0:n, :].rearrange("p (c t) -> p c t", c=4),
                                             ACT.Copy).then_inc(S["sc_kept"], 1)
                if q == 129:
                    act.wait_ge(S["gate_d"], f + 1)
                    nc.scalar.activation(fv[0:n], gate_f[0:n, :].rearrange("p (h k) -> p h k", h=PH), ACT.Exp).then_inc(S["gate_exp"], 1)

            def sample_front(k, f):
                m_step = k + SKIP_M
                if k == 5:
                    act.wait_ge(S["k7_turned"], 1)
                    act.wait_ge(S["y_ready"], f - 2)
                    nc.scalar.activation(r3[:, 896:1024], F[5][:, 0:P], ACT.Copy).then_inc(S["k7_kept"], 1)
                if k == 6:
                    act.wait_ge(S["turned"], f + 1)
                    act.wait_ge(S["out_kv"], 16 * 5)
                    nc.scalar.activation(v_n[0:NS, 1, :], F[2][0:NS, 0:P], ACT.Copy).then_inc(S["v_kept"], 1)
                    nc.scalar.activation(r3[0:NS, 896:1024], F[2][0:NS, P:2 * P], ACT.Copy).then_inc(S["v_kept"], 1)
                if k == 9:
                    act.wait_ge(S["s_bias_mm"], 1)
                    nc.scalar.activation(s_bias, F[5][:, 0:264].rearrange("p (g j) -> p g j", g=KV), ACT.Copy)\
                      .then_inc(S["s_bias_kept"], 1)
                for kv in range(KV):
                    if k == 12 + 7 * kv:
                        act.wait_ge(S["s_masked"], 2 * f + kv + 1)
                        own.mark(nc.scalar.activation(s_probs, s_probs, ACT.Exp, bias=nmax[:, kv:kv + 1],
                                                      accum_out=den[:, kv:kv + 1]))
                        nc.scalar.activation(esink[:, kv:kv + 1], esink[:, kv:kv + 1], ACT.Exp).then_inc(S["p_ready"], 1)
                    if k == 14 + 7 * kv:
                        act.wait_ge(S["p_turned"], 2 * f + kv + 1)
                        for c in range(9):
                            m = P if c < 8 else NS
                            src = F[3 + c // 4][0:m, P * (c % 4):P * (c % 4 + 1)]
                            last = nc.scalar.activation(s_probs_t[c][0:m, :], src, ACT.Copy)
                        last.then_inc(S["p_kept"], 1)
                if m_step == 42:
                    act.wait_ge(S["s_turned"], 1)
                    nc.scalar.activation(s_nat[:, 0:512], F[0][0:NS, :], ACT.Copy)
                    nc.scalar.activation(s_nat[:, 512:1024], F[1][0:NS, :], ACT.Silu)
                    nc.scalar.activation(slots(C_QH, 4, spj), slots(C_QH, 4, spj), ACT.Silu)
                    nc.scalar.activation(slots(C_F, 4, spj), slots(C_F, 4, spj), ACT.Sigmoid).then_inc(S["kept_ig"], 1)
                if m_step == 44:
                    act.wait_ge(S["hg_f"], f + 1)
                    nc.scalar.activation(s_cum.rearrange("p (c t) -> p c t", c=4), slots(C_F, 4, spj), ACT.Ln)\
                      .then_inc(S["hg_ln"], 1)
                for l in range(2):
                    if m_step == 48 + 2 * l:
                        act.wait_ge(S["lev_d"], (NL - 1) * f + l + 1)
                        nc.scalar.activation(s_lev[l], s_lev[l], ACT.Exp).then_inc(S["lev_e"], 1)
                if m_step == 50:
                    nc.scalar.activation(s_qe, s_cum, ACT.Exp).then_inc(S["qe_exp"], 1)
                if m_step == 54:
                    act.wait_ge(S["kd_d"], f + 1)
                    nc.scalar.activation(s_lev[0], s_lev[0], ACT.Exp).then_inc(S["kd_exp"], 1)
                if m_step == 58:
                    act.wait_ge(S["kd_turned"], f + 1)
                    nc.scalar.activation(s_kdn, F[2][0:NS, :], ACT.Copy).then_inc(S["kd_kept"], 1)
                if m_step == 69:
                    act.wait_ge(S["st_mm"], DEC_B)
                    nc.scalar.activation(s_ot, F[4][:, 0:P], ACT.Copy).then_inc(S["ot_kept"], 1)
                if m_step == 71:
                    act.wait_ge(S["ot_turned"], 1)
                    act.wait_ge(S["out_kv"], 16 * (5 + 2 * DEC_B))
                    nc.scalar.activation(mix[0:NS, 512:1024], F[5][0:NS, :], ACT.Copy).then_inc(S["o_kept"], 1)
                if m_step == 73:
                    act.wait_ge(S["o_kept"], 2)
                    for h in range(HG):
                        own.mark(nc.scalar.activation(r2[0:NS, P * h:P * (h + 1)], mix[0:NS, 512 + P * h:512 + P * (h + 1)],
                                                      ACT.Square, accum_out=ssq4[0:NS, h:h + 1]))
                    own.settle()
                    nc.scalar.activation(ssq4[0:NS, :], ssq4[0:NS, :], ACT.Sqrt, bias=eps[0:NS, :], scale=1.0 / P)\
                      .then_inc(S["rms_root"], 1)

            def body(p):
                w, v, u, f = parts(p)
                for k in range(PICKS):
                    if v is not None and k < steps_of(v):
                        if k == 0:
                            act.wait_ge(S["wv_ready"], v + 1)
                            if w is None:
                                act.wait_ge(S["proj_out3"], 16 * CHUNKS)
                        act.wait_ge(S["vsum"], summed(PICKS * v + k - 1))
                        m = NS if is_sample(v) else P
                        nc.scalar.activation(diag[:, k % 2, 0:m], fold if is_sample(v) else ident[:, :], ACT.Copy,
                                             scale=w_v[:, k:k + 1]).then_inc(S["diag_ready"], 1)
                    if block_at(p, k - 1) is not None:
                        (keep_second if p == -2 else keep_third)(block_at(p, k - 1))
                    if k == 2 and w is not None:
                        m = ntok(w)
                        act.wait_ge(S["y_taken"], w + 1)
                        own.mark(nc.scalar.activation(r2[0:m, 0:D], hx[0:m, :], ACT.Square, accum_out=ssq_y[0:m, :]))
                        own.settle()
                        nc.scalar.activation(rstd_y[0:m, :], ssq_y[0:m, :], ACT.Sqrt, bias=eps[0:m, :], scale=1.0 / D)\
                          .then_inc(S["y_root"], 1)
                    if f is not None:
                        front(k, f)
                if u is not None:
                    act.wait_ge(S["dots"], PICKS * u + steps_of(u))
                    nc.scalar.activation(act_u[:, 0:steps_of(u)], act_u[:, 0:steps_of(u)], ACT.Gelu)\
                      .then_inc(S["act_ready"], 1)

            periods(act, own, body)

        @block.tensor
        def _(pe):
            pe.wait_ge(S["consts_in"], 16 * 12)
            def turn_tile(i):
                n = ntok(ORDER[i])
                pe.wait_ge(S["a_scaled"], i + 1)
                for j in range(2):
                    if i >= 1:
                        pe.wait_ge(S["a_kept"], 2 * i - 1 + j)
                    for c in range(4):
                        cc = 4 * j + c
                        last = nc.tensor.transpose(ps[:, j, c * P:c * P + n], x_a[i % 2][0:n, cc * P:(cc + 1) * P],
                                                   ident[0:n, 0:n])
                last.then_inc(S["a_turned"], 1)

            for i in range(FIRST):
                turn_tile(i)
            pe.wait_ge(S["table_in"], 32)
            pe.wait_ge(S["set_up"], 1)
            for half in range(2):
                if half:
                    pe.wait_ge(S["bias_kept"], 1)
                for h in range(4):
                    last = nc.tensor.matmul(ps[:, 4 + h, 0:SKEW], table[:, 4 * half + h, :], bucket_of, start=True, stop=True)
                last.then_inc(S["bias_mm"], 1)
            pe.wait_ge(S["a_kept"], 2 * FIRST)
            pe.wait_ge(S["bias_kept"], 2)

            def project(c, buffer, turn):
                pe.wait_ge(S[f"w_a{buffer}"], 16 * turn + 16)
                if not isinstance(c, int) or c >= 2:
                    pe.wait_ge(S["kept"], c - 1)
                bank = 2 + buffer % 2
                for d in range(DC):
                    last = nc.tensor.matmul(ps[:, bank, 0:PASS1 + NS], w_first[buffer][:, d, :], xn_t[:, d, 0:PASS1 + NS],
                                            start=(d == 0), stop=(d == DC - 1))
                last.then_inc(S["wp_done"], 1)
            for n in range(6):
                project(n, n % 4, n // 4)
                turn_tile(FIRST + n)
            for n in (6, 7):
                project(n, n % 4, n // 4)
            with pe.Fori(2, CHUNKS // 4) as it:
                for n in range(4):
                    project(4 * it + n, n, it)
            for n in range(4 * (CHUNKS // 4), CHUNKS):
                project(n, n % 4, n // 4)

            pe.wait_ge(S["keys_in"], 16)
            pe.wait_ge(S["w_q_in"], 128)
            pe.wait_ge(S["kept"], CHUNKS)
            for c in range(2 * PH):
                if c >= 2:
                    pe.wait_ge(S["m_kept"], c - 1)
                for d in range(DC):
                    last = nc.tensor.matmul(ps[:, 4 + 2 * (c % 2) + d // 4, P * (d % 4):P * (d % 4 + 1)],
                                            w_sc[:, c, P * d:P * (d + 1)], keys[:, c, :], start=True, stop=True)
                last.then_inc(S["m_mm"], 1)

            def project_second(b):
                j = b % 2
                if b == 0:
                    pe.wait_ge(S["a_kept"], 2 * (TILES + 1))
                pe.wait_ge(S[f"w_a{j}"], 16 * (CHUNKS // 4 + 1 + b // 2 + 1))
                if b >= 2:
                    pe.wait_ge(S["kept"], CHUNKS + b - 1)
                for c in range(DC):
                    last = nc.tensor.matmul(ps[:, j, :], wp[j][:, c, :], xn_t[:, c, PASS1 + NS:PASS1 + NS + PASS2],
                                            start=(c == 0), stop=(c == DC - 1))
                last.then_inc(S["wp_done"], 1)

            def project_third(b):
                j = b % 2
                if b < 2:
                    pe.wait_ge(S[f"w_a{j}"], 16 * (CHUNKS // 4 + 1 + CHUNKS // 2 + 1))
                    pe.wait_ge(S["kept"], 2 * CHUNKS)
                else:
                    pe.wait_ge(S[f"w_b{j}"], 16 * (b // 2))
                    pe.wait_ge(S["kept3"], b - 1)
                for c in range(DC):
                    last = nc.tensor.matmul(ps[:, j, 0:PASS3], wp[j][:, c, :], xn_t3[:, c, :],
                                            start=(c == 0), stop=(c == DC - 1))
                last.then_inc(S["block3"], 1)

            def turn(bank, src, count, n=P, m=P):
                for c in range(count):
                    last = nc.tensor.transpose(bank[0:m, c * n:(c + 1) * n], src[0:n, c * m:(c + 1) * m], ident[0:n, 0:n])
                return last

            def front(k, f):
                q = k + (SKIP_S if is_sample(f) else SKIP)
                first = isinstance(f, int) and f == 0
                lo = 1 if first else 0
                n = NS if is_sample(f) else P
                if is_sample(f):
                    sample_front(k, f)
                else:
                    if k == 4:
                        if first:
                            pe.wait_ge(S["m_kept"], 2 * PH)
                            pe.wait_ge(S["w_o_in"], 16)
                        pe.wait_ge(S["proj_in"], 48 * f + 48)
                        for c in range(4):
                            nc.tensor.transpose(F[0][:, P * c:P * (c + 1)], slots(C_I + c, 1)[:, 0, :], ident[:, :])
                        for c in range(4):
                            nc.tensor.transpose(F[1][:, P * c:P * (c + 1)], slots(C_G + c, 1)[:, 0, :], ident[:, :])
                        nc.tensor.transpose(F[2][:, 0:P], slots(C_V, 1)[:, 0, :], ident[:, :]).then_inc(S["turned"], 1)
                    for kv in range(KV):
                        part = slice(DH * kv, DH * (kv + 1))
                        base = 3 if kv == 0 else 0
                        if k == 8 + 4 * kv:
                            pe.wait_ge(S["kept_ig"], f + 1)
                            pe.wait_ge(S["kv_shifted"], f + 1)
                            for j in range(GRP):
                                last = nc.tensor.matmul(F[base + j // 2][:, 256 * (j % 2) + P * lo:256 * (j % 2) + 256],
                                                        slots(C_Q + j, 1)[part, 0, :], k_t[part, lo:2, :],
                                                        start=True, stop=True)
                            last.then_inc(S["scores"], 1)
                        if k == 14 + 7 * kv:
                            pe.wait_ge(S["p_ready"], 2 * f + kv + 1)
                            for j in range(GRP):
                                for b in range(lo, 2):
                                    last = nc.tensor.transpose(F[base + j // 2][:, 256 * (j % 2) + P * b:256 * (j % 2) + P * (b + 1)],
                                                               probs[:, j, P * b:P * (b + 1)], ident[:, :])
                            last.then_inc(S["p_turned"], 1)
                        if k == 18 + 7 * kv:
                            pe.wait_ge(S["p_kept"], 2 * f + kv + 1)
                            pe.wait_ge(S["v_kept"], f + 1)
                            for j in range(GRP):
                                h = GRP * kv + j
                                for b in range(lo, 2):
                                    last = nc.tensor.matmul(F[5][:, DH * h:DH * (h + 1)], probs_t[:, j, b, :],
                                                            v_n[:, b, part], start=(b == lo), stop=(b == 1))
                            last.then_inc(S["pv"], 1)
                    for l in range(NL):
                        if k == 35 + 2 * l:
                            if l < NL - 1:
                                pe.wait_ge(S["lev_q"], (NL - 1) * f + l + 1)
                                lhs = rhs = lev[l % 2].rearrange("p (c t) -> p c t", c=4)
                            else:
                                lhs, rhs = slots(C_F, 4), slots(C_QH, 4)
                            if l >= 2:
                                pe.wait_ge(S["lev_kept"], NL * f + l - 1)
                            for h in range(HG):
                                last = nc.tensor.matmul(F[l % 2][:, P * h:P * (h + 1)], lhs[:, h, :], rhs[:, h, :],
                                                        start=True, stop=True)
                            last.then_inc(S["lev_mm"], 1)
                    if k == 50:
                        pe.wait_ge(S["kd_ready"], f + 1)
                        turn(F[2], lev[1], HG).then_inc(S["kd_turned"], 1)
                    if k == 53:
                        pe.wait_ge(S["lev_kept"], NL * f + NL)
                        pe.wait_ge(S["kd_kept"], f + 1)
                        pe.wait_ge(S["qe_ready"], f + 1)
                        pe.wait_ge(S["s_new"], f)
                        for h in range(HG):
                            cols = slice(P * h, P * (h + 1))
                            nc.tensor.matmul(F[3][:, cols], a_t[:, h, :], slots(C_I, 4)[:, h, :], start=True, stop=False)
                            nc.tensor.matmul(F[3][:, cols], slots(C_Q, 4)[:, h, :], state[:, h, :], start=False, stop=True)
                        for h in range(HG):
                            cols = slice(P * h, P * (h + 1))
                            last = nc.tensor.matmul(F[4][:, cols], kd_n[:, cols], slots(C_I, 4)[:, h, :], start=True, stop=True)
                        last.then_inc(S["hg_out"], 1)
                if q == 75:
                    pe.wait_ge(S["mix_ready"], f + 1)
                    turn(F[0], mix[:, 0:512], 4, n)
                    turn(F[1], mix[:, 512:1024], 4, n).then_inc(S["mix_turned"], 1)
                if 77 <= q < 85:
                    j, part = divmod(q - 77, 4)
                    if part == 0:
                        pe.wait_ge(S["mix_kept"], f + 1)
                    for c in range(2 * part, 2 * part + 2):
                        last = nc.tensor.matmul(F[2 + j][0:n, :], mix_t[:, c, 0:n], w_o[:, c, 512 * j:512 * (j + 1)],
                                                start=(c == 0), stop=(c == DC - 1))
                    if part == 3:
                        last.then_inc(S["h_mm"], 1)
                if q == 88:
                    pe.wait_ge(S["hn_ready"], f + 1)
                    turn(F[4], hn[:, 0:512], 4, n)
                    turn(F[5], hn[:, 512:1024], 4, n).then_inc(S["hn_turned"], 1)
                if 90 <= q < 114:
                    g, part = divmod(q - 90, 6)
                    if part == 0:
                        pe.wait_ge(S["hn_kept"], f + 1)
                    for d in range((8 * part + 5) // 6, (8 * part + 13) // 6):
                        last = nc.tensor.matmul(F[g][0:n, :], hn_t[:, d, 0:n], w_sc[:, 4 * g:4 * g + 4, P * d:P * (d + 1)],
                                                start=(d == 0), stop=(d == DC - 1))
                    if part == 5:
                        last.then_inc(S["sc_mm"], 1)

            def sample_front(k, f):
                m_step = k + SKIP_M
                if k == 1:
                    nc.tensor.transpose(F[5][:, 0:P], k_t[:, 1, :], ident[:, :]).then_inc(S["k7_turned"], 1)
                if k == 4:
                    pe.wait_ge(S["proj_in"], 48 * f + 48)
                    nc.tensor.transpose(F[2][0:NS, 0:P], slots(C_V, 1, spj)[:, 0, :], ident[:, :])
                    nc.tensor.transpose(F[2][0:NS, P:2 * P], k_t[:, 1, 0:NS], ident[:, :]).then_inc(S["turned"], 1)
                if k == 7:
                    pe.wait_ge(S["s_tab_ready"], 2)
                    pe.wait_ge(S["caches_in"], 64)
                    pe.wait_ge(S["k7_kept"], 1)
                    for g in range(KV):
                        last = nc.tensor.matmul(F[5][:, 132 * g:132 * (g + 1)], s_tab[:, P * g:P * (g + 1)], s_oh,
                                                start=True, stop=True)
                    last.then_inc(S["s_bias_mm"], 1)
                for kv in range(KV):
                    part = slice(DH * kv, DH * (kv + 1))
                    if k == 10 + 7 * kv:
                        if kv == 0:
                            pe.wait_ge(S["v_kept"], f + 2)
                        else:
                            pe.wait_ge(S["mix_attn"], f + kv)
                        for j in range(GRP):
                            q = slots(C_Q + j, 1, spj)[part, 0, :]
                            out_rows = slice(NS * j, NS * (j + 1))
                            nc.tensor.matmul(F[0][out_rows, :], q, kc_t[part, 0:512], start=True, stop=True)
                            nc.tensor.matmul(F[1][out_rows, :], q, kc_t[part, 512:1024], start=True, stop=True)
                            last = nc.tensor.matmul(F[2][out_rows, 0:NS], q, k_t[part, 1, 0:NS], start=True, stop=True)
                        last.then_inc(S["scores"], 1)
                    if k == 13 + 7 * kv:
                        pe.wait_ge(S["p_ready"], 2 * f + kv + 1)
                        pe.wait_ge(S["s_bias_kept"], 1)
                        for c in range(9):
                            m = P if c < 8 else NS
                            last = nc.tensor.transpose(F[3 + c // 4][0:m, P * (c % 4):P * (c % 4 + 1)],
                                                       s_probs[:, P * c:P * c + m], ident[:, :])
                        last.then_inc(S["p_turned"], 1)
                    if k == 15 + 7 * kv:
                        pe.wait_ge(S["p_kept"], 2 * f + kv + 1)
                        for c in range(9):
                            m = P if c < 8 else NS
                            values = vc[:, c, part] if c < 8 else v_n[0:NS, 1, part]
                            last = nc.tensor.matmul(F[2][:, 64:128], s_probs_t[c][0:m, :], values,
                                                    start=(c == 0), stop=(c == 8))
                        last.then_inc(S["pv"], 1)
                if m_step == 40:
                    for c in range(4):
                        nc.tensor.transpose(F[0][0:NS, P * c:P * (c + 1)], slots(C_I + c, 1, spj)[:, 0, :], ident[:, :])
                    for c in range(4):
                        last = nc.tensor.transpose(F[1][0:NS, P * c:P * (c + 1)], slots(C_G + c, 1, spj)[:, 0, :], ident[:, :])
                    last.then_inc(S["s_turned"], 1)
                for l in range(3):
                    if m_step == 50 + 2 * l:
                        if l < 2:
                            pe.wait_ge(S["lev_q"], (NL - 1) * f + l + 1)
                            lhs = rhs = s_lev[l].rearrange("p (c t) -> p c t", c=4)
                        else:
                            lhs, rhs = slots(C_F, 4, spj), slots(C_QH, 4, spj)
                        if l == 0:
                            pe.wait_ge(S["kept_ig"], f + 1)
                        else:
                            pe.wait_ge(S["lev_kept"], NL * f + l)
                        for h in range(HG):
                            last = nc.tensor.matmul(F[0][0:NS, NS * h:NS * (h + 1)], lhs[:, h, :], rhs[:, h, :],
                                                    start=True, stop=True)
                        last.then_inc(S["lev_mm"], 1)
                if m_step == 57:
                    pe.wait_ge(S["kd_ready"], f + 1)
                    for h in range(HG):
                        last = nc.tensor.transpose(F[2][0:NS, P * h:P * (h + 1)], s_lev[0][:, NS * h:NS * (h + 1)], ident[:, :])
                    last.then_inc(S["kd_turned"], 1)
                if m_step == 59:
                    pe.wait_ge(S["lev_kept"], NL * f + 3)
                    for h in range(HG):
                        cols = slice(P * h, P * (h + 1))
                        nc.tensor.matmul(F[3][0:NS, cols], a_t[0:NS, h, 0:NS], s_nat[:, cols], start=True, stop=True)
                for b in range(DEC_B):
                    if m_step == 60 + b:
                        pe.wait_ge(S["qe_ready"], f + 1)
                        pe.wait_ge(S[f"st_in{b % 3}"], 16 * (b // 3 + 1))
                        pe.wait_ge(S["kdm_ready"], b + 1)
                        if b >= 2:
                            pe.wait_ge(S["st_new"], b - 1)
                        for h in range(HG):
                            col = NS * h + DEC_T * b
                            nc.tensor.matmul(F[4][:, col:col + DEC_T], s_st[b % 3][:, P * h:P * (h + 1)],
                                             s_qe[:, col:col + DEC_T], start=True, stop=True)
                        for h in range(HG):
                            cols = slice(P * h, P * (h + 1))
                            last = nc.tensor.matmul(F[b % 2][:, cols], s_kdm[b % 2][:, cols], s_nat[:, cols],
                                                    start=True, stop=True)
                        last.then_inc(S["st_mm"], 1)
                if m_step == 70:
                    pe.wait_ge(S["ot_kept"], 1)
                    for h in range(HG):
                        last = nc.tensor.transpose(F[5][0:NS, P * h:P * (h + 1)], s_ot[:, NS * h:NS * (h + 1)], ident[:, :])
                    last.then_inc(S["ot_turned"], 1)

            def body(p):
                w, v, u, f = parts(p)
                for k in range(PICKS):
                    if v is not None and k < steps_of(v):
                        if k == 0 and w is not None:
                            pe.wait_ge(S["y_taken"], v)
                        pe.wait_ge(S["diag_ready"], PICKS * v + k + 1)
                        pe.wait_ge(v_row[k % V_RING], 16 * (PICKS // V_RING) * v + 16 * (k // V_RING + 1))
                        m = NS if is_sample(v) else P
                        for x, y in ((0, 512), (512, D - SIDE if side_sum(v, k) else D)):
                            last = nc.tensor.matmul(Y[x // 512][0:m, 0:y - x], diag[:, k % 2, 0:m],
                                                    v_rows[:, k % V_RING, x:y], start=(k == 0), stop=(k == steps_of(v) - 1))
                        last.then_inc(S["vsum"], 1)
                    if block_at(p, k) is not None:
                        (project_second if p == -2 else project_third)(block_at(p, k))
                    if f is not None:
                        front(k, f)

            pe.sem_inc(S["vsum"], summed(0))
            periods(pe, None, body)

        @block.vector
        def _(dve):
            own = Own(dve, S["own_dve"], DVE_PER)
            mark, settle = own.mark, own.settle
            V = nc.vector
            mark(V.memset(eps, EPS))
            mark(V.memset(one, 1.0))
            mark(V.memset(hn[BUCKETS:BUCKETS + 1, :], NEG))
            mark(V.memset(state[:, :, :], 0.0))
            mark(V.memset(a_t[:, :, :], 0.0))
            V.memset(mix_scale[:, 0:4], 1.0).then_inc(S["set_up"], 1)
            dve.wait_ge(S["consts_in"], 16 * 12)
            mark(V.tensor_copy(level_masks[:, :, :], hn_u[:, :].rearrange("p (l t) -> p l t", l=NL)))
            lb_e = lb_in.rearrange("p (r h) -> p r h", r=2)
            mark(V.tensor_tensor(lb, lb_e[:, 0, :], lb_e[:, 1, :], ALU.max))
            settle()
            for r in range(2):
                last = V.tensor_tensor(lb_e[:, r, :], lb_e[:, r, :], lb, ALU.subtract)
            last.then_inc(S["lb_shifted"], 1)
            dve.wait_ge(S["lb_exp"], 1)
            mark(V.tensor_tensor(oml, lb_e[:, 0, :], lb_e[:, 1, :], ALU.add))
            settle()
            mark(V.reciprocal(oml, oml))
            settle()
            mark(V.tensor_tensor(lb, lb_e[:, 0, :], oml, ALU.mult))
            settle()
            mark(V.tensor_scalar(oml, lb, -1.0, 1.0, ALU.mult, ALU.add))
            settle()

            def scale_and_keep(i):
                tile = ORDER[i]
                n = ntok(tile)
                dve.wait_ge(S["a_root"], i + 1)
                mark(V.reciprocal(rstd[0:n, :], rstd[0:n, :]))
                settle()
                V.tensor_scalar(x_a[i % 2][0:n, :], x_a[i % 2][0:n, :], rstd[0:n, :], None, ALU.mult)\
                    .then_inc(S["a_scaled"], 1)
                dve.wait_ge(S["a_turned"], i + 1)
                dst, col = (xn_t, column[tile]) if tile in column else (xn_t3, P * (tile - (TILES - 2)))
                for j in range(2):
                    V.tensor_tensor(dst[:, 4 * j:4 * j + 4, col:col + n],
                                    ps[:, j, :].rearrange("p (c t) -> p c t", c=4)[:, :, 0:n],
                                    w_mix[:, 4 * j:4 * j + 4].unsqueeze(2).to_broadcast([P, 4, n]), ALU.mult)\
                        .then_inc(S["a_kept"], 1)
            for i in range(TILES + 1):
                scale_and_keep(i)
            for c in range(2 * PH):
                dve.wait_ge(S["m_mm"], c + 1)
                bank = 4 + 2 * (c % 2)
                V.tensor_copy(w_sc[:, c, :].rearrange("p (b x) -> p b x", b=2), ps[:, bank:bank + 2, :])\
                    .then_inc(S["m_kept"], 1)

            def mask_scores(f, kv, lo):
                dve.wait_ge(S["scores"], 2 * f + kv + 1)
                if isinstance(f, int) and f == 0:
                    dve.wait_ge(S["bias_in"], 16 * HEADS)
                if kv:
                    dve.wait_ge(S["p_turned"], 2 * f + kv)
                for j in range(2):
                    h = GRP * kv + 2 * j
                    bank = F[(3 if kv == 0 else 0) + j].rearrange("p (h s) -> p h s", h=2)
                    mark(V.scalar_tensor_tensor(probs[:, 2 * j:2 * j + 2, lo:2 * P], bank[:, :, lo:2 * P], SCALE,
                                                bias_v[:, h:h + 2, lo:2 * P], ALU.mult, ALU.add))
                settle()
                heads = slice(GRP * kv, GRP * (kv + 1))
                mark(V.tensor_reduce(rmax, probs[:, :, lo:2 * P], AX.X, ALU.max))
                settle()
                mark(V.tensor_tensor(rmax, rmax, sinks[:, heads], ALU.max))
                settle()
                V.tensor_tensor(esink[:, heads], sinks[:, heads], rmax, ALU.subtract)
                V.tensor_scalar(nmax[:, heads], rmax, -1.0, None, ALU.mult).then_inc(S["s_masked"], 1)

            def level_exponents(l, m, cum_v, out):
                b = cum_v.rearrange("p (x two m) -> p x two m", two=2, m=m)
                o = out.rearrange("p (x two m) -> p x two m", two=2, m=m)
                ref = b[:, :, 0, m - 1:m].to_broadcast([P, b.shape[1], m])
                V.tensor_tensor(o[:, :, 1, :], b[:, :, 1, :], ref, ALU.subtract)
                V.tensor_tensor(o[:, :, 0, :], ref, b[:, :, 0, :], ALU.subtract).then_inc(S["lev_d"], 1)

            def level_factors(l, m, e, q, kk):
                o = e.rearrange("p (x two m) -> p x two m", two=2, m=m)
                q = q.rearrange("p (x two m) -> p x two m", two=2, m=m)
                kk = kk.rearrange("p (x two m) -> p x two m", two=2, m=m)
                V.tensor_tensor(o[:, :, 1, :], o[:, :, 1, :], q[:, :, 1, :], ALU.mult)
                V.tensor_tensor(o[:, :, 0, :], o[:, :, 0, :], kk[:, :, 0, :], ALU.mult).then_inc(S["lev_q"], 1)

            flat = "p c t -> p (c t)"

            def front(k, f):
                q = k + (SKIP_S if is_sample(f) else SKIP)
                first = isinstance(f, int) and f == 0
                n = NS if is_sample(f) else P
                lo = P if first else 0
                if is_sample(f):
                    sample_front(k, f)
                else:
                    q_s, k_s = slots(C_QH, 4).rearrange(flat), slots(C_F, 4).rearrange(flat)
                    for kv in range(KV):
                        if k == 10 + 7 * kv:
                            mask_scores(f, kv, lo)
                    if k == 20:
                        dve.wait_ge(S["kept_ig"], f + 1)
                        for h in range(HG):
                            last = V.tensor_scalar(slots(C_F, 4)[:, h, :], slots(C_F, 4)[:, h, :], oml[:, h:h + 1],
                                                   lb[:, h:h + 1], ALU.mult, ALU.add)
                        last.then_inc(S["hg_f"], 1)
                    if k == 27:
                        dve.wait_ge(S["pv"], 2 * f + 2)
                        dve.wait_ge(S["p_ready"], 2 * f + 2)
                        mark(V.tensor_tensor(den, den, esink, ALU.add))
                        settle()
                        mark(V.reciprocal(den, den))
                        settle()
                        V.tensor_tensor(mix[:, 0:512].rearrange("p (h d) -> p h d", h=HEADS),
                                        F[5].rearrange("p (h d) -> p h d", h=HEADS),
                                        den.unsqueeze(2).to_broadcast([P, HEADS, DH]), ALU.mult).then_inc(S["mix_attn"], 1)
                    if k == 30:
                        dve.wait_ge(S["hg_ln"], f + 1)
                        V.tensor_scalar(k_s, k_s, -1.0, 1.0, ALU.mult, ALU.add)
                        for h in range(HG):
                            last = V.tensor_tensor_scan(cum[:, P * h:P * (h + 1)], one.to_broadcast([P, P]),
                                                        cum[:, P * h:P * (h + 1)], 0.0, ALU.mult, ALU.add)
                        last.then_inc(S["hg_k"], 1)
                        dve.wait_ge(S["hg_k"], f + 1)
                    for l in range(NL):
                        if k == 32 + 2 * l and l < NL - 1:
                            if l >= 2:
                                dve.wait_ge(S["lev_mm"], NL * f + l - 1)
                            level_exponents(l, LEVELS[l], cum, lev[l % 2])
                        if k == 34 + 2 * l and l < NL - 1:
                            dve.wait_ge(S["lev_e"], (NL - 1) * f + l + 1)
                            level_factors(l, LEVELS[l], lev[l % 2], q_s, k_s)
                        if k == 36 + 2 * l:
                            hold(dve, S["lev_mm"], NL * f + l + 1, S["held_dve"])
                            if l:
                                hold(dve, S["lev_kept"], NL * f + l, S["held_dve"])
                            V.copy_predicated(a_t[:, :, :], level_masks[:, l:l + 1, :].to_broadcast([P, HG, P]),
                                              F[l % 2].rearrange("p (c t) -> p c t", c=4)).then_inc(S["lev_kept"], 1)
                    if k == 40:
                        dve.wait_ge(S["qe_exp"], f + 1)
                        mark(V.tensor_copy(decay, slots(C_Q, 4)[:, :, P - 1]))
                        settle()
                        V.tensor_tensor(slots(C_Q, 4), slots(C_Q, 4), slots(C_QH, 4), ALU.mult).then_inc(S["qe_ready"], 1)
                    if k == 47:
                        dve.wait_ge(S["lev_mm"], NL * f + 6)
                        c3 = cum.rearrange("p (c t) -> p c t", c=4)
                        V.tensor_tensor(lev[1].rearrange("p (c t) -> p c t", c=4),
                                        c3[:, :, P - 1:P].to_broadcast([P, HG, P]), c3, ALU.subtract).then_inc(S["kd_d"], 1)
                    if k == 49:
                        dve.wait_ge(S["kd_exp"], f + 1)
                        V.tensor_tensor(lev[1], lev[1], k_s, ALU.mult).then_inc(S["kd_ready"], 1)
                    if k == 55:
                        dve.wait_ge(S["hg_out"], f + 1)
                        settle()
                        for h in range(HG):
                            last = V.scalar_tensor_tensor(state[:, h, :], state[:, h, :], decay[:, h:h + 1],
                                                          F[4][:, P * h:P * (h + 1)], ALU.mult, ALU.add)
                        last.then_inc(S["s_new"], 1)
                if q == 74:
                    dve.wait_ge(S["rms_root"], f + 1)
                    mark(V.reciprocal(ssq4[0:n, :], ssq4[0:n, :]))
                    settle()
                    m3 = mix[0:n, 512:1024].rearrange("p (h d) -> p h d", h=HG)
                    mark(V.tensor_tensor(m3, m3, ssq4[0:n, :].unsqueeze(2).to_broadcast([n, HG, P]), ALU.mult))
                    settle()
                    g_s = s_nat[:, 512:1024].rearrange("p (h d) -> p h d", h=HG) if is_sample(f) else slots(C_G, 4)
                    V.tensor_tensor(m3, m3, g_s, ALU.mult).then_inc(S["mix_ready"], 1)
                if q == 76:
                    dve.wait_ge(S["mix_turned"], f + 1)
                    for j in range(2):
                        last = V.tensor_tensor(mix_t[:, 4 * j:4 * j + 4, 0:n],
                                               F[j][:, 0:4 * n].rearrange("p (c t) -> p c t", c=4),
                                               mix_scale[:, 4 * j:4 * j + 4].unsqueeze(2).to_broadcast([P, 4, n]), ALU.mult)
                    last.then_inc(S["mix_kept"], 1)
                if q == 85:
                    dve.wait_ge(S["h_mm"], 2 * f + 2)
                    dve.wait_ge(S["x_in"], 16 * f + 16)
                    for j in range(2):
                        cols = slice(512 * j, 512 * (j + 1))
                        last = V.tensor_tensor(hx[0:n, cols], F[2 + j][0:n, :], hx[0:n, cols], ALU.add)
                    last.then_inc(S["h_ready"], 1)
                if q == 87:
                    dve.wait_ge(S["ssq_root"], f + 1)
                    dve.wait_ge(S["norms_in"], 32)
                    mark(V.reciprocal(rstd[0:n, :], rstd[0:n, :]))
                    settle()
                    V.scalar_tensor_tensor(hn[0:n, :], hx[0:n, :], rstd[0:n, :], w_ffn[0:n, :], ALU.mult, ALU.mult)\
                        .then_inc(S["hn_ready"], 1)
                    dve.wait_ge(S["hn_ready"], f + 1)
                for g in range(4):
                    if q == 97 + 6 * g:
                        hold(dve, S["sc_kept"], 4 * f + g + 1, S["held_dve"])
                        top16([sc[0:n, c, :] for c in range(4 * g, 4 * g + 4)], [sv[0:n, c, :] for c in range(4 * g, 4 * g + 4)],
                              [si[0:n, c, :] for c in range(4 * g, 4 * g + 4)])
                if q == 116:
                    settle()
                    sv4 = sv[0:n].rearrange("p (h two) k -> p h two k", two=2)
                    for j in range(2):
                        hs = slice(4 * j, 4 * j + 4)
                        mark(V.tensor_tensor(cand[0:n, hs, :].rearrange("p h (x y) -> p h x y", x=TOPK),
                                             sv4[:, hs, 0, :].unsqueeze(3).to_broadcast([n, 4, TOPK, TOPK]),
                                             sv4[:, hs, 1, :].unsqueeze(2).to_broadcast([n, 4, TOPK, TOPK]), ALU.add))
                    mark(V.tensor_copy(si_f[0:n], si[0:n]))
                    settle()
                for j in range(4):
                    if q == 118 + 2 * j:
                        top16([cand[0:n, h, :] for h in (2 * j, 2 * j + 1)], [fv[0:n, h, :] for h in (2 * j, 2 * j + 1)],
                              [fi[0:n, h, :] for h in (2 * j, 2 * j + 1)])
                if q == 126:
                    settle()
                    fi_x = r3[0:n, 896:1024].bitcast(U32)
                    mark(V.tensor_scalar(pos[0][0:n].bitcast(U32), fi_x, 4, None, ALU.logical_shift_right))
                    mark(V.tensor_scalar(pos[1][0:n].bitcast(U32), fi_x, 15, None, ALU.bitwise_and))
                    V.tensor_tensor(gate_f[0:n, :].rearrange("p (h k) -> p h k", h=PH), fv[0:n],
                                    fv[0:n, :, 0:1].to_broadcast([n, PH, TOPK]), ALU.subtract)\
                        .then_inc(S["gate_d"], 1)
                    settle()
                    for j in range(2):
                        mark(V.tensor_copy(pos[2 + j][0:n], pos[j][0:n].bitcast(U32)))
                    settle()
                for j in range(2):
                    if q == 128 + 2 * j:
                        oh = onehot[0:n]
                        settle()
                        mark(V.tensor_tensor(oh, pos[2 + j][0:n].unsqueeze(2).to_broadcast([n, PICKS, TOPK]),
                                             iota16[0:n].unsqueeze(1).to_broadcast([n, PICKS, TOPK]), ALU.is_equal))
                        settle()
                        si4 = si_f[0:n].rearrange("p (h two) k -> p h two k", two=2)[:, :, j, :]
                        oh4 = oh.rearrange("p (h k) x -> p h k x", h=PH)
                        mark(V.tensor_tensor(oh4, oh4, si4.unsqueeze(2).to_broadcast([n, PH, TOPK, TOPK]), ALU.mult))
                        settle()
                        mark(V.tensor_reduce(pos[j][0:n], oh, AX.X, ALU.add))
                if q == 133:
                    settle()
                    if not first:
                        dve.wait_ge(S["idx_taken"], 2 * f)
                    dve.wait_ge(S["gate_exp"], f + 1)
                    g3 = gate_f[0:n].rearrange("p (h k) -> p h k", h=PH)
                    mark(V.tensor_reduce(gsum[0:n], fv[0:n], AX.X, ALU.add))
                    settle()
                    mark(V.reciprocal(gsum[0:n], gsum[0:n]))
                    settle()
                    if not is_sample(f):
                        mark(V.scalar_tensor_tensor(idx_f[:, :], pos[0], float(P), pos[1], ALU.mult, ALU.add))
                        V.tensor_tensor(g3, fv[:], gsum.unsqueeze(2).to_broadcast([P, PH, TOPK]), ALU.mult)\
                            .then_inc(S["topk_done"], 1)
                        mark(V.memset(rmax[:, 0:1], 0.0))
                        settle()
                    else:
                        for g in range(SGRP):
                            cols, part = slice(NS * g, NS * (g + 1)), slice(NS * g, NS * (g + 1))
                            V.scalar_tensor_tensor(idx_f[part, 0:NS], pos[0][0:NS, cols], float(P), pos[1][0:NS, cols],
                                                   ALU.mult, ALU.add)
                            hs = slice(2 * g, 2 * g + 2)
                            last = V.tensor_tensor(gate_f[part, 0:NS].rearrange("p (h k) -> p h k", h=2), fv[0:NS, hs, :],
                                                   gsum[0:NS, hs].unsqueeze(2).to_broadcast([NS, 2, TOPK]), ALU.mult)
                        last.then_inc(S["topk_done"], 1)
                        dve.wait_ge(S["topk_done"], f + 1)

            def top16(values, best, places):
                for x, b in zip(values, best):
                    mark(V.max(b[:, 0:8], x))
                own.settle_held(S["held_dve"])
                for x, b, i in zip(values, best, places):
                    mark(V.max_index(i[:, 0:8], b[:, 0:8], x))
                    mark(V.match_replace(x, b[:, 0:8], x, LOWEST))
                own.settle_held(S["held_dve"])
                for x, b in zip(values, best):
                    mark(V.max(b[:, 8:16], x))
                own.settle_held(S["held_dve"])
                for x, b, i in zip(values, best, places):
                    mark(V.max_index(i[:, 8:16], b[:, 8:16], x))

            def sample_front(k, f):
                m_step = k + SKIP_M
                q_s, k_s = slots(C_QH, 4, spj).rearrange(flat), slots(C_F, 4, spj).rearrange(flat)
                if k == 2:
                    for g in range(KV):
                        V.tensor_tensor(s_tab[:, P * g:P * (g + 1)].rearrange("p (h b t) -> p h b t", h=GRP, b=DEC_B),
                                        tab_rep[:, GRP * g:GRP * (g + 1)].unsqueeze(2).unsqueeze(3).to_broadcast([P, GRP, DEC_B, DEC_T]),
                                        tsel.unsqueeze(1).unsqueeze(1).to_broadcast([P, GRP, DEC_B, DEC_T]), ALU.mult)\
                            .then_inc(S["s_tab_ready"], 1)
                for kv in range(KV):
                    if k == 11 + 7 * kv:
                        dve.wait_ge(S["scores"], 2 * f + kv + 1)
                        dve.wait_ge(S["s_bias_kept"], 1)
                        dve.wait_ge(S["caches_in"], 64)
                        if kv:
                            dve.wait_ge(S["p_turned"], 2 * f + 1)
                        for b, (x, y) in enumerate(((0, 512), (512, 1024), (1024, 1024 + NS))):
                            mark(V.scalar_tensor_tensor(s_probs[:, x:y], F[b][:, 0:y - x], SCALE, s_mask[:, x:y], ALU.mult, ALU.add))
                        settle()
                        old = s_probs[:, 0:D].rearrange("p (b j) -> p b j", b=DEC_B)
                        new = s_probs[:, D:D + NS].rearrange("p (b j) -> p b j", b=DEC_B)
                        mark(V.tensor_tensor(old, old, s_bias[:, kv:kv + 1, 0:P].to_broadcast([P, DEC_B, P]), ALU.add))
                        mark(V.tensor_tensor(new, new, s_bias[:, kv:kv + 1, P:P + DEC_T].to_broadcast([P, DEC_B, DEC_T]), ALU.add))
                        settle()
                        mark(V.tensor_reduce(rmax[:, 0:1], s_probs, AX.X, ALU.max))
                        settle()
                        mark(V.tensor_tensor(rmax[:, 0:1], rmax[:, 0:1], sinks_s[:, kv:kv + 1], ALU.max))
                        settle()
                        V.tensor_tensor(esink[:, kv:kv + 1], sinks_s[:, kv:kv + 1], rmax[:, 0:1], ALU.subtract)
                        V.tensor_scalar(nmax[:, kv:kv + 1], rmax[:, 0:1], -1.0, None, ALU.mult).then_inc(S["s_masked"], 1)
                    if k == 16 + 7 * kv:
                        dve.wait_ge(S["pv"], 2 * f + kv + 1)
                        mark(V.tensor_tensor(den[:, kv:kv + 1], den[:, kv:kv + 1], esink[:, kv:kv + 1], ALU.add))
                        settle()
                        mark(V.reciprocal(den[:, kv:kv + 1], den[:, kv:kv + 1]))
                        settle()
                        for j in range(GRP):
                            part, h = slice(NS * j, NS * (j + 1)), GRP * kv + j
                            last = V.tensor_scalar(mix[0:NS, DH * h:DH * (h + 1)], F[2][part, 64:128], den[part, kv:kv + 1],
                                                   None, ALU.mult)
                        last.then_inc(S["mix_attn"], 1)
                if m_step == 43:
                    dve.wait_ge(S["kept_ig"], f + 1)
                    for h in range(HG):
                        last = V.tensor_scalar(slots(C_F, 4, spj)[:, h, :], slots(C_F, 4, spj)[:, h, :], oml[:, h:h + 1],
                                               lb[:, h:h + 1], ALU.mult, ALU.add)
                    last.then_inc(S["hg_f"], 1)
                    dve.wait_ge(S["hg_out"], f)
                    mark(V.memset(a_t[0:NS, :, 0:NS], 0.0))
                    mark(V.memset(s_reset, 1.0))
                    settle()
                    mark(V.memset(s_reset.rearrange("p (x t) -> p x t", t=DEC_T)[:, :, 0:1], 0.0))
                if m_step == 45:
                    dve.wait_ge(S["hg_ln"], f + 1)
                    settle()
                    V.tensor_scalar(k_s, k_s, -1.0, 1.0, ALU.mult, ALU.add)
                    V.tensor_tensor_scan(s_cum, s_reset, s_cum, 0.0, ALU.mult, ALU.add).then_inc(S["hg_k"], 1)
                    dve.wait_ge(S["hg_k"], f + 1)
                for l in range(3):
                    if m_step == 47 + 2 * l and l < 2:
                        level_exponents(l, LEVELS[5 + l], s_cum, s_lev[l])
                    if m_step == 49 + 2 * l and l < 2:
                        dve.wait_ge(S["lev_e"], (NL - 1) * f + l + 1)
                        level_factors(l, LEVELS[5 + l], s_lev[l], q_s, k_s)
                    if m_step == 51 + 2 * l:
                        dve.wait_ge(S["lev_mm"], NL * f + l + 1)
                        if l:
                            dve.wait_ge(S["lev_kept"], NL * f + l)
                        V.copy_predicated(a_t[0:NS, :, 0:NS], level_masks[0:NS, 5 + l:6 + l, 0:NS].to_broadcast([NS, HG, NS]),
                                          F[0][0:NS, 0:P].rearrange("p (c t) -> p c t", c=4)).then_inc(S["lev_kept"], 1)
                if m_step == 52:
                    dve.wait_ge(S["qe_exp"], f + 1)
                    mark(V.tensor_copy(s_dec, s_qe.rearrange("p (x t) -> p x t", t=DEC_T)[:, :, DEC_T - 1]))
                    settle()
                    V.tensor_tensor(s_qe, s_qe, q_s, ALU.mult).then_inc(S["qe_ready"], 1)
                    dve.wait_ge(S["lev_mm"], NL * f + 1)
                    c3 = s_cum.rearrange("p (x t) -> p x t", t=DEC_T)
                    V.tensor_tensor(s_lev[0].rearrange("p (x t) -> p x t", t=DEC_T),
                                    c3[:, :, DEC_T - 1:DEC_T].to_broadcast([P, HG * DEC_B, DEC_T]), c3, ALU.subtract)\
                        .then_inc(S["kd_d"], 1)
                if m_step == 56:
                    dve.wait_ge(S["kd_exp"], f + 1)
                    V.tensor_tensor(s_lev[0], s_lev[0], k_s, ALU.mult).then_inc(S["kd_ready"], 1)
                for b in range(DEC_B):
                    if m_step == 59 + b:
                        dve.wait_ge(S["kd_kept"], f + 1)
                        if b >= 2:
                            dve.wait_ge(S["st_mm"], b - 1)
                        V.tensor_scalar(s_kdm[b % 2], s_kdn, bsel[0:NS, b:b + 1], None, ALU.mult).then_inc(S["kdm_ready"], 1)
                    if m_step == 61 + b:
                        dve.wait_ge(S["st_mm"], b + 1)
                        settle()
                        for h in range(HG):
                            cols = slice(P * h, P * (h + 1))
                            last = V.scalar_tensor_tensor(s_st[b % 3][:, cols], s_st[b % 3][:, cols],
                                                          s_dec[:, DEC_B * h + b:DEC_B * h + b + 1], F[b % 2][:, cols],
                                                          ALU.mult, ALU.add)
                        last.then_inc(S["st_new"], 1)
                if m_step == 72:
                    dve.wait_ge(S["o_kept"], 1)
                    V.tensor_tensor(mix[0:NS, 512:1024], mix[0:NS, 512:1024], F[3][0:NS, :], ALU.add).then_inc(S["o_kept"], 1)

            def body(p):
                w, v, u, f = parts(p)
                for k in range(PICKS):
                    if u is not None and k < steps_of(u):
                        dve.wait_ge(u_row[k % U_RING], 16 * (PICKS // U_RING) * u + 16 * (k // U_RING + 1))
                        V.tensor_tensor_reduce(u_rows[:, k % U_RING, :], u_rows[:, k % U_RING, :], hn_u[:, :], 1.0, 0.0,
                                               ALU.mult, ALU.add, act_u[:, k:k + 1]).then_inc(S["dots"], 1)
                    if side_sum(v, k):
                        dve.wait_ge(v_row[k % V_RING], 16 * (PICKS // V_RING) * v + 16 * (k // V_RING + 1))
                        row, side = v_rows[:, k % V_RING, D - SIDE:D], hn[:, 0:SIDE]
                        if k == NS:
                            V.tensor_scalar(side, row, w_v[:, k:k + 1], None, ALU.mult).then_inc(S["side_added"], 1)
                        else:
                            dve.wait_ge(S["side_added"], k - NS)
                            V.scalar_tensor_tensor(side, row, w_v[:, k:k + 1], side, ALU.mult, ALU.add)\
                                .then_inc(S["side_added"], 1)
                    if w is not None:
                        finish(k, w)
                    if f is not None:
                        front(k, f)
                if f is not None:
                    if u is not None:
                        dve.wait_ge(S["dots"], PICKS * u + steps_of(u))
                    if is_sample(f):
                        for g in range(SGRP):
                            mark(V.tensor_copy(hn_u[NS * g:NS * (g + 1), :], hn[0:NS, :]))
                    else:
                        V.tensor_copy(hn_u[:, :], hn[:, :]).then_inc(S["hn_taken"], 1)
                if u is not None:
                    n = steps_of(u)
                    dve.wait_ge(S["act_ready"], u + 1)
                    if v is not None:
                        dve.wait_ge(S["diag_ready"], PICKS * v + steps_of(v))
                        if side_sum(v, NS):
                            dve.wait_ge(S["side_added"], PICKS - NS)
                    V.tensor_tensor(w_v[:, 0:n], act_u[:, 0:n], gate_u[:, 0:n], ALU.mult).then_inc(S["wv_ready"], 1)
                    dve.wait_ge(S["wv_ready"], u + 1)
                if f is not None:
                    n = NS if is_sample(f) else PICKS
                    mark(V.tensor_copy(gate_u[:, 0:n], gate_f[:, 0:n]))
                    settle()
                    if not is_sample(f):
                        dve.wait_ge(S["hn_taken"], f + 1)

            def finish(k, w):
                m = ntok(w)
                if k == 1:
                    dve.wait_ge(S["vsum"], summed(PICKS * w + steps_of(w)))
                    dve.wait_ge(S["h_back"], 16 * w + 16)
                    for j in range(2):
                        cols = slice(512 * j, 512 * (j + 1))
                        last = V.tensor_tensor(hx[0:m, cols], Y[j][0:m, :], hx[0:m, cols], ALU.add)
                    if side_sum(w, NS):
                        mark(last)
                        settle()
                        last = V.tensor_tensor(hx[:, D - SIDE:D], hn[:, 0:SIDE], hx[:, D - SIDE:D], ALU.add)
                    last.then_inc(S["y_taken"], 1)
                if k == 3:
                    dve.wait_ge(S["y_root"], w + 1)
                    mark(V.reciprocal(rstd_y[0:m, :], rstd_y[0:m, :]))
                    settle()
                    V.scalar_tensor_tensor(hx[0:m, :], hx[0:m, :], rstd_y[0:m, :], w_fin[0:m, :], ALU.mult, ALU.mult)\
                        .then_inc(S["y_ready"], 1)

            periods(dve, own, body)



def bucket(dist):
    exact = BUCKETS // 2
    n = np.maximum(dist, 0)
    nf = np.maximum(n, 1).astype(np.float32)
    step = np.log(nf / np.float32(exact)) / np.float32(np.log(WINDOW / exact)) * np.float32(BUCKETS - exact)
    return np.where(n < exact, n, np.minimum(exact + step.astype(np.int32), BUCKETS - 1))


def constants():
    dist = 2 * P - 1 - np.arange(SKEW)
    valid = (dist >= 0) & (dist <= WINDOW)
    bucket_of = np.zeros((BUCKETS + 1, SKEW), np.float32)
    bucket_of[np.where(valid, bucket(dist), BUCKETS), np.arange(SKEW)] = 1.0
    s, t = np.arange(P)[:, None], np.arange(P)[None, :]
    masks = np.zeros((P, NL, P), np.float32)
    for l, m in enumerate(LEVELS):
        masks[:, l] = (s // (2 * m) == t // (2 * m)) & (s % (2 * m) < m) & (t % (2 * m) >= m)
    masks[:, NL - 1] = s == t
    d_s = (WINDOW + np.arange(DEC_T))[:, None] - np.arange(WINDOW + DEC_T)[None, :]
    ok = (d_s >= 0) & (d_s <= WINDOW)
    onehot = (bucket(d_s)[:, None, :] == np.arange(BUCKETS)[None, :, None]) & ok[:, None, :]
    same = np.arange(DEC_B)[:, None] == np.arange(DEC_B)[None, :]
    allowed = same[:, None, :, None] & ok[None, :, None, :]
    flat = np.concatenate([allowed[..., :WINDOW].reshape(NS, -1), allowed[..., WINDOW:].reshape(NS, -1)], axis=1)
    p = np.arange(P)
    return {
        "ident": np.eye(P, dtype=np.float32),
        "bucket_of": bucket_of,
        "level_masks": masks.reshape(P, NL * P),
        "iota16": np.tile(np.arange(TOPK, dtype=np.float32), (P, 1)),
        "tsel": (p[:, None] // BUCKETS == np.arange(DEC_T)[None]).astype(np.float32),
        "bsel": (p[:, None] // DEC_T == np.arange(DEC_B)[None]).astype(np.float32),
        "fold": (p[:, None] % NS == np.arange(NS)[None]).astype(np.float32),
        "s_onehot": onehot.reshape(DEC_T * BUCKETS, -1).astype(np.float32),
        "s_mask": np.tile(np.where(flat, 0.0, NEG).astype(np.float32), (GRP, 1)),
    }


def layout(i):
    w_in = i["w_in"][0]
    aw = HEADS * DH
    q = w_in[:, :aw].reshape(D, KV, GRP, DH).transpose(0, 2, 1, 3).reshape(D, aw)
    w_in = np.concatenate([q, w_in[:, aw:]], axis=1)
    sinks = i["attn_sinks"][0]
    return {
        "x_prompt": i["x_prompt"][0],
        "x_sample": i["x_sample"].reshape(NS, D),
        "w_in": w_in.reshape(DC, P, CHUNKS, P).transpose(2, 1, 0, 3),
        "w_o": i["w_o"][0],
        "w_q_t": i["peer_w_q"][0].T,
        "keys_t": i["peer_sub_keys"][0].reshape(2 * PH, P, P).transpose(2, 0, 1),
        "peer_u": i["peer_u"][0],
        "peer_v": i["peer_v"][0],
        "norm_mix_t": i["norm_mix_w"][0].reshape(DC, P).T,
        "hg_norm_t": i["hg_norm_w"][0].reshape(HG, P).T,
        "hg_lb_t": i["hg_lb"].reshape(2 * HG, P).T,
        "norm_ffn": np.tile(i["norm_ffn_w"], (P, 1)),
        "norm_final": np.tile(i["norm_final_w"], (P, 1)),
        "sinks": np.tile(sinks, (P, 1)),
        "sinks_s": np.repeat(sinks.reshape(KV, GRP).T, NS, axis=0),
        "table": np.repeat(i["rel_bias_table"][:, :, None], P, axis=2),
        "table_rep": np.tile(i["rel_bias_table"], (DEC_T, 1)),
        "cache_k": i["cache_k_win"][0].reshape(DEC_B, WINDOW, P),
        "cache_v": i["cache_v_win"][0].reshape(DEC_B, WINDOW, P),
        "cache_k_t": i["cache_k_win"][0].reshape(DEC_B, WINDOW, P).transpose(0, 2, 1),
        "state_in": i["state_hgrn"][0].transpose(0, 2, 1, 3),
    }


OUTS = {"y_prompt": (SEQ, D), "y_sample": (NS, D), "k_win_prompt": (WINDOW, P), "v_win_prompt": (WINDOW, P),
        "state_prompt": (P, HG, P), "k_win_sample": (DEC_B, WINDOW, P), "v_win_sample": (DEC_B, WINDOW, P),
        "state_out": (DEC_B, P, HG * P)}


def kernel(**inputs):
    import concourse.bacc as _bacc
    from concourse.bass_utils import run_bass_kernel_spmd as _run

    nc = _bacc.Bacc("TRN2", target_bir_lowering=False, num_devices=1)
    given = {k: np.asarray(v) for k, v in inputs.items()}
    arrays, aps = {}, {}
    for name, array in (layout(given) | constants()).items():
        array = np.ascontiguousarray(array)
        arrays[f"in_{name}"] = array
        aps[name] = nc.dram_tensor(f"in_{name}", array.shape, mybir.dt.from_np(array.dtype), kind="ExternalInput").ap()
    for name, shape in OUTS.items():
        aps[name] = nc.dram_tensor(f"out_{name}", shape, F32, kind="ExternalOutput").ap()
    build(nc, aps)
    r = _run(nc, [arrays], core_ids=[0]).results[0]
    o = {name: r[f"out_{name}"] for name in OUTS}
    win = (1, -1, WINDOW, KV, DH)
    return (o["y_prompt"].reshape(1, SEQ, D), o["y_sample"].reshape(DEC_B, DEC_T, D),
            o["k_win_prompt"].reshape(win), o["v_win_prompt"].reshape(win),
            np.ascontiguousarray(o["state_prompt"].transpose(1, 0, 2)).reshape(1, 1, HG, P, P),
            o["k_win_sample"].reshape(win), o["v_win_sample"].reshape(win),
            np.ascontiguousarray(o["state_out"].reshape(DEC_B, P, HG, P).transpose(0, 2, 1, 3)).reshape(1, DEC_B, HG, P, P))
```
